# Optimizing a Trainium2 kernel written in Bass

```python
import jax, jax.numpy as jnp
from jax import lax
import numpy as np

D_MODEL = 1024
BATCH = 1
SEQ = 1024
DEPTH = 2
DEC_BATCH = 1
DEC_SEQ = 64
PAST_LEN = 512

CHUNK = 64
N_EVEN = (DEPTH + 1) // 2
N_ODD = DEPTH // 2
A_HEADS = 4
A_HEAD_DIM = 128
A_WIDTH = A_HEADS * A_HEAD_DIM
B_HEADS = 8
B_NOPE = 64
B_ROPE = 32
B_VDIM = 64
B_QK = B_NOPE + B_ROPE
B_WIDTH = B_HEADS * B_VDIM
Q_RANK = 384
KV_RANK = 256
ROPE_THETA = 10000.0
Q_BLOCK = 128
MLA_SCALE = B_QK ** -0.5
C_HEADS = 16
C_HEAD_DIM = 64
C_WIDTH = C_HEADS * C_HEAD_DIM
LEFT_CHUNKS = 8
MAX_REL = 128
N_REL = 2 * MAX_REL + 1
C_SCALE = C_HEAD_DIM ** -0.5
BAND_BUF = min(LEFT_CHUNKS * CHUNK, PAST_LEN)
D_FF = ((8 * D_MODEL + 3 * 256 - 1) // (3 * 256)) * 256
IN_AB = 4 * A_WIDTH + 2 * A_HEADS + Q_RANK + KV_RANK + B_ROPE
AB_SPLITS = (A_WIDTH, 2 * A_WIDTH, 3 * A_WIDTH, 4 * A_WIDTH, 4 * A_WIDTH + A_HEADS,
             4 * A_WIDTH + 2 * A_HEADS, 4 * A_WIDTH + 2 * A_HEADS + Q_RANK,
             4 * A_WIDTH + 2 * A_HEADS + Q_RANK + KV_RANK)

kernel_name = 'mlstm_mla_band_streaming_step'

def rmsnorm(x, g, eps=1e-6):
    xf = x.astype(jnp.float32)
    y = xf * lax.rsqrt(jnp.mean(xf * xf, axis=-1, keepdims=True) + eps)
    return (y * g.astype(jnp.float32)).astype(x.dtype)

def rope(x, pos):
    half = x.shape[-1] // 2
    inv = ROPE_THETA ** (-jnp.arange(half, dtype=jnp.float32) / half)
    ang = pos.astype(jnp.float32)[:, None] * inv[None, :]
    bshape = (1, pos.shape[0]) + (1,) * (x.ndim - 3) + (half,)
    cos = jnp.cos(ang).reshape(bshape)
    sin = jnp.sin(ang).reshape(bshape)
    xf = x.astype(jnp.float32)
    x1, x2 = xf[..., :half], xf[..., half:]
    return jnp.concatenate([x1 * cos - x2 * sin, x1 * sin + x2 * cos], axis=-1).astype(x.dtype)

def swiglu(h, wg, wu, wd):
    return (jax.nn.silu(h @ wg) * (h @ wu)) @ wd

def tail_rows(t, n):
    L = t.shape[1]
    if L >= n:
        return t[:, L - n:]
    return jnp.pad(t, ((0, 0), (n - L, 0)) + ((0, 0),) * (t.ndim - 2))

def mlstm_chunk(carry, inp):
    c_mat, n_vec, m_st = carry
    q, k, v, ig, lf = inp
    L = q.shape[2]
    b = jnp.cumsum(lf, axis=-1)
    causal = jnp.tril(jnp.ones((L, L), dtype=bool))
    log_d = jnp.where(causal, b[..., :, None] - b[..., None, :] + ig[..., None, :], -jnp.inf)
    inter = b + m_st[..., None]
    m_t = jnp.maximum(inter, jnp.max(log_d, axis=-1))
    w_inter = jnp.exp(inter - m_t)
    s = jnp.einsum('bhtd,bhsd->bhts', q, k) * jnp.exp(log_d - m_t[..., None])
    num = w_inter[..., None] * jnp.einsum('bhtd,bhde->bhte', q, c_mat) + jnp.einsum('bhts,bhse->bhte', s, v)
    den = w_inter * jnp.einsum('bhtd,bhd->bht', q, n_vec) + jnp.sum(s, axis=-1)
    h = num / jnp.maximum(jnp.abs(den), jnp.exp(-m_t))[..., None]
    b_last = b[..., -1]
    g = b_last[..., None] - b + ig
    m_new = jnp.maximum(b_last + m_st, jnp.max(g, axis=-1))
    decay = jnp.exp(b_last + m_st - m_new)
    wk = jnp.exp(g - m_new[..., None])
    c_new = decay[..., None, None] * c_mat + jnp.einsum('bhs,bhsd,bhse->bhde', wk, k, v)
    n_new = decay[..., None] * n_vec + jnp.einsum('bhs,bhsd->bhd', wk, k)
    return (c_new, n_new, m_new), h

def mlstm_prompt(q, k, v, ig, lf):
    bsz, nh, s_len, dh = q.shape
    nc = s_len // CHUNK

    def to_chunks(t):
        t = t.reshape(t.shape[:2] + (nc, CHUNK) + t.shape[3:])
        return jnp.moveaxis(t, 2, 0)

    init = (jnp.zeros((bsz, nh, dh, dh), jnp.float32),
            jnp.zeros((bsz, nh, dh), jnp.float32),
            jnp.zeros((bsz, nh), jnp.float32))
    final, hs = lax.scan(mlstm_chunk, init,
                         (to_chunks(q), to_chunks(k), to_chunks(v), to_chunks(ig), to_chunks(lf)))
    h = jnp.moveaxis(hs, 0, 2).reshape(bsz, nh, s_len, dh)
    return h, final

def ab_in(h, pos, w_in, b_g, q_norm, kv_norm, w_uq, w_uk):
    bsz, L, _ = h.shape
    z = h @ w_in
    q_a, k_a, v_a, o_a, i_a, f_a, c_q, c_kv, k_r = jnp.split(z, AB_SPLITS, axis=-1)

    def heads(t):
        return t.reshape(bsz, L, A_HEADS, A_HEAD_DIM).transpose(0, 2, 1, 3).astype(jnp.float32)

    qa = heads(q_a)
    ka = heads(k_a) * (A_HEAD_DIM ** -0.5)
    va = heads(v_a)
    ig = (i_a + b_g[:A_HEADS]).astype(jnp.float32).transpose(0, 2, 1)
    lf = jax.nn.log_sigmoid((f_a + b_g[A_HEADS:]).astype(jnp.float32)).transpose(0, 2, 1)
    cq = rmsnorm(c_q, q_norm)
    qb = (cq @ w_uq).reshape(bsz, L, B_HEADS, B_QK)
    q_lat = jnp.einsum('blhn,rhn->blhr', qb[..., :B_NOPE], w_uk)
    q_rope = rope(qb[..., B_NOPE:], pos)
    ckv = rmsnorm(c_kv, kv_norm)
    krope = rope(k_r, pos)
    return (qa, ka, va, ig, lf, o_a), (q_lat, q_rope, ckv, krope)

def ab_out(h_a, o_a, hnorm, o_lat, w_uv, w_out):
    bsz, L, _ = o_a.shape
    ha = rmsnorm(jnp.swapaxes(h_a, 1, 2), hnorm.reshape(A_HEADS, A_HEAD_DIM)).reshape(bsz, L, A_WIDTH)
    ha = (ha * jax.nn.sigmoid(o_a.astype(jnp.float32))).astype(o_a.dtype)
    hb = jnp.einsum('blhr,rhv->blhv', o_lat, w_uv).reshape(bsz, L, B_WIDTH)
    return jnp.concatenate([ha, hb], axis=-1) @ w_out

def mla_attend(q_lat, q_rope, q_pos, ckv, krope, k_pos):
    s = (jnp.einsum('bqhr,bkr->bhqk', q_lat, ckv)
         + jnp.einsum('bqhe,bke->bhqk', q_rope, krope)).astype(jnp.float32) * MLA_SCALE
    visible = (k_pos[None, :] // CHUNK) <= (q_pos[:, None] // CHUNK)
    p = jax.nn.softmax(jnp.where(visible, s, -jnp.inf), axis=-1).astype(ckv.dtype)
    return jnp.einsum('bhqk,bkr->bqhr', p, ckv)

def mla_prompt_attend(q_lat, q_rope, ckv, krope, pos):
    bsz, s_len = q_lat.shape[:2]
    nb = s_len // Q_BLOCK

    def blk(t):
        return jnp.moveaxis(t.reshape((bsz, nb, Q_BLOCK) + t.shape[2:]), 1, 0)

    def one(args):
        ql, qr, qp = args
        return mla_attend(ql, qr, qp, ckv, krope, pos)

    o = lax.map(one, (blk(q_lat), blk(q_rope), pos.reshape(nb, Q_BLOCK)))
    return jnp.moveaxis(o, 0, 1).reshape((bsz, s_len) + o.shape[3:])

def c_in(h, w_qkv):
    bsz, L, _ = h.shape
    z = (h @ w_qkv).reshape(bsz, L, 3, C_HEADS, C_HEAD_DIM)
    return z[:, :, 0], z[:, :, 1], z[:, :, 2]

def band_attend(q, k, v, q_pos, k_pos, rel_bias):
    s = jnp.einsum('bqhd,bkhd->bhqk', q, k).astype(jnp.float32) * C_SCALE
    idx = jnp.clip(q_pos[:, None] - k_pos[None, :], -MAX_REL, MAX_REL) + MAX_REL
    s = s + rel_bias[:, idx].astype(jnp.float32)
    qc = (q_pos // CHUNK)[:, None]
    kc = (k_pos // CHUNK)[None, :]
    valid = (k_pos[None, :] >= 0) & (kc <= qc) & (kc >= qc - LEFT_CHUNKS)
    p = jax.nn.softmax(jnp.where(valid, s, -jnp.inf), axis=-1).astype(v.dtype)
    return jnp.einsum('bhqk,bkhd->bqhd', p, v)

def band_prompt(q, k, v, rel_bias):
    bsz, s_len, nh, dh = q.shape
    nc = s_len // CHUNK
    left = LEFT_CHUNKS * CHUNK
    band = left + CHUNK
    pad = ((0, 0), (left, 0), (0, 0), (0, 0))
    kp = jnp.pad(k, pad)
    vp = jnp.pad(v, pad)

    def one(c):
        start = c * CHUNK
        qc = lax.dynamic_slice_in_dim(q, start, CHUNK, axis=1)
        kc = lax.dynamic_slice_in_dim(kp, start, band, axis=1)
        vc = lax.dynamic_slice_in_dim(vp, start, band, axis=1)
        q_pos = start + jnp.arange(CHUNK, dtype=jnp.int32)
        k_pos = start - left + jnp.arange(band, dtype=jnp.int32)
        return band_attend(qc, kc, vc, q_pos, k_pos, rel_bias)

    o = lax.map(one, jnp.arange(nc, dtype=jnp.int32))
    return jnp.moveaxis(o, 0, 1).reshape(bsz, s_len, nh, dh)

def setup_inputs(seed: int = 0) -> dict:
    key = jax.random.key(seed)
    ks = jax.random.split(key, 40)
    cnt = [0]

    def nrm(shape, scale=1.0):
        k = ks[cnt[0]]
        cnt[0] += 1
        return scale * jax.random.normal(k, shape, jnp.float32)

    x_prompt = nrm((BATCH, SEQ, D_MODEL))
    x_sample = nrm((DEC_BATCH, DEC_SEQ, D_MODEL))
    cache_mla_ckv = nrm((N_EVEN, DEC_BATCH, PAST_LEN, KV_RANK))
    cache_mla_krope = nrm((N_EVEN, DEC_BATCH, PAST_LEN, B_ROPE))
    state_mlstm_C = nrm((N_EVEN, DEC_BATCH, A_HEADS, A_HEAD_DIM, A_HEAD_DIM), 0.3)
    state_mlstm_n = nrm((N_EVEN, DEC_BATCH, A_HEADS, A_HEAD_DIM), 0.3)
    state_mlstm_m = nrm((N_EVEN, DEC_BATCH, A_HEADS), 0.5)
    cache_band_k = nrm((N_ODD, DEC_BATCH, BAND_BUF, C_HEADS, C_HEAD_DIM))
    cache_band_v = nrm((N_ODD, DEC_BATCH, BAND_BUF, C_HEADS, C_HEAD_DIM))
    norm_mix = 1.0 + nrm((DEPTH, D_MODEL), 0.05)
    norm_ffn = 1.0 + nrm((DEPTH, D_MODEL), 0.05)
    norm_final = 1.0 + nrm((D_MODEL,), 0.05)
    w_in_ab = nrm((N_EVEN, D_MODEL, IN_AB), D_MODEL ** -0.5)
    b_i = nrm((N_EVEN, A_HEADS), 0.1)
    b_f = jnp.linspace(3.0, 6.0, A_HEADS, dtype=jnp.float32)[None, :] + nrm((N_EVEN, A_HEADS), 0.1)
    b_gates = jnp.concatenate([b_i, b_f], axis=-1)
    mlstm_hnorm = 1.0 + nrm((N_EVEN, A_WIDTH), 0.05)
    mla_q_norm = 1.0 + nrm((N_EVEN, Q_RANK), 0.05)
    mla_kv_norm = 1.0 + nrm((N_EVEN, KV_RANK), 0.05)
    mla_w_uq = nrm((N_EVEN, Q_RANK, B_HEADS * B_QK), Q_RANK ** -0.5)
    mla_w_uk = nrm((N_EVEN, KV_RANK, B_HEADS, B_NOPE), KV_RANK ** -0.5)
    mla_w_uv = nrm((N_EVEN, KV_RANK, B_HEADS, B_VDIM), KV_RANK ** -0.5)
    w_out_ab = nrm((N_EVEN, A_WIDTH + B_WIDTH, D_MODEL), (A_WIDTH + B_WIDTH) ** -0.5)
    w_qkv_c = nrm((N_ODD, D_MODEL, 3 * C_WIDTH), D_MODEL ** -0.5)
    w_out_c = nrm((N_ODD, C_WIDTH, D_MODEL), C_WIDTH ** -0.5)
    rel_bias_c = nrm((N_ODD, C_HEADS, N_REL), 0.5)
    w_gate = nrm((DEPTH, D_MODEL, D_FF), D_MODEL ** -0.5)
    w_up = nrm((DEPTH, D_MODEL, D_FF), D_MODEL ** -0.5)
    w_down = nrm((DEPTH, D_FF, D_MODEL), D_FF ** -0.5)
    return {'x_prompt': x_prompt, 'x_sample': x_sample,
            'cache_mla_ckv': cache_mla_ckv, 'cache_mla_krope': cache_mla_krope,
            'state_mlstm_C': state_mlstm_C, 'state_mlstm_n': state_mlstm_n, 'state_mlstm_m': state_mlstm_m,
            'cache_band_k': cache_band_k, 'cache_band_v': cache_band_v,
            'norm_mix': norm_mix, 'norm_ffn': norm_ffn, 'norm_final': norm_final,
            'w_in_ab': w_in_ab, 'b_gates': b_gates, 'mlstm_hnorm': mlstm_hnorm,
            'mla_q_norm': mla_q_norm, 'mla_kv_norm': mla_kv_norm,
            'mla_w_uq': mla_w_uq, 'mla_w_uk': mla_w_uk, 'mla_w_uv': mla_w_uv, 'w_out_ab': w_out_ab,
            'w_qkv_c': w_qkv_c, 'w_out_c': w_out_c, 'rel_bias_c': rel_bias_c,
            'w_gate': w_gate, 'w_up': w_up, 'w_down': w_down}

def reference(x_prompt, x_sample, cache_mla_ckv, cache_mla_krope, state_mlstm_C, state_mlstm_n,
              state_mlstm_m, cache_band_k, cache_band_v, norm_mix, norm_ffn, norm_final,
              w_in_ab, b_gates, mlstm_hnorm, mla_q_norm, mla_kv_norm, mla_w_uq, mla_w_uk, mla_w_uv,
              w_out_ab, w_qkv_c, w_out_c, rel_bias_c, w_gate, w_up, w_down):
    pos_p = jnp.arange(SEQ, dtype=jnp.int32)
    pos_s = PAST_LEN + jnp.arange(DEC_SEQ, dtype=jnp.int32)
    pos_sk = jnp.arange(PAST_LEN + DEC_SEQ, dtype=jnp.int32)
    band_pos_s = (PAST_LEN - BAND_BUF) + jnp.arange(BAND_BUF + DEC_SEQ, dtype=jnp.int32)
    xp, xs = x_prompt, x_sample
    p_ckv, p_kr, p_C, p_n, p_m, p_bk, p_bv = [], [], [], [], [], [], []
    s_ckv, s_kr, s_C, s_n, s_m, s_bk, s_bv = [], [], [], [], [], [], []
    for layer in range(DEPTH):
        j = layer // 2
        hp = rmsnorm(xp, norm_mix[layer])
        hs = rmsnorm(xs, norm_mix[layer])
        if layer % 2 == 0:
            w = (w_in_ab[j], b_gates[j], mla_q_norm[j], mla_kv_norm[j], mla_w_uq[j], mla_w_uk[j])
            (qa, ka, va, ig, lf, oa), (ql, qr, ckv, kr) = ab_in(hp, pos_p, *w)
            ha, (c_f, n_f, m_f) = mlstm_prompt(qa, ka, va, ig, lf)
            olat = mla_prompt_attend(ql, qr, ckv, kr, pos_p)
            xp = xp + ab_out(ha, oa, mlstm_hnorm[j], olat, mla_w_uv[j], w_out_ab[j])
            p_ckv.append(ckv)
            p_kr.append(kr)
            p_C.append(c_f.astype(xp.dtype))
            p_n.append(n_f.astype(xp.dtype))
            p_m.append(m_f.astype(xp.dtype))
            (qa, ka, va, ig, lf, oa), (ql, qr, ckv, kr) = ab_in(hs, pos_s, *w)
            init = (state_mlstm_C[j].astype(jnp.float32), state_mlstm_n[j].astype(jnp.float32),
                    state_mlstm_m[j].astype(jnp.float32))
            (c_s, n_s, m_s), ha = mlstm_chunk(init, (qa, ka, va, ig, lf))
            keys_ckv = jnp.concatenate([cache_mla_ckv[j], ckv], axis=1)
            keys_kr = jnp.concatenate([cache_mla_krope[j], kr], axis=1)
            olat = mla_attend(ql, qr, pos_s, keys_ckv, keys_kr, pos_sk)
            xs = xs + ab_out(ha, oa, mlstm_hnorm[j], olat, mla_w_uv[j], w_out_ab[j])
            s_ckv.append(ckv)
            s_kr.append(kr)
            s_C.append(c_s.astype(state_mlstm_C.dtype))
            s_n.append(n_s.astype(state_mlstm_n.dtype))
            s_m.append(m_s.astype(state_mlstm_m.dtype))
        else:
            q, k, v = c_in(hp, w_qkv_c[j])
            o = band_prompt(q, k, v, rel_bias_c[j])
            xp = xp + o.reshape(o.shape[0], o.shape[1], C_WIDTH) @ w_out_c[j]
            p_bk.append(tail_rows(k, BAND_BUF))
            p_bv.append(tail_rows(v, BAND_BUF))
            q, k, v = c_in(hs, w_qkv_c[j])
            kb = jnp.concatenate([cache_band_k[j], k], axis=1)
            vb = jnp.concatenate([cache_band_v[j], v], axis=1)
            o = band_attend(q, kb, vb, pos_s, band_pos_s, rel_bias_c[j])
            xs = xs + o.reshape(o.shape[0], o.shape[1], C_WIDTH) @ w_out_c[j]
            s_bk.append(kb[:, -BAND_BUF:])
            s_bv.append(vb[:, -BAND_BUF:])
        xp = xp + swiglu(rmsnorm(xp, norm_ffn[layer]), w_gate[layer], w_up[layer], w_down[layer])
        xs = xs + swiglu(rmsnorm(xs, norm_ffn[layer]), w_gate[layer], w_up[layer], w_down[layer])
    y_prompt = rmsnorm(xp, norm_final)
    y_sample = rmsnorm(xs, norm_final)
    return (y_prompt, y_sample,
            jnp.stack(p_ckv), jnp.stack(p_kr), jnp.stack(p_C), jnp.stack(p_n), jnp.stack(p_m),
            jnp.stack(p_bk), jnp.stack(p_bv),
            jnp.stack(s_ckv), jnp.stack(s_kr), jnp.stack(s_C), jnp.stack(s_n), jnp.stack(s_m),
            jnp.stack(s_bk), jnp.stack(s_bv))


_drawn_inputs = setup_inputs


def setup_inputs(seed=0):
    import zlib

    import numpy as np

    out = dict(_drawn_inputs(seed))
    spreads = {}
    factors = {'mla_q_norm': 8.0, 'mlstm_hnorm': 2.998}
    for name, (base, spread) in spreads.items():
        noise = np.random.default_rng([zlib.crc32(name.encode()), seed]).standard_normal(out[name].shape)
        drawn = base * np.exp(spread * noise) if base else spread * noise
        out[name] = __import__('jax').numpy.asarray(drawn.astype(out[name].dtype))
    for name, factor in factors.items():
        out[name] = (out[name] * factor).astype(out[name].dtype)
    return out
```

```python
from contextlib import ExitStack

import numpy as np

import concourse.bass as bass
from concourse import mybir

ALU = mybir.AluOpType
ACT = mybir.ActivationFunctionType
AX_X = mybir.AxisListType.X
F32 = mybir.dt.float32
F32R = mybir.dt.float32r

D_MODEL, SEQ, DEC_SEQ, PAST_LEN = 1024, 1024, 64, 512
A_HEADS, A_DIM = 4, 128
B_HEADS, B_NOPE, B_ROPE, B_VDIM = 8, 64, 32, 64
Q_RANK, KV_RANK = 384, 256
CHUNK = 64
C_HEADS, C_DIM, MAX_REL = 16, 64, 128
D_FF = ((8 * D_MODEL + 767) // 768) * 256
MLA_SCALE = (B_NOPE + B_ROPE) ** -0.5
C_SCALE = C_DIM ** -0.5
EPS = 1e-6
NEG = -1e30

P = 128
KT = D_MODEL // P
T = SEQ + DEC_SEQ
NT = (T + P - 1) // P
CHUNKS = [(0, 384), (384, 384), (768, T - 768)]
NC = len(CHUNKS)
UNIT = 2 * P
KEYS = T + PAST_LEN

Z_Q, Z_K, Z_V, Z_O = 0, 512, 1024, 1536
Z_CQ, Z_CKV, Z_MISC = 2048, 2432, 2688
Z_KR, Z_KRS, Z_I, Z_F = Z_MISC, Z_MISC + 32, Z_MISC + 64, Z_MISC + 96
Z_ROWS = Z_MISC + P
G_MIX0, G_FFN0, G_MIX1, G_FFN1, G_FINAL, G_Q, G_KV, G_H = 0, 8, 16, 24, 32, 40, 43, 45
G_COLS = 49


def tile_width(t):
    return min(P, T - t * P)


class Stage:

    def __init__(self, nc, name):
        self.nc, self.name, self.ctx, self.sems = nc, name, ExitStack(), []

    def __enter__(self):
        self.ctx.__enter__()
        return self

    def __exit__(self, *a):
        self.ctx.__exit__(*a)
        if self.sems and a[0] is None:
            self.nc.clear_and_free_semaphores(self.sems)
            self.nc.all_engine_barrier()

    def sb(self, name, shape, dt=F32):
        return self.ctx.enter_context(self.nc.sbuf_tensor(f"{self.name}_{name}", shape, dt))

    def ps(self, name, shape, dt=F32):
        return self.ctx.enter_context(self.nc.psum_tensor(f"{self.name}_{name}", shape, dt))

    def sem(self, name):
        self.sems.append(self.nc.alloc_semaphore(name=f"{self.name}_{name}"))
        return self.sems[-1]

    def block(self):
        return self.ctx.enter_context(self.nc.Block())


def load_stage(nc, S, D):
    with Stage(nc, "load") as st:
        xin = st.sb("xin", [P, 3, D_MODEL])
        banks = st.ps("banks", [P, 8, 512])
        ident_in, const_in = st.sem("ident_in"), st.sem("const_in")
        row_in = [st.sem(f"row_in{i}") for i in range(3)]
        turned, act_out, dve_out = st.sem("turned"), st.sem("act_out"), st.sem("dve_out")
        block = st.block()

        @block.sync
        def _(sp):
            sp.dma_start(S["ident"][:], D["ident"]).then_inc(ident_in, 16)
            sp.dma_start(S["ones"][:], D["ones"]).then_inc(const_in, 16)
            sp.dma_start(S["gains"][:], D["gains"]).then_inc(const_in, 16)
            sp.dma_start(S["halves"][:], D["halves"]).then_inc(const_in, 16)
            for t in range(NT):
                w = tile_width(t)
                if t >= 3:
                    sp.wait_ge(turned, 2 * (t - 2))
                src = D["x_prompt"][t * P:t * P + w, :] if t < SEQ // P else D["x_sample"]
                sp.dma_start(xin[0:w, t % 3, :], src).then_inc(row_in[t % 3], 16)
            rel = D["rel"]
            width = rel.shape[1]
            rows = bass.AP(rel.tensor, P - 1, [[width, C_HEADS], [-1, P], [1, 2 * P]])
            sp.dma_start(D["bias"], rows).then_inc(const_in, 16)
            sp.wait_ge(const_in, 64)

        @block.tensor
        def _(pe):
            pe.wait_ge(ident_in, 16)
            for t in range(NT):
                w = tile_width(t)
                pe.wait_ge(row_in[t % 3], 16 * (t // 3 + 1))
                for j in range(2):
                    if t >= 4:
                        pe.wait_ge(dve_out if j else act_out, t - 3)
                    for q in range(4):
                        k = 4 * j + q
                        last = nc.tensor.transpose(banks[:, (2 * t + j) % 8, q * P:q * P + w],
                                                   xin[0:w, t % 3, k * P:(k + 1) * P], S["ident"][0:w, 0:w])
                    last.then_inc(turned, 1)

        def empty(t, j):
            w = tile_width(t)
            src = banks[:, (2 * t + j) % 8, :].rearrange("p (q n) -> p q n", q=4)[:, :, 0:w]
            return S["xT"][:, 4 * j:4 * j + 4, t * P:t * P + w], src

        @block.scalar
        def _(act):
            for t in range(NT):
                act.wait_ge(turned, 2 * t + 1)
                nc.scalar.activation(*empty(t, 0), ACT.Copy).then_inc(act_out, 1)

        @block.vector
        def _(dve):
            for t in range(NT):
                dve.wait_ge(turned, 2 * t + 2)
                nc.vector.tensor_copy(*empty(t, 1)).then_inc(dve_out, 1)


def norm_stage(nc, S, name, g0):
    xT, hhi, hlo = S["xT"], S["hhi"], S["hlo"]
    with Stage(nc, name) as st:
        W = CHUNKS[0][1]
        sq = st.sb("sq", [P, 2, KT, W])
        var = st.sb("var", [P, NC, W])
        hf = st.sb("hf", [P, 4, W])
        mean = st.ps("mean", [P, NC, 512])
        rstd = st.ps("rstd", [P, NC, 512])
        squared, summed, recip, rooted = (st.sem(n) for n in ("squared", "summed", "recip", "rooted"))
        scaled, hi_done, lo_done = (st.sem(n) for n in ("scaled", "hi_done", "lo_done"))
        eps_added = st.sem("eps_added")
        block = st.block()

        @block.scalar
        def _(act):
            def square(c):
                c0, w = CHUNKS[c]
                if c >= 2:
                    act.wait_ge(summed, c - 1)
                nc.scalar.activation(sq[:, c % 2, :, 0:w], xT[:, :, c0:c0 + w], ACT.Square).then_inc(squared, 1)

            def root(c):
                w = CHUNKS[c][1]
                act.wait_ge(recip, c + 1)
                nc.scalar.activation(rstd[:, c, 0:w], var[:, c, 0:w], ACT.Sqrt).then_inc(rooted, 1)

            square(0)
            square(1)
            root(0)
            square(2)
            root(1)
            for c, (c0, w) in enumerate(CHUNKS):
                if c + 1 < NC and c > 0:
                    root(c + 1)
                for k in range(KT):
                    act.wait_ge(scaled, c * KT + k + 1)
                    nc.scalar.activation(hhi[:, k, c0:c0 + w], hf[:, k % 4, 0:w], ACT.Copy).then_inc(hi_done, 1)

        @block.tensor
        def _(pe):
            for c, (c0, w) in enumerate(CHUNKS):
                pe.wait_ge(squared, c + 1)
                for k in range(KT):
                    last = nc.tensor.matmul(mean[:, c, 0:w], S["ones"][:], sq[:, c % 2, k, 0:w],
                                            start=(k == 0), stop=(k == KT - 1))
                last.then_inc(summed, 1)

        @block.vector
        def _(dve):
            def reciprocal(c):
                w = CHUNKS[c][1]
                dve.wait_ge(summed, c + 1)
                nc.vector.tensor_scalar(var[:, c, 0:w], mean[:, c, 0:w], 1.0 / D_MODEL, EPS, ALU.mult,
                                        ALU.add).then_inc(eps_added, 1)
                dve.wait_ge(eps_added, c + 1)
                nc.vector.reciprocal(var[:, c, 0:w], var[:, c, 0:w]).then_inc(recip, 1)

            reciprocal(0)
            reciprocal(1)
            for c, (c0, w) in enumerate(CHUNKS):
                if c + 1 < NC and c > 0:
                    reciprocal(c + 1)
                dve.wait_ge(rooted, c + 1)
                for k in range(KT):
                    n = c * KT + k
                    if n >= 4:
                        dve.wait_ge(lo_done, n - 3)
                    nc.vector.scalar_tensor_tensor(out=hf[:, k % 4, 0:w], in0=xT[:, k, c0:c0 + w],
                                                   scalar=S["gains"][:, g0 + k:g0 + k + 1], in1=rstd[:, c, 0:w],
                                                   op0=ALU.mult, op1=ALU.mult).then_inc(scaled, 1)

        @block.gpsimd
        def _(pool):
            for c, (c0, w) in enumerate(CHUNKS):
                for k in range(KT):
                    pool.wait_ge(hi_done, c * KT + k + 1)
                    nc.gpsimd.tensor_tensor(hlo[:, k, c0:c0 + w], hf[:, k % 4, 0:w], hhi[:, k, c0:c0 + w],
                                            ALU.subtract).then_inc(lo_done, 1)


def three_pass(nc, out, whi, wlo, hhi, hlo, kts, c0, w):
    for k in range(kts):
        nc.tensor.matmul(out, whi[:, k, :], hhi[:, k, c0:c0 + w], start=(k == 0), stop=False)
        nc.tensor.matmul(out, whi[:, k, :], hlo[:, k, c0:c0 + w], start=False, stop=False)
        last = nc.tensor.matmul(out, wlo[:, k, :], hhi[:, k, c0:c0 + w], start=False, stop=(k == kts - 1))
    return last


def project_stage(nc, S, name, weights, units, out_rows=None):
    xT, hhi, hlo = S["xT"], S["hhi"], S["hlo"]
    w_view = weights.rearrange("(k p) n -> p k n", p=P)
    with Stage(nc, name) as st:
        stage = st.sb("stage", [P, KT, UNIT])
        whi = st.sb("whi", [P, 2, KT, P], F32R)
        wlo = st.sb("wlo", [P, 2, KT, P], F32R)
        rows = st.sb("rows", [P, 2, T]) if out_rows is not None else None
        banks = st.ps("banks", [P, 8, 512])
        w_in, hi_done, lo_done = st.sem("w_in"), st.sem("hi_done"), st.sem("lo_done")
        summed = st.sem("summed")
        emptied = st.sem("emptied")
        stored = [st.sem(f"stored{h}") for h in range(2)]
        block = st.block()

        @block.sync
        def _(sp):
            def load(u):
                sp.dma_start(stage[:], w_view[:, :, bass.ds(u * UNIT, UNIT)]).then_inc(w_in, 16)

            def store(u):
                for h in range(2):
                    sp.wait_ge(emptied, u * 2 * NC + (h + 1) * NC + 2 * NC)
                    sp.dma_start(out_rows[bass.ds(u * UNIT + h * P, P), :], rows[:, h, :]).then_inc(stored[h], 16)

            load(0)
            if out_rows is not None:
                for h in range(2):
                    sp.sem_inc(stored[h], 16)
            with sp.Fori(0, units - 1) as u:
                sp.wait_ge(lo_done, 2 * u + 2)
                load(u + 1)
                if out_rows is not None:
                    store(u)
            if out_rows is not None:
                store(units - 1)
                for h in range(2):
                    sp.wait_ge(stored[h], 16 * (units + 1))

        @block.scalar
        def _(act):
            with act.Fori(0, units) as u:
                act.wait_ge(w_in, 16 * u + 16)
                for h in range(2):
                    act.wait_ge(summed, 2 * NC * u + (h + 1) * NC)
                    nc.scalar.activation(whi[:, h], stage[:, :, h * P:(h + 1) * P], ACT.Copy).then_inc(hi_done, 1)

        @block.gpsimd
        def _(pool):
            with pool.Fori(0, units) as u:
                for h in range(2):
                    pool.wait_ge(hi_done, 2 * u + h + 1)
                    nc.gpsimd.tensor_tensor(wlo[:, h], stage[:, :, h * P:(h + 1) * P], whi[:, h],
                                            ALU.subtract).then_inc(lo_done, 1)

        @block.tensor
        def _(pe):
            pe.sem_inc(summed, 2 * NC)
            with pe.Fori(0, units) as u:
                for h in range(2):
                    pe.wait_ge(lo_done, 2 * u + h + 1)
                    for c, (c0, w) in enumerate(CHUNKS):
                        b = h * NC + c
                        pe.wait_ge(emptied, 2 * NC * u + b + 1)
                        last = three_pass(nc, banks[:, b, 0:w], whi[:, h], wlo[:, h], hhi, hlo, KT, c0, w)
                        last.then_inc(summed, 1)

        @block.vector
        def _(dve):
            dve.sem_inc(emptied, 2 * NC)
            with dve.Fori(0, units) as u:
                for h in range(2):
                    if out_rows is not None:
                        dve.wait_ge(stored[h], 16 * u + 16)
                    for c, (c0, w) in enumerate(CHUNKS):
                        b = h * NC + c
                        dve.wait_ge(summed, 2 * NC * u + b + 1 + 2 * NC)
                        if out_rows is not None:
                            nc.vector.tensor_copy(rows[:, h, c0:c0 + w], banks[:, b, 0:w]).then_inc(emptied, 1)
                        else:
                            x = xT[:, bass.ds(2 * u + h, 1), c0:c0 + w].rearrange("p a n -> p (a n)")
                            nc.vector.tensor_tensor(x, x, banks[:, b, 0:w], ALU.add).then_inc(emptied, 1)




R = A_HEADS * NT


def gate_stage(nc, S, D):
    PROMPT = SEQ // P
    with Stage(nc, "gate") as st:
        gi = st.sb("gi", [A_HEADS, NT * P])
        gf = st.sb("gf", [A_HEADS, NT * P])
        e1 = st.sb("e1", [A_HEADS, T])
        bias = st.sb("bias", [A_HEADS, 2])
        ig = st.sb("ig", [R, P])
        lf = st.sb("lf", [R, P])
        lfT = st.sb("lfT", [P, R])
        b = st.sb("b", [R, P])
        a = st.sb("a", [R, P])
        amax = st.sb("amax", [R, P])
        rows = st.sb("rows", [1, 4, A_HEADS, NT])
        logs = st.sb("logs", [1, 2, R])
        m_in = st.sb("m_in", [R, 1])
        u = st.sb("u", [R, P])
        w = st.sb("w", [R, P])
        nm = st.sb("nm", [R, P])
        wk = st.sb("wk", [P, R])
        m0 = st.sb("m0", [1, A_HEADS])
        m_out = st.sb("m_out", [1, 2, A_HEADS])
        ps = st.ps("ps", [P, 8, 512])
        z_in, dve, act, pe = st.sem("z_in"), st.sem("dve"), st.sem("act"), st.sem("pe")
        parked, back, out = st.sem("parked"), st.sem("back"), st.sem("out")
        block = st.block()
        r_b, r_a, r_min, r_mout = (rows[:, i] for i in range(4))
        flat = lambda x: x.rearrange("p h c -> p (h c)")

        done = {}

        @block.vector
        def _(eng):
            n = [0]

            def step(ins):
                ins.then_inc(dve, 1)
                n[0] += 1
                eng.wait_ge(dve, n[0])

            v = nc.vector
            step(v.memset(gi[:, T:], NEG))
            step(v.memset(gf[:, T:], 0.0))
            step(v.memset(r_min[:, :, 0], 0.0))
            eng.wait_ge(z_in, 96)
            step(v.tensor_scalar(gi[:, 0:T], gi[:, 0:T], bias[:, 0:1], None, ALU.add))
            step(v.tensor_scalar(gf[:, 0:T], gf[:, 0:T], bias[:, 1:2], None, ALU.add))
            step(v.scalar_tensor_tensor(out=e1[:], in0=gf[:, 0:T], scalar=-1.0, in1=gf[:, 0:T], op0=ALU.mult,
                                        op1=ALU.min))
            step(v.tensor_scalar(gf[:, 0:T], gf[:, 0:T], 0.0, None, ALU.min))
            eng.wait_ge(act, 2)
            step(v.tensor_tensor(gf[:, 0:T], gf[:, 0:T], e1[:], ALU.subtract))
            eng.wait_ge(pe, 1)
            step(v.tensor_copy(lfT[:], ps[:, 0, 0:R]))
            eng.wait_ge(pe, 2)
            step(v.tensor_copy(b[:], ps[0:R, 1, 0:P]))
            eng.wait_ge(back, 32)
            step(v.tensor_tensor(a[:], ig[:], b[:], ALU.subtract))
            eng.wait_ge(pe, 3)
            step(v.tensor_copy(S["aT"][:], ps[:, 2, 0:R]))
            step(v.tensor_tensor_scan(amax[:], a[:], a[:], NEG, ALU.max, ALU.max))
            eng.wait_ge(pe, 4)
            step(v.tensor_copy(rows[:, 0:2].rearrange("p i h c -> p (i h c)"), ps[0:1, 3, 0:2 * R]))
            step(v.tensor_copy(r_min[:, :, NT - 1], m0[:]))
            for c in list(range(PROMPT)) + [NT - 1]:
                step(v.tensor_tensor(r_mout[:, :, c], r_min[:, :, c], r_a[:, :, c], ALU.max))
                step(v.tensor_tensor(r_mout[:, :, c], r_mout[:, :, c], r_b[:, :, c], ALU.add))
                if c + 1 < PROMPT:
                    step(v.tensor_copy(r_min[:, :, c + 1], r_mout[:, :, c]))
            step(v.tensor_copy(m_out[:, 0, :], r_mout[:, :, PROMPT - 1]))
            step(v.tensor_copy(m_out[:, 1, :], r_mout[:, :, NT - 1]))
            done["m"] = n[0]
            step(v.tensor_tensor(logs[:, 1, :], flat(r_b), flat(r_mout), ALU.subtract))
            step(v.tensor_tensor(logs[:, 0, :], logs[:, 1, :], flat(r_min), ALU.add))
            done["logs"] = n[0]
            eng.wait_ge(pe, 5)
            step(v.tensor_copy(m_in[:], ps[0:R, 4, 0:1]))
            step(v.tensor_scalar(u[:], amax[:], m_in[:], -1.0, ALU.max, ALU.mult))
            done["u"] = n[0]
            step(v.tensor_tensor(nm[:], u[:], b[:], ALU.subtract))
            done["nm"] = n[0]
            eng.wait_ge(pe, 7)
            step(v.tensor_tensor(wk[:], S["aT"][:], ps[:, 7, 0:R], ALU.add))
            done["wk"] = n[0]

        @block.sync
        def _(sp):
            sp.dma_start(gi[:, 0:T], D["z"][Z_I:Z_I + A_HEADS, :]).then_inc(z_in, 16)
            sp.dma_start(gf[:, 0:T], D["z"][Z_F:Z_F + A_HEADS, :]).then_inc(z_in, 16)
            sp.dma_start(bias[:], D["b_gates"]).then_inc(z_in, 16)
            sp.dma_start(S["upper"][:], D["upper"]).then_inc(z_in, 16)
            sp.dma_start(S["lower"][:], D["lower"]).then_inc(z_in, 16)
            sp.dma_start(m0[:], D["s_m0"]).then_inc(z_in, 16)
            sp.wait_ge(dve, 8)
            sp.dma_start(D["gates"][0], gi[:]).then_inc(parked, 16)
            sp.dma_start(D["gates"][1], gf[:]).then_inc(parked, 16)
            sp.wait_ge(parked, 32)
            sp.dma_start(ig[:], D["gates"][0].rearrange("h (c t) -> (h c) t", t=P)).then_inc(back, 16)
            sp.dma_start(lf[:], D["gates"][1].rearrange("h (c t) -> (h c) t", t=P)).then_inc(back, 16)
            sp.wait_ge(dve, done["m"])
            sp.dma_start(D["p_m"], m_out[:, 0, :]).then_inc(out, 16)
            sp.dma_start(D["s_m"], m_out[:, 1, :]).then_inc(out, 16)
            sp.wait_ge(dve, done["u"])
            sp.dma_start(D["u"].rearrange("h (c t) -> (h c) t", t=P), u[:]).then_inc(out, 16)
            sp.wait_ge(act, 4)
            sp.dma_start(D["w"].rearrange("h (c t) -> (h c) t", t=P), w[:]).then_inc(out, 16)
            sp.wait_ge(out, 64)

        @block.scalar
        def _(eng):
            eng.wait_ge(dve, 6)
            nc.scalar.activation(e1[:], e1[:], ACT.Exp).then_inc(act, 1)
            eng.wait_ge(act, 1)
            nc.scalar.activation(e1[:], e1[:], ACT.Ln, bias=1.0).then_inc(act, 1)
            eng.wait_ge(pe, 6)
            nc.scalar.activation(S["decay"][:], ps[:, 6, 0:R], ACT.Exp).then_inc(act, 1)
            eng.wait_ge(dve, done["u"])
            nc.scalar.activation(w[:], u[:], ACT.Exp, bias=m_in[:]).then_inc(act, 1)
            eng.wait_ge(dve, done["wk"])
            nc.scalar.activation(S["wk"][:], wk[:], ACT.Exp).then_inc(act, 1)
            eng.wait_ge(pe, 8)
            nc.scalar.activation(S["enm"][:], ps[:, 0, 0:R], ACT.Exp).then_inc(act, 1)

        @block.tensor
        def _(eng):
            eng.wait_ge(back, 32)
            nc.tensor.transpose(ps[:, 0, 0:R], lf[:], S["ident"][0:R, 0:R]).then_inc(pe, 1)
            eng.wait_ge(dve, 9)
            nc.tensor.matmul(ps[0:R, 1, 0:P], lfT[:], S["upper"][:], start=True, stop=True).then_inc(pe, 1)
            eng.wait_ge(dve, 11)
            nc.tensor.transpose(ps[:, 2, 0:R], a[:], S["ident"][0:R, 0:R]).then_inc(pe, 1)
            eng.wait_ge(dve, 13)
            nc.tensor.transpose(ps[0:1, 3, 0:R], b[:, P - 1:P], S["ident"][0:R, 0:R])
            nc.tensor.transpose(ps[0:1, 3, R:2 * R], amax[:, P - 1:P], S["ident"][0:R, 0:R]).then_inc(pe, 1)
            eng.wait_ge(dve, done["m"])
            nc.tensor.matmul(ps[0:R, 4, 0:1], flat(r_min), S["ones"][0:1, 0:1], start=True, stop=True).then_inc(pe, 1)
            eng.wait_ge(dve, done["logs"])
            nc.tensor.matmul(ps[:, 6, 0:R], S["ones"][0:1, :], logs[:, 0, :], start=True, stop=True).then_inc(pe, 1)
            nc.tensor.matmul(ps[:, 7, 0:R], S["ones"][0:1, :], logs[:, 1, :], start=True, stop=True).then_inc(pe, 1)
            eng.wait_ge(dve, done["nm"])
            nc.tensor.transpose(ps[:, 0, 0:R], nm[:], S["ident"][0:R, 0:R]).then_inc(pe, 1)


def mlstm_stage(nc, S, D):
    PROMPT = SEQ // P
    N = 2 * NT
    E1 = A_DIM + 1
    hhi, hlo = S["hhi"], S["hlo"]
    with Stage(nc, "mlstm") as st:
        qT, kT, vT, oT = (st.sb(x, [P, 2, T]) for x in ("qT", "kT", "vT", "oT"))
        dm = st.sb("dm", [P, 2, NT, P])
        qw = st.sb("qw", [P, 2, NT * P])
        cols = st.sb("cols", [P, 4, N])
        kw = st.sb("kw", [P, N, A_DIM])
        v1 = st.sb("v1", [P, 2, NT, E1])
        state = st.sb("state", [P, 2, 2, E1])
        sd = st.sb("sd", [P, 2, P])
        h = st.sb("h", [P, N, A_DIM])
        den = st.sb("den", [P, N])
        ssq = st.sb("ssq", [P, N])
        junk = st.sb("junk", [P, 2, A_DIM])
        gated = st.sb("gated", [P, 2, P])
        pS = st.ps("pS", [P, 2, 512])
        pN = st.ps("pN", [P, 2, 512])
        pU = st.ps("pU", [P, 2, 512])
        pT = st.ps("pT", [P, 2, 512])
        names = ("zin", "uin", "pair_done", "set_up", "dadd", "dexp", "turned", "kept", "sm", "sdm", "nm", "um",
                 "upd", "dn", "rd", "hs", "sq", "mv", "rt", "hn", "ht", "gt", "hi", "lo", "stored", "ones", "sg", "apart", "cleared")
        s = {x: st.sem(x) for x in names}
        block = st.block()
        TR = 2 * N

        @block.sync
        def _(sp):
            sp.sem_inc(s["stored"], 16 * 8)
            with sp.Fori(0, 2) as hp:
                sp.wait_ge(s["pair_done"], hp + 1)
                sp.wait_ge(s["lo"], N * hp + 1)
                for e in range(2):
                    for dst, row in ((qT, Z_Q), (kT, Z_K), (vT, Z_V), (oT, Z_O)):
                        sp.dma_start(dst[:, e, :], D["z"][bass.ds(hp * 2 * P + row + e * P, P), :]).then_inc(s["zin"], 16)
                    for dst, name in ((dm[:, e].rearrange("p c t -> p (c t)"), "u"), (qw[:, e], "w")):
                        src = D[name][bass.ds(2 * hp + e, 1), :].to_broadcast([P, NT * P])
                        sp.dma_start(dst, src).then_inc(s["uin"], 16)
                sp.wait_ge(s["stored"], 128 * hp + 128)
                for e in range(2):
                    sp.dma_start(state[:, e, 1, 0:A_DIM], D["s_C0"][bass.ds(2 * hp + e, 1)].rearrange("a p n -> p (a n)"))\
                      .then_inc(s["zin"], 16)
                    sp.dma_start(state[:, e, 1, A_DIM:E1], D["s_n0"][bass.ds(2 * hp + e, 1)].rearrange("a p n -> p (a n)"))\
                      .then_inc(s["zin"], 16)
                for g, (c_out, n_out) in enumerate((("p_C", "p_n"), ("s_C", "s_n"))):
                    for e in range(2):
                        sp.wait_ge(s["upd"], N * hp + 2 * (PROMPT - 1 + g) + e + 1)
                        sp.dma_start(D[c_out][bass.ds(2 * hp + e, 1)].rearrange("a p n -> p (a n)"),
                                     state[:, e, g, 0:A_DIM]).then_inc(s["stored"], 16)
                        sp.dma_start(D[n_out][bass.ds(2 * hp + e, 1)].rearrange("a p n -> p (a n)"),
                                     state[:, e, g, A_DIM:E1]).then_inc(s["stored"], 16)
            sp.wait_ge(s["stored"], 128 * 3)

        @block.gpsimd
        def _(pool):
            nc.gpsimd.memset(v1[:], 1.0).then_inc(s["ones"], 1)
            pool.sem_inc(s["lo"], 1)
            with pool.Fori(0, 2) as hp:
                for n in range(N):
                    c, e = n // 2, n % 2
                    w = tile_width(c)
                    pool.wait_ge(s["hi"], N * hp + n + 1)
                    dst = slice(c * P, c * P + w)
                    ht = bass.ds(2 * hp + e, 1)
                    nc.gpsimd.tensor_tensor(hlo[:, ht, dst].rearrange("p a n -> p (a n)"), gated[:, n % 2, 0:w],
                                            hhi[:, ht, dst].rearrange("p a n -> p (a n)"), ALU.subtract)\
                      .then_inc(s["lo"], 1)

        @block.scalar
        def _(act):
            with act.Fori(0, 2) as hp:
                for e in range(2):
                    act.wait_ge(s["dadd"], 4 * hp + 2 * e + 2)
                    nc.scalar.activation(dm[:, e], dm[:, e], ACT.Exp).then_inc(s["dexp"], 1)
                for n in range(N):
                    w = tile_width(n // 2)
                    act.wait_ge(s["hs"], N * hp + n + 1)
                    if n >= 2:
                        act.wait_ge(s["sq"], N * hp + n - 1)
                    nc.scalar.activation(junk[0:w, n % 2], h[0:w, n, :], ACT.Square, accum_out=ssq[0:w, n:n + 1])\
                      .then_inc(s["sq"], 1)
                act.wait_ge(s["mv"], 2 * hp + 2)
                nc.scalar.activation(ssq[:], ssq[:], ACT.Sqrt).then_inc(s["rt"], 1)
                nc.scalar.activation(oT[:], oT[:], ACT.Sigmoid).then_inc(s["sg"], 1)
                for n in range(N):
                    c, e = n // 2, n % 2
                    w = tile_width(c)
                    act.wait_ge(s["gt"], N * hp + n + 1)
                    dst = hhi[:, bass.ds(2 * hp + e, 1), c * P:c * P + w].rearrange("p a n -> p (a n)")
                    nc.scalar.activation(dst, gated[:, n % 2, 0:w], ACT.Copy).then_inc(s["hi"], 1)

        @block.tensor
        def _(pe):
            with pe.Fori(0, 2) as hp:
                pe.wait_ge(s["set_up"], 3 * hp + 3)
                for n in range(N):
                    c, e = n // 2, n % 2
                    w = tile_width(c)
                    for j, src in enumerate((kT, vT)):
                        m = 2 * n + j
                        if m >= 2:
                            pe.wait_ge(s["kept"], TR * hp + m - 1)
                        if w < P:
                            pe.sem_inc(s["apart"], 1)
                        nc.tensor.transpose(pT[0:w, j, 0:P], src[:, e, c * P:c * P + w], S["ident"][:])\
                          .then_inc(s["turned"], 1)

                def scores(n):
                    c, e = n // 2, n % 2
                    w = tile_width(c)
                    if n >= 2:
                        pe.wait_ge(s["sdm"], N * hp + n - 1)
                    nc.tensor.matmul(pS[0:w, n % 2, 0:w], kT[:, e, c * P:c * P + w], qT[:, e, c * P:c * P + w],
                                     start=True, stop=True).then_inc(s["sm"], 1)

                scores(0)
                pe.wait_ge(s["kept"], TR * hp + TR)
                for n in range(N):
                    c, e = n // 2, n % 2
                    w = tile_width(c)
                    g = int(c == NT - 1)
                    if n + 1 < N:
                        scores(n + 1)
                    if n >= 2:
                        pe.wait_ge(s["upd"], N * hp + n - 1)
                    nc.tensor.matmul(pU[:, n % 2, 0:E1], kw[0:w, n, :], v1[0:w, e, c, :], start=True, stop=True)\
                      .then_inc(s["um"], 1)
                    pe.wait_ge(s["sdm"], N * hp + n + 1)
                    if n >= 2:
                        pe.wait_ge(s["hs"], N * hp + n - 1)
                    nc.tensor.matmul(pN[0:w, n % 2, 0:E1], qw[:, e, c * P:c * P + w], state[:, e, g, :],
                                     start=True, stop=False)
                    nc.tensor.matmul(pN[0:w, n % 2, 0:E1], sd[0:w, n % 2, 0:w], v1[0:w, e, c, :],
                                     start=False, stop=True).then_inc(s["nm"], 1)
                for n in range(N):
                    c, e = n // 2, n % 2
                    w = tile_width(c)
                    pe.wait_ge(s["hn"], N * hp + n + 1)
                    if n >= 2:
                        pe.wait_ge(s["gt"], N * hp + n - 1)
                    if w < P:
                        pe.sem_inc(s["apart"], 1)
                    nc.tensor.transpose(pT[:, n % 2, 0:w], h[0:w, n, :], S["ident"][0:w, 0:w]).then_inc(s["ht"], 1)

        @block.vector
        def _(dve):
            v = nc.vector
            dve.sem_inc(s["pair_done"], 1)
            dve.wait_ge(s["ones"], 1)
            v.memset(ssq[:], 1.0).then_inc(s["cleared"], 1)
            with dve.Fori(0, 2) as hp:
                dve.wait_ge(s["uin"], 64 * hp + 64)
                pair = bass.ds(hp * N, N)
                for i, src in enumerate(("aT", "enm", "wk", "decay")):
                    v.tensor_copy(cols[:, i, :], S[src][:, pair]).then_inc(s["rd"], 1)
                dve.wait_ge(s["rd"], (4 + N) * hp + 4)
                mask = S["lower"][:].rearrange("p (a t) -> p a t", a=1).to_broadcast([P, NT, P])
                for e in range(2):
                    a = cols[:, 0, e * NT:(e + 1) * NT].rearrange("p (c a) -> p c a", a=1).to_broadcast([P, NT, P])
                    v.tensor_tensor(dm[:, e], dm[:, e], a, ALU.add).then_inc(s["dadd"], 1)
                    dve.wait_ge(s["dadd"], 4 * hp + 2 * e + 1)
                    v.tensor_tensor(dm[:, e], dm[:, e], mask, ALU.add).then_inc(s["dadd"], 1)
                dve.wait_ge(s["zin"], 16 * 12 * hp + 16 * 12)
                v.tensor_scalar(kT[:], kT[:], A_DIM ** -0.5, None, ALU.mult).then_inc(s["set_up"], 1)
                v.tensor_tensor(qw[:, :, 0:T], qw[:, :, 0:T], qT[:], ALU.mult).then_inc(s["set_up"], 1)
                v.memset(state[:, :, 0, :], 0.0).then_inc(s["set_up"], 1)
                for n in range(N):
                    c, e = n // 2, n % 2
                    w = tile_width(c)
                    dve.wait_ge(s["turned"], TR * hp + 2 * n + 1)
                    i = e * NT + c
                    v.tensor_scalar(kw[0:w, n, :], pT[0:w, 0, 0:P], cols[0:w, 2, i:i + 1], None, ALU.mult)\
                     .then_inc(s["kept"], 1)
                    dve.wait_ge(s["turned"], TR * hp + 2 * n + 2)
                    v.tensor_copy(v1[0:w, e, c, 0:A_DIM], pT[0:w, 1, 0:P]).then_inc(s["kept"], 1)
                dve.wait_ge(s["set_up"], 3 * hp + 3)
                dve.wait_ge(s["dexp"], 2 * hp + 2)
                for n in range(N):
                    c, e = n // 2, n % 2
                    w = tile_width(c)
                    g = int(c == NT - 1)
                    i = e * NT + c
                    dve.wait_ge(s["sm"], N * hp + n + 1)
                    if n >= 2:
                        dve.wait_ge(s["nm"], N * hp + n - 1)
                    v.tensor_tensor(sd[0:w, n % 2, 0:w], dm[0:w, e, c, 0:w], pS[0:w, n % 2, 0:w], ALU.mult)\
                     .then_inc(s["sdm"], 1)
                    dve.wait_ge(s["nm"], N * hp + n + 1)
                    dve.wait_ge(s["um"], N * hp + n + 1)
                    if n >= 2:
                        dve.wait_ge(s["upd"], N * hp + n - 1)
                    v.scalar_tensor_tensor(out=state[:, e, g, :], in0=state[:, e, g, :], scalar=cols[:, 3, i:i + 1],
                                           in1=pU[:, n % 2, 0:E1], op0=ALU.mult, op1=ALU.add).then_inc(s["upd"], 1)
                    v.tensor_scalar(den[0:w, n:n + 1], pN[0:w, n % 2, A_DIM:E1], -1.0, cols[0:w, 1, i:i + 1],
                                    ALU.mult, ALU.max).then_inc(s["dn"], 1)
                    dve.wait_ge(s["dn"], 2 * N * hp + 2 * n + 1)
                    v.tensor_tensor(den[0:w, n:n + 1], pN[0:w, n % 2, A_DIM:E1], den[0:w, n:n + 1], ALU.max)\
                     .then_inc(s["dn"], 1)
                    dve.wait_ge(s["dn"], 2 * N * hp + 2 * n + 2)
                    v.reciprocal(den[0:w, n:n + 1], den[0:w, n:n + 1]).then_inc(s["rd"], 1)
                    dve.wait_ge(s["rd"], (4 + N) * hp + 4 + n + 1)
                    v.tensor_scalar(h[0:w, n, :], pN[0:w, n % 2, 0:A_DIM], den[0:w, n:n + 1], None, ALU.mult)\
                     .then_inc(s["hs"], 1)
                dve.wait_ge(s["sq"], N * hp + N)
                v.tensor_scalar(ssq[:], ssq[:], 1.0 / A_DIM, EPS, ALU.mult, ALU.add).then_inc(s["mv"], 1)
                dve.wait_ge(s["mv"], 2 * hp + 1)
                v.reciprocal(ssq[:], ssq[:]).then_inc(s["mv"], 1)
                dve.wait_ge(s["rt"], hp + 1)
                for n in range(N):
                    w = tile_width(n // 2)
                    v.tensor_scalar(h[0:w, n, :], h[0:w, n, :], ssq[0:w, n:n + 1], None, ALU.mult).then_inc(s["hn"], 1)
                dve.wait_ge(s["sg"], hp + 1)
                for n in range(N):
                    c, e = n // 2, n % 2
                    w = tile_width(c)
                    dve.wait_ge(s["ht"], N * hp + n + 1)
                    if n >= 2:
                        dve.wait_ge(s["lo"], N * hp + n)
                    g = bass.ds(2 * hp + G_H + e, 1)
                    v.scalar_tensor_tensor(out=gated[:, n % 2, 0:w], in0=pT[:, n % 2, 0:w], scalar=S["gains"][:, g],
                                           in1=oT[:, e, c * P:c * P + w], op0=ALU.mult, op1=ALU.mult)\
                     .then_inc(s["gt"], 1)
                dve.sem_inc(s["pair_done"], 1)


def ffn_stage(nc, S, name, w_gate, w_up, w_down):
    xT, hhi, hlo = S["xT"], S["hhi"], S["hlo"]
    parts = D_FF // UNIT
    F = UNIT // P
    srcs = [w_gate.rearrange("(k p) n -> p k n", p=P), w_up.rearrange("(k p) n -> p k n", p=P),
            w_down.rearrange("(a f p) n -> a p f n", f=F, p=P)]
    W = CHUNKS[0][1]
    with Stage(nc, name) as st:
        stage = [st.sb(f"stage{m}", [P, KT * UNIT]) for m in range(3)]
        whi = [st.sb(f"whi{m}", [P, KT * UNIT], F32R) for m in range(3)]
        wlo = [st.sb(f"wlo{m}", [P, KT * UNIT], F32R) for m in range(3)]
        ahi = st.sb("ahi", [P, F, T], F32R)
        alo = st.sb("alo", [P, F, T], F32R)
        silu = st.sb("silu", [P, F, W])
        act32 = st.sb("act32", [P, F, W])
        banks = st.ps("banks", [P, 8, 512])
        w_in = [st.sem(f"w_in{m}") for m in range(3)]
        w_hi = [st.sem(f"w_hi{m}") for m in range(3)]
        w_lo = [st.sem(f"w_lo{m}") for m in range(3)]
        gate_sum, up_sum, silu_done, product = (st.sem(n) for n in ("gate_sum", "up_sum", "silu_done", "product"))
        a_hi, a_lo = st.sem("a_hi"), st.sem("a_lo")
        out_sum, added = st.sem("out_sum"), st.sem("added")
        block = st.block()
        G = NC * F
        O = NC * KT

        def cols(m, tiles):
            return tiles[m][:].rearrange("p (k f n) -> p f k n", k=KT, f=F)

        @block.sync
        def _(sp):
            def load(i, m):
                src = srcs[m][:, :, bass.ds(i * UNIT, UNIT)] if m < 2 else \
                    srcs[m][bass.ds(i, 1), :, :, :].rearrange("a p f n -> p (a f) n")
                dst = stage[m][:].rearrange("p (a n) -> p a n", a=KT if m < 2 else F)
                sp.dma_start(dst, src).then_inc(w_in[m], 16)

            for m in range(3):
                load(0, m)
            with sp.Fori(1, parts) as i:
                for m in range(3):
                    sp.wait_ge(w_lo[m], i)
                    load(i, m)

        @block.scalar
        def _(act):
            with act.Fori(0, parts) as i:
                for m in range(3):
                    act.wait_ge(w_in[m], 16 * i + 16)
                    if m < 2:
                        act.wait_ge(up_sum, G * i + G)
                    else:
                        act.wait_ge(out_sum, O * i + O)
                    nc.scalar.activation(whi[m][:], stage[m][:], ACT.Copy).then_inc(w_hi[m], 1)
                for c, (c0, w) in enumerate(CHUNKS):
                    for f in range(F):
                        n = G * i + c * F + f
                        act.wait_ge(gate_sum, n + 1)
                        act.wait_ge(product, n + 1)
                        nc.scalar.activation(silu[:, f, 0:w], banks[:, 2 * f, 0:w], ACT.Silu).then_inc(silu_done, 1)
                    for f in range(F):
                        n = G * i + c * F + f
                        act.wait_ge(product, n + 1 + F)
                        nc.scalar.activation(ahi[:, f, c0:c0 + w], act32[:, f, 0:w], ACT.Copy).then_inc(a_hi, 1)

        @block.gpsimd
        def _(pool):
            pool.sem_inc(a_lo, F)
            with pool.Fori(0, parts) as i:
                for m in range(3):
                    pool.wait_ge(w_hi[m], i + 1)
                    nc.gpsimd.tensor_tensor(wlo[m][:], stage[m][:], whi[m][:], ALU.subtract).then_inc(w_lo[m], 1)
                for c, (c0, w) in enumerate(CHUNKS):
                    for f in range(F):
                        n = G * i + c * F + f
                        pool.wait_ge(a_hi, n + 1)
                        nc.gpsimd.tensor_tensor(alo[:, f, c0:c0 + w], act32[:, f, 0:w], ahi[:, f, c0:c0 + w],
                                                ALU.subtract).then_inc(a_lo, 1)

        @block.tensor
        def _(pe):
            pe.sem_inc(up_sum, G)
            pe.sem_inc(out_sum, O)
            with pe.Fori(0, parts) as i:
                pe.wait_ge(w_lo[0], i + 1)
                pe.wait_ge(w_lo[1], i + 1)
                for c, (c0, w) in enumerate(CHUNKS):
                    for f in range(F):
                        pe.wait_ge(product, G * i + c * F + f + 1)
                        for m, done in ((0, gate_sum), (1, up_sum)):
                            three_pass(nc, banks[:, 2 * f + m, 0:w], cols(m, whi)[:, f], cols(m, wlo)[:, f],
                                       hhi, hlo, KT, c0, w).then_inc(done, 1)
                pe.wait_ge(w_lo[2], i + 1)
                down = [t[2][:].rearrange("p (f k n) -> p k f n", f=F, k=KT) for t in (whi, wlo)]
                for c, (c0, w) in enumerate(CHUNKS):
                    pe.wait_ge(a_lo, G * i + (c + 2) * F)
                    for k in range(KT):
                        pe.wait_ge(added, O * i + c * KT + k + 1)
                        three_pass(nc, banks[:, 4 + k % 4, 0:w], down[0][:, k], down[1][:, k],
                                   ahi, alo, F, c0, w).then_inc(out_sum, 1)

        @block.vector
        def _(dve):
            dve.sem_inc(product, F)
            dve.sem_inc(added, 4)
            with dve.Fori(0, parts) as i:
                for c, (c0, w) in enumerate(CHUNKS):
                    for f in range(F):
                        n = G * i + c * F + f
                        dve.wait_ge(silu_done, n + 1)
                        dve.wait_ge(up_sum, n + 1 + G)
                        dve.wait_ge(a_lo, n + 1)
                        nc.vector.tensor_tensor(act32[:, f, 0:w], silu[:, f, 0:w], banks[:, 2 * f + 1, 0:w],
                                                ALU.mult).then_inc(product, 1)
                for c, (c0, w) in enumerate(CHUNKS):
                    for k in range(KT):
                        dve.wait_ge(out_sum, O * i + c * KT + k + 1 + O)
                        x = xT[:, k, c0:c0 + w]
                        nc.vector.tensor_tensor(x, x, banks[:, 4 + k % 4, 0:w], ALU.add).then_inc(added, 1)


def final_stage(nc, S, D):
    xT = S["xT"]
    with Stage(nc, "final") as st:
        sq = st.sb("sq", [P, 2, KT, P])
        var = st.sb("var", [P, 2, P])
        rstd = st.sb("rstd", [P, 2, P])
        y = st.sb("y", [P, 2, KT, P])
        out = st.sb("out", [P, 3, D_MODEL])
        mean = st.ps("mean", [P, 2, 512])
        banks = st.ps("banks", [P, 4, 512])
        squared, summed, eps_added, recip, rooted = (st.sem(n) for n in ("squared", "summed", "eps_added", "recip", "rooted"))
        scaled, turned, emptied = st.sem("scaled"), st.sem("turned"), st.sem("emptied")
        stored = [st.sem(f"stored{i}") for i in range(3)]
        block = st.block()

        def copy_out(act, t):
            w = tile_width(t)
            if t >= 3:
                act.wait_ge(stored[t % 3], 16 * (t // 3))
            for j in range(2):
                act.wait_ge(turned, 2 * t + j + 1)
                nc.scalar.activation(out[0:w, t % 3, j * 512:(j + 1) * 512], banks[0:w, (2 * t + j) % 4, :],
                                     ACT.Copy).then_inc(emptied, 1)

        @block.scalar
        def _(act):
            def square(t):
                w = tile_width(t)
                if t >= 2:
                    act.wait_ge(summed, t - 1)
                nc.scalar.activation(sq[:, t % 2, :, 0:w], xT[:, :, t * P:t * P + w], ACT.Square).then_inc(squared, 1)

            square(0)
            for t in range(NT):
                w = tile_width(t)
                if t + 1 < NT:
                    square(t + 1)
                act.wait_ge(recip, t + 1)
                if t >= 2:
                    act.wait_ge(scaled, KT * (t - 1))
                nc.scalar.activation(rstd[:, t % 2, 0:w], var[:, t % 2, 0:w], ACT.Sqrt).then_inc(rooted, 1)
                if t >= 1:
                    copy_out(act, t - 1)
            copy_out(act, NT - 1)

        @block.tensor
        def _(pe):
            def total(t):
                w = tile_width(t)
                pe.wait_ge(squared, t + 1)
                if t >= 2:
                    pe.wait_ge(eps_added, t - 1)
                for k in range(KT):
                    last = nc.tensor.matmul(mean[:, t % 2, 0:w], S["ones"][:], sq[:, t % 2, k, 0:w],
                                            start=(k == 0), stop=(k == KT - 1))
                last.then_inc(summed, 1)

            total(0)
            for t in range(NT):
                w = tile_width(t)
                if t + 1 < NT:
                    total(t + 1)
                for j in range(2):
                    pe.wait_ge(scaled, KT * t + 4 * (j + 1))
                    if t >= 2:
                        pe.wait_ge(emptied, 2 * (t - 2) + j + 1)
                    for q in range(4):
                        last = nc.tensor.transpose(banks[0:w, (2 * t + j) % 4, q * P:(q + 1) * P],
                                                   y[:, t % 2, 4 * j + q, 0:w], S["ident"][:])
                    last.then_inc(turned, 1)

        @block.vector
        def _(dve):
            def reciprocal(t):
                w = tile_width(t)
                dve.wait_ge(summed, t + 1)
                if t >= 2:
                    dve.wait_ge(rooted, t - 1)
                nc.vector.tensor_scalar(var[:, t % 2, 0:w], mean[:, t % 2, 0:w], 1.0 / D_MODEL, EPS, ALU.mult,
                                        ALU.add).then_inc(eps_added, 1)
                dve.wait_ge(eps_added, t + 1)
                nc.vector.reciprocal(var[:, t % 2, 0:w], var[:, t % 2, 0:w]).then_inc(recip, 1)

            reciprocal(0)
            for t in range(NT):
                w = tile_width(t)
                if t + 1 < NT:
                    reciprocal(t + 1)
                dve.wait_ge(rooted, t + 1)
                if t >= 2:
                    dve.wait_ge(turned, 2 * (t - 1))
                for k in range(KT):
                    nc.vector.scalar_tensor_tensor(
                        out=y[:, t % 2, k, 0:w], in0=xT[:, k, t * P:t * P + w],
                        scalar=S["gains"][:, G_FINAL + k:G_FINAL + k + 1], in1=rstd[:, t % 2, 0:w],
                        op0=ALU.mult, op1=ALU.mult).then_inc(scaled, 1)

        @block.sync
        def _(sp):
            for t in range(NT):
                w = tile_width(t)
                sp.wait_ge(emptied, 2 * t + 2)
                dst = D["y_prompt"][t * P:t * P + w, :] if t < SEQ // P else D["y_sample"]
                sp.dma_start(dst, out[0:w, t % 3, :]).then_inc(stored[t % 3], 16)
            for i in range(3):
                sp.wait_ge(stored[i], 16 * ((NT - i + 2) // 3))



def latent_stage(nc, S, D):
    RQ, RK = Q_RANK // P, KV_RANK // P
    CT = PAST_LEN // P
    cqT, ckvT, kT = S["cqT"], S["ckvT"], S["kT"]
    lo, hi = B_NOPE, B_NOPE + B_ROPE
    with Stage(nc, "latent") as st:
        sq = st.sb("sq", [P, RQ, T])
        var = st.sb("var", [P, 2, T])
        krs = st.sb("krs", [P, T])
        cs = st.sb("cs", [P, 2, T])
        cache = st.sb("cache", [P, CT, KV_RANK])
        rcache = st.sb("rcache", [P, CT, B_ROPE])
        rows = st.sb("rows", [P, NT, KV_RANK])
        rrows = st.sb("rrows", [P, NT, B_ROPE])
        mean = st.ps("mean", [P, 2, NC, 512])
        turn = st.ps("turn", [P, 2, 512])
        z_in, c_in = st.sem("z_in"), st.sem("c_in")
        squared, summed, var_done, rooted, normed = (st.sem(x) for x in ("squared", "summed", "var_done", "rooted", "normed"))
        dve_step, turned, copied, out, krope = (st.sem(x) for x in ("dve_step", "turned", "copied", "out", "krope"))
        block = st.block()
        lat = [(cqT, RQ, G_Q, Q_RANK), (ckvT, RK, G_KV, KV_RANK)]

        @block.sync
        def _(sp):
            sp.dma_start(cqT[:], D["z"][Z_CQ:Z_CKV, :].rearrange("(k p) t -> p k t", p=P)).then_inc(z_in, 16)
            sp.dma_start(ckvT[:, :, 0:T], D["z"][Z_CKV:Z_MISC, :].rearrange("(k p) t -> p k t", p=P)).then_inc(z_in, 16)
            sp.dma_start(kT[lo:hi, 0, 0:T], D["z"][Z_KR:Z_KR + B_ROPE, :]).then_inc(c_in, 16)
            sp.dma_start(krs[lo:hi, :], D["z"][Z_KRS:Z_KRS + B_ROPE, :]).then_inc(c_in, 16)
            sp.dma_start(cs[lo:hi], D["rope_k"]).then_inc(c_in, 16)
            sp.dma_start(cache[:], D["c_ckv"].rearrange("(c p) r -> p c r", p=P)).then_inc(c_in, 16)
            sp.dma_start(rcache[:], D["c_krope"].rearrange("(c p) r -> p c r", p=P)).then_inc(c_in, 16)
            sp.wait_ge(copied, 2 * CT + 2 * NT)
            for dst, src in (("ckv", rows), ("krope", rrows)):
                sp.dma_start(D["p_" + dst].rearrange("(c p) r -> p c r", p=P), src[:, 0:NT - 1, :]).then_inc(out, 16)
                sp.dma_start(D["s_" + dst], src[0:DEC_SEQ, NT - 1, :]).then_inc(out, 16)
            sp.wait_ge(out, 64)

        @block.scalar
        def _(act):
            for i, (x, kts, _, _) in enumerate(lat):
                act.wait_ge(z_in, 32)
                if i:
                    act.wait_ge(summed, NC)
                nc.scalar.activation(sq[:, 0:kts, :], x[:, :, 0:T], ACT.Square).then_inc(squared, 1)
            for i in range(2):
                act.wait_ge(var_done, 2 * NC * (i + 1))
                nc.scalar.activation(var[:, i], var[:, i], ACT.Sqrt).then_inc(rooted, 1)

        @block.tensor
        def _(pe):
            for i, (_, kts, _, _) in enumerate(lat):
                pe.wait_ge(squared, i + 1)
                for c, (c0, w) in enumerate(CHUNKS):
                    for k in range(kts):
                        last = nc.tensor.matmul(mean[:, i, c, 0:w], S["ones"][:], sq[:, k, c0:c0 + w],
                                                start=(k == 0), stop=(k == kts - 1))
                    last.then_inc(summed, 1)
            pe.wait_ge(c_in, 16 * 5)
            m = 0
            for c in range(CT):
                if m >= 2:
                    pe.wait_ge(copied, m - 1)
                for k in range(RK):
                    last = nc.tensor.transpose(turn[:, m % 2, k * P:(k + 1) * P], cache[:, c, k * P:(k + 1) * P], S["ident"][:])
                last.then_inc(turned, 1)
                m += 1
            for c in range(CT):
                pe.wait_ge(copied, m - 1)
                nc.tensor.transpose(turn[0:B_ROPE, m % 2, 0:P], rcache[:, c, :], S["ident"][:]).then_inc(turned, 1)
                m += 1
            pe.wait_ge(normed, RQ + RK)
            pe.wait_ge(krope, 3)
            for c in range(NT):
                w = tile_width(c)
                pe.wait_ge(copied, m - 1)
                for k in range(RK):
                    last = nc.tensor.transpose(turn[0:w, m % 2, k * P:(k + 1) * P], ckvT[:, k, c * P:c * P + w], S["ident"][:])
                last.then_inc(turned, 1)
                m += 1
            for c in range(NT):
                w = tile_width(c)
                pe.wait_ge(copied, m - 1)
                nc.tensor.transpose(turn[0:w, m % 2, 0:B_ROPE], kT[lo:hi, 0, c * P:c * P + w],
                                    S["ident"][lo:hi, lo:hi]).then_inc(turned, 1)
                m += 1

        @block.vector
        def _(dve):
            v = nc.vector
            dve.wait_ge(c_in, 16 * 5)
            kr = kT[lo:hi, 0, 0:T]
            v.tensor_tensor(kr, kr, cs[lo:hi, 0], ALU.mult).then_inc(dve_step, 1)
            v.tensor_tensor(krs[lo:hi], krs[lo:hi], cs[lo:hi, 1], ALU.mult).then_inc(dve_step, 1)
            dve.wait_ge(dve_step, 2)
            v.tensor_tensor(kr, kr, krs[lo:hi], ALU.add).then_inc(krope, 1)
            m = 0
            for c in range(CT):
                dve.wait_ge(turned, m + 1)
                v.tensor_copy(ckvT[:, :, T + c * P:T + (c + 1) * P],
                              turn[:, m % 2, 0:RK * P].rearrange("p (k n) -> p k n", k=RK)).then_inc(copied, 1)
                m += 1
            for c in range(CT):
                dve.wait_ge(turned, m + 1)
                v.tensor_copy(kT[lo:hi, 0, T + c * P:T + (c + 1) * P], turn[0:B_ROPE, m % 2, 0:P]).then_inc(copied, 1)
                m += 1
            dve.wait_ge(krope, 1)
            dve.wait_ge(copied, m)
            v.tensor_copy(kT[lo:hi, 1, :], kT[lo:hi, 0, :]).then_inc(krope, 2)
            n = 0
            for i, (x, kts, g0, rank) in enumerate(lat):
                for c, (c0, w) in enumerate(CHUNKS):
                    dve.wait_ge(summed, NC * i + c + 1)
                    v.tensor_scalar(var[:, i, c0:c0 + w], mean[:, i, c, 0:w], 1.0 / rank, EPS, ALU.mult, ALU.add)\
                     .then_inc(var_done, 1)
                    n += 1
                    dve.wait_ge(var_done, n)
                    v.reciprocal(var[:, i, c0:c0 + w], var[:, i, c0:c0 + w]).then_inc(var_done, 1)
                    n += 1
            for i, (x, kts, g0, rank) in enumerate(lat):
                dve.wait_ge(rooted, i + 1)
                for k in range(kts):
                    v.scalar_tensor_tensor(out=x[:, k, 0:T], in0=x[:, k, 0:T], scalar=S["gains"][:, g0 + k:g0 + k + 1],
                                           in1=var[:, i], op0=ALU.mult, op1=ALU.mult).then_inc(normed, 1)
            for c in range(NT):
                w = tile_width(c)
                dve.wait_ge(turned, m + 1)
                v.tensor_copy(rows[0:w, c, :], turn[0:w, m % 2, 0:KV_RANK]).then_inc(copied, 1)
                m += 1
            for c in range(NT):
                w = tile_width(c)
                dve.wait_ge(turned, m + 1)
                v.tensor_copy(rrows[0:w, c, :], turn[0:w, m % 2, 0:B_ROPE]).then_inc(copied, 1)
                m += 1


def attention_stage(nc, S, D, kind):
    mla = kind == "mla"
    pairs = (B_HEADS if mla else C_HEADS) // 2
    cat0 = (A_HEADS * A_DIM // P) if mla else 0
    N = 2 * NT
    CT = PAST_LEN // P
    VT = NT + CT
    H = 64
    RQ, RK = Q_RANK // P, KV_RANK // P
    hhi, hlo = S["hhi"], S["hlo"]

    def key_tiles(t):
        if t == NT - 1:
            return [(T + c * P, P, NT + c) for c in range(CT)] + [(SEQ, DEC_SEQ, NT - 1)]
        first = 0 if mla else max(0, t - 4)
        return [(j * P, P, j) for j in range(first, t + 1)]

    if mla:
        KC = [(c, 400) for c in range(0, KEYS, 400)]
        items = [("knope", i, 1, 1) for i in range(len(KC))] + [("qnope", i, 1, 1) for i in range(NC)]
        for i in range(NC):
            items += [("qrope", i, 0, 1), ("qswap", i, 0, 1)]
        items += [("v", i, 0, 1) for i in range(4)]
    else:
        items = [("kcache", 0, 0, 1), ("v", 0, 0, 1), ("k", 0, 1, 0), ("v", 1, 0, 1), ("k", 1, 1, 0), ("v", 2, 0, 1)]
    NI = len(items)
    act_before = [sum(x[2] for x in items[:m]) for m in range(NI + 1)]
    dve_before = [sum(x[3] for x in items[:m]) for m in range(NI + 1)]
    NA, ND = act_before[-1], dve_before[-1]

    with Stage(nc, kind) as st:
        V = st.sb("V", [P, VT, P])
        p = st.sb("p", [P, 2, 1024])
        pT = st.sb("pT", [P, 2, 1024])
        neg_max, total, inv = (st.sb(x, [P, N]) for x in ("neg_max", "total", "inv"))
        o = st.sb("o", [P, 2, P])
        if mla:
            kT = S["kT"]
            qT = st.sb("qT", [B_NOPE + B_ROPE, 2, T])
            w_nope, w_rope, w_swap = st.sb("w_nope", [P, RQ, P]), st.sb("w_rope", [P, RQ, 64]), st.sb("w_swap", [P, RQ, 64])
            w_uk, w_uv = st.sb("w_uk", [P, RK, P]), st.sb("w_uv", [P, RK, P])
            rope = st.sb("rope", [64, 2, T])
            t1, t2 = st.sb("t1", [64, T]), st.sb("t2", [64, T])
        else:
            qin, kin, vin = (st.sb(x, [P, T]) for x in ("qin", "kin", "vin"))
            cin = st.sb("cin", [P, CT, P])
            bin_ = st.sb("bin", [P, 2, 256])
            qT, kT = st.sb("qT", [P, T]), st.sb("kT", [P, KEYS])
            ktok = st.sb("ktok", [P, 5, P])
            far = st.sb("far", [P, 2])
            bias = st.sb("bias", [P, 2, 256])
        pS = st.ps("pS", [P, 4, 512])
        pP = st.ps("pP", [P, 2, 512])
        pO = st.ps("pO", [P, 512])
        pOT = st.ps("pOT", [P, 512])
        names = ("loaded", "prepped", "act_kept", "dve_kept", "pool_kept", "tables", "scored", "biased", "maxed",
                 "exped", "turned", "p_kept", "summed", "inverted", "normed", "o_turned", "hi", "lo", "apart",
                 "stored", "far_done", "bias_done", "v_loaded")
        s = {x: st.sem(x) for x in names}
        block = st.block()

        def value_tiles(i):
            tiles = [(j * P, tile_width(j), j) for j in range(NT)] + [(T + c * P, P, NT + c) for c in range(CT)]
            return [tiles[j] for j in (range(0, 4), range(4, 8), range(NT, VT), range(8, 9))[i]]

        def q_of(t, e):
            w = tile_width(t)
            return qT[:, e, t * P:t * P + w] if mla else qT[H * e:H * e + H, t * P:t * P + w]

        def k_of(e, c0, w):
            return kT[:, e, c0:c0 + w] if mla else kT[H * e:H * e + H, c0:c0 + w]

        def scores_of(n):
            return pS[:, 2 * (n % 2):2 * (n % 2) + 2, :].rearrange("p b n -> p (b n)")

        turned_of = pP[:].rearrange("p b n -> p (b n)")

        def head_out(t, hp):
            w = tile_width(t)
            cols = slice(t * P, t * P + w)
            return [x[:, bass.ds(hp + cat0, 1), cols].rearrange("p a n -> p (a n)") for x in (hhi, hlo)]

        @block.sync
        def _(sp):
            def load(hp):
                if mla:
                    for dst, name, width in ((w_nope, "w_qn", P), (w_rope, "w_qr", 64), (w_swap, "w_qs", 64),
                                             (w_uk, "w_uk", P), (w_uv, "w_uv", P)):
                        src = D[name].rearrange("(k p) n -> p k n", p=P)[:, :, bass.ds(hp * width, width)]
                        sp.dma_start(dst[:], src).then_inc(s["loaded"], 16)
                else:
                    for i, dst in enumerate((qin, kin, vin)):
                        sp.dma_start(dst[:], D["z"][bass.ds(hp * P + i * D_MODEL, P), :]).then_inc(s["loaded"], 16)
                    src = D["c_k"].rearrange("(c p) n -> p c n", p=P)[:, :, bass.ds(hp * P, P)]
                    sp.dma_start(cin[:], src).then_inc(s["loaded"], 16)
                    sp.dma_start(bin_[:], D["bias"][bass.ds(2 * hp, 2), :, :].rearrange("h p j -> p h j"))\
                      .then_inc(s["loaded"], 16)

            def store(hp):
                col = bass.ds(hp * P, P)
                sp.wait_ge(s["act_kept"], NA * hp + NA)
                sp.sem_inc(s["apart"], 1)
                sp.wait_ge(s["dve_kept"], ND * hp + ND)
                sp.sem_inc(s["apart"], 1)
                for src, new, kv in ((ktok[:, 0:4, :], ktok[0:DEC_SEQ, 4, :], "bk"), (V[:, 4:8, :], V[0:DEC_SEQ, 8, :], "bv")):
                    sp.dma_start(D["p_" + kv].rearrange("(c p) n -> p c n", p=P)[:, :, col], src).then_inc(s["stored"], 16)
                    sp.dma_start(D["s_" + kv][PAST_LEN - DEC_SEQ:PAST_LEN, col], new).then_inc(s["stored"], 16)

            def load_v(hp):
                src = D["c_v"].rearrange("(c p) n -> p c n", p=P)[:, :, bass.ds(hp * P, P)]
                sp.dma_start(V[:, NT:VT, :], src).then_inc(s["v_loaded"], 16)

            if mla:
                sp.dma_start(rope[:], D["rope_q"]).then_inc(s["tables"], 16)
            load(0)
            if not mla:
                load_v(0)
                for kv in ("k", "v"):
                    sp.dma_start(D["s_b" + kv][0:PAST_LEN - DEC_SEQ, :], D["c_" + kv][DEC_SEQ:PAST_LEN, :])\
                      .then_inc(s["tables"], 16)
            with sp.Fori(1, pairs) as hp:
                sp.wait_ge(s["prepped"], NI * hp)
                if not mla:
                    sp.sem_inc(s["apart"], 1)
                    sp.wait_ge(s["pool_kept"], 2 * hp)
                    sp.wait_ge(s["far_done"], 2 * hp)
                sp.sem_inc(s["apart"], 1)
                load(hp)
                if not mla:
                    store(hp - 1)
                    sp.wait_ge(s["summed"], N * hp + 2)
                    sp.sem_inc(s["apart"], 1)
                    load_v(hp)
            if not mla:
                store(pairs - 1)
                sp.wait_ge(s["stored"], 64 * pairs + 64)
                sp.wait_ge(s["tables"], 32)

        @block.tensor
        def _(pe):
            pe.sem_inc(s["summed"], 2)
            pe.sem_inc(s["o_turned"], 2)

            def start_item(hp, m):
                if m >= 4:
                    if act_before[m - 3] > 0:
                        pe.wait_ge(s["act_kept"], NA * hp + act_before[m - 3])
                    if dve_before[m - 3] > 0:
                        pe.wait_ge(s["dve_kept"], ND * hp + dve_before[m - 3])

            def prepare(hp):
                pe.wait_ge(s["exped"], N * hp + 2)
                pe.wait_ge(s["loaded"], 80 * hp + 80)
                for m, (name, i, _, _) in enumerate(items):
                    start_item(hp, m)
                    bank = pS[:, m % 4, :]
                    if name == "knope":
                        c0, w = KC[i]
                        parts = [(bank[:, 0:w], w_uk[:, k, :], S["ckvT"][:, k, c0:c0 + w], k, RK) for k in range(RK)]
                    elif name in ("qnope", "qrope", "qswap"):
                        c0, w = CHUNKS[i]
                        wt = {"qnope": w_nope, "qrope": w_rope, "qswap": w_swap}[name]
                        M = P if name == "qnope" else 64
                        parts = [(bank[0:M, 0:w], wt[:, k, :], S["cqT"][:, k, c0:c0 + w], k, RQ) for k in range(RQ)]
                    elif mla:
                        parts = []
                        for q, (c0, w, _) in enumerate(value_tiles(i)):
                            parts += [(bank[0:w, q * P:(q + 1) * P], S["ckvT"][:, k, c0:c0 + w], w_uv[:, k, :], k, RK)
                                      for k in range(RK)]
                    else:
                        parts = None
                        src = {"kcache": None, "v": vin, "k": kin}[name]
                        tiles = range(4) if name == "kcache" else {"v": (range(0, 4), range(4, 8), range(8, 9)),
                                                                   "k": (range(4, 8), range(8, 9))}[name][i]
                        for q, c in enumerate(tiles):
                            if src is None:
                                last = nc.tensor.transpose(bank[:, q * P:(q + 1) * P], cin[:, c, :], S["ident"][:])
                            else:
                                w = tile_width(c)
                                if w < P:
                                    pe.sem_inc(s["apart"], 1)
                                last = nc.tensor.transpose(bank[0:w, q * P:(q + 1) * P], src[:, c * P:c * P + w],
                                                           S["ident"][:])
                    for out, lhsT, rhs, k, kts in parts or []:
                        last = nc.tensor.matmul(out, lhsT, rhs, start=(k == 0), stop=(k == kts - 1))
                    last.then_inc(s["prepped"], 1)
                pe.wait_ge(s["act_kept"], NA * hp + NA)
                pe.wait_ge(s["dve_kept"], ND * hp + ND)
                if not mla:
                    pe.wait_ge(s["pool_kept"], 2 * hp + 2)
                    pe.wait_ge(s["v_loaded"], 16 * hp + 16)

            def score(hp, n):
                t, e = n // 2, n % 2
                w = tile_width(t)
                tiles = key_tiles(t)
                W = sum(x[1] for x in tiles)
                pe.wait_ge(s["exped"], N * hp + n + 1)
                if w < P:
                    pe.sem_inc(s["apart"], 1)
                out = scores_of(n)
                masks = []
                if t < NT - 1 and mla:
                    masks.append((0, W - CHUNK))
                if t >= 4 and t < NT - 1 and not mla:
                    masks.append((1, 0))
                runs = []
                c = 0
                for k0, kw, _ in tiles:
                    if runs and runs[-1][1] + runs[-1][2] == k0 and runs[-1][2] + kw <= 512 and c % 512:
                        runs[-1][2] += kw
                    else:
                        runs.append([c, k0, kw])
                    c += kw
                for r, (c, k0, kw) in enumerate(runs):
                    here = [m for m in masks if c <= m[1] < c + kw]
                    last = nc.tensor.matmul(out[0:w, c:c + kw], q_of(t, e), k_of(e, k0, kw), start=True, stop=not here)
                    for half, mc in here:
                        last = nc.tensor.matmul(out[0:w, mc:mc + CHUNK], S["halves"][0:1, half * P:half * P + w],
                                                S["halves"][0:1, 2 * P:2 * P + CHUNK], start=False, stop=True)
                last.then_inc(s["scored"], 1)

            def turn(hp, n):
                t = n // 2
                w = tile_width(t)
                pe.wait_ge(s["exped"], N * hp + n + 3)
                pe.wait_ge(s["p_kept"], N * hp + n + 1)
                if w < P:
                    pe.sem_inc(s["apart"], 1)
                c = 0
                for b, (_, kw, _) in enumerate(key_tiles(t)):
                    last = nc.tensor.transpose(turned_of[0:kw, b * P:b * P + w], p[0:w, n % 2, c:c + kw], S["ident"][0:w, 0:w])
                    c += kw
                last.then_inc(s["turned"], 1)

            def weigh(hp, n):
                t, e = n // 2, n % 2
                w = tile_width(t)
                tiles = key_tiles(t)
                pe.wait_ge(s["p_kept"], N * hp + n + 2)
                pe.wait_ge(s["normed"], N * hp + n + 1)
                if w < P:
                    pe.sem_inc(s["apart"], 1)
                for b, (_, kw, vt) in enumerate(tiles):
                    last = nc.tensor.matmul(pO[0:w, 0:H], pT[0:kw, n % 2, b * P:b * P + w],
                                            V[0:kw, vt, e * H:(e + 1) * H], start=(b == 0), stop=(b == len(tiles) - 1))
                last.then_inc(s["summed"], 1)

            def turn_out(hp, t):
                w = tile_width(t)
                pe.wait_ge(s["normed"], N * hp + 2 * t + 2 + 1)
                pe.wait_ge(s["lo"], NT * hp + t + 1)
                if w < P:
                    pe.sem_inc(s["apart"], 1)
                nc.tensor.transpose(pOT[:, 0:w], o[0:w, t % 2, :], S["ident"][0:w, 0:w]).then_inc(s["o_turned"], 1)

            with pe.Fori(0, pairs) as hp:
                prepare(hp)
                for n in range(-1, N + 3):
                    if n + 1 < N:
                        score(hp, n + 1)
                    if 0 <= n < N:
                        turn(hp, n)
                    if 0 <= n - 1 < N:
                        weigh(hp, n - 1)
                    if n >= 4 and n % 2 == 0:
                        turn_out(hp, (n - 4) // 2)

        @block.scalar
        def _(act):
            act.sem_inc(s["exped"], 2)
            act.sem_inc(s["p_kept"], 1)

            def exp(hp, n):
                t = n // 2
                w = tile_width(t)
                W = sum(x[1] for x in key_tiles(t))
                act.wait_ge(s["maxed"], N * hp + n + 1)
                nc.scalar.activation(p[0:w, n % 2, 0:W], scores_of(n)[0:w, 0:W], ACT.Exp, bias=neg_max[0:w, n:n + 1],
                                     accum_out=total[0:w, n:n + 1]).then_inc(s["exped"], 1)

            def keep(hp, n):
                t = n // 2
                w = tile_width(t)
                tiles = key_tiles(t)
                act.wait_ge(s["turned"], N * hp + n + 1)
                act.wait_ge(s["summed"], N * hp + n + 1)
                if w == P:
                    cols = len(tiles) * P
                    nc.scalar.activation(pT[:, n % 2, 0:cols], turned_of[:, 0:cols], ACT.Copy).then_inc(s["p_kept"], 1)
                else:
                    wide = lambda x: x.rearrange("p (b n) -> p b n", n=P)[:, 0:CT, 0:w]
                    nc.scalar.activation(wide(pT[:, n % 2, :]), wide(turned_of), ACT.Copy)
                    nc.scalar.activation(pT[0:DEC_SEQ, n % 2, CT * P:CT * P + w], turned_of[0:DEC_SEQ, CT * P:CT * P + w],
                                         ACT.Copy).then_inc(s["p_kept"], 1)

            def high(hp, t):
                w = tile_width(t)
                act.wait_ge(s["o_turned"], NT * hp + t + 3)
                nc.scalar.activation(head_out(t, hp)[0], pOT[:, 0:w], ACT.Copy).then_inc(s["hi"], 1)

            with act.Fori(0, pairs) as hp:
                for m, (name, i, mine, _) in enumerate(items):
                    if not mine:
                        continue
                    act.wait_ge(s["prepped"], NI * hp + m + 1)
                    bank = pS[:, m % 4, :]
                    if name == "knope":
                        c0, w = KC[i]
                        nc.scalar.activation(kT[0:B_NOPE, 0, c0:c0 + w], bank[0:B_NOPE, 0:w], ACT.Copy).then_inc(s["act_kept"], 1)
                    elif name == "qnope":
                        c0, w = CHUNKS[i]
                        nc.scalar.activation(qT[0:B_NOPE, 0, c0:c0 + w], bank[0:B_NOPE, 0:w], ACT.Copy, scale=MLA_SCALE)\
                          .then_inc(s["act_kept"], 1)
                    else:
                        if hp is not None and i == 0:
                            act.wait_ge(s["stored"], 64 * hp + 64)
                        w = P if i == 0 else DEC_SEQ
                        dst = ktok[:, 0:4, :].rearrange("p c n -> p (c n)") if i == 0 else ktok[0:w, 4, :]
                        nc.scalar.activation(dst, bank[0:w, 0:512 if i == 0 else P], ACT.Copy).then_inc(s["act_kept"], 1)
                for n in range(-1, N + 3):
                    if n + 1 < N:
                        exp(hp, n + 1)
                    if 0 <= n < N:
                        keep(hp, n)
                    if n >= 4 and n % 2 == 0:
                        high(hp, (n - 4) // 2)

        @block.vector
        def _(dve):
            v = nc.vector
            dve.sem_inc(s["normed"], 1)
            dve.sem_inc(s["lo"], 1)
            if mla:
                dve.wait_ge(s["tables"], 16)
            else:
                dve.sem_inc(s["stored"], 64)

            def kept(name, i, bank, hp):
                if name == "knope":
                    c0, w = KC[i]
                    return v.tensor_copy(kT[0:B_NOPE, 1, c0:c0 + w], bank[B_NOPE:2 * B_NOPE, 0:w])
                if name == "qnope":
                    c0, w = CHUNKS[i]
                    return v.tensor_scalar(qT[0:B_NOPE, 1, c0:c0 + w], bank[B_NOPE:2 * B_NOPE, 0:w], MLA_SCALE, None, ALU.mult)
                if name in ("qrope", "qswap"):
                    c0, w = CHUNKS[i]
                    dst, table = (t1, 0) if name == "qrope" else (t2, 1)
                    return v.tensor_tensor(dst[:, c0:c0 + w], rope[:, table, c0:c0 + w], bank[0:64, 0:w], ALU.mult)
                if name == "kcache":
                    return v.tensor_copy(kT[:, T:KEYS], bank)
                if mla:
                    tiles = value_tiles(i)
                    w, first, count = tiles[0][1], tiles[0][2], len(tiles)
                else:
                    w, first, count = (P, 4 * i, 4) if i < 2 else (DEC_SEQ, 8, 1)
                return v.tensor_copy(V[0:w, first:first + count, :].rearrange("p c n -> p (c n)"), bank[0:w, 0:count * P])

            def prepare(hp):
                if not mla:
                    dve.wait_ge(s["loaded"], 80 * hp + 80)
                    v.tensor_copy(far[:], bin_[:, :, 0]).then_inc(s["far_done"], 1)
                    dve.wait_ge(s["far_done"], 2 * hp + 1)
                    for e in range(2):
                        last = v.tensor_scalar(bias[:, e, :], bin_[:, e, :], far[:, e:e + 1], None, ALU.subtract)
                    last.then_inc(s["far_done"], 1)
                    dve.wait_ge(s["far_done"], 2 * hp + 2)
                    v.memset(bias[0:CHUNK, :, 256 - CHUNK:256], NEG).then_inc(s["bias_done"], 1)
                    dve.wait_ge(s["bias_done"], hp + 1)
                    dve.wait_ge(s["stored"], 64 * hp + 64)
                for m, (name, i, _, mine) in enumerate(items):
                    if not mine:
                        continue
                    dve.wait_ge(s["prepped"], NI * hp + m + 1)
                    ins = kept(name, i, pS[:, m % 4, :], hp)
                    if name == "qswap":
                        ins.then_inc(s["inverted"], 1)
                        dve.wait_ge(s["inverted"], (N + NC) * hp + i + 1)
                        c0, w = CHUNKS[i]
                        for e in range(2):
                            ins = v.tensor_tensor(qT[B_NOPE:B_NOPE + B_ROPE, e, c0:c0 + w],
                                                  t1[e * B_ROPE:(e + 1) * B_ROPE, c0:c0 + w],
                                                  t2[e * B_ROPE:(e + 1) * B_ROPE, c0:c0 + w], ALU.add)
                    ins.then_inc(s["dve_kept"], 1)

            def maximum(hp, n):
                t, e = n // 2, n % 2
                w = tile_width(t)
                W = sum(x[1] for x in key_tiles(t))
                x = scores_of(n)
                dve.wait_ge(s["scored"], N * hp + n + 1)
                if not mla:
                    near = (P, 128, 256) if t == 0 else (256, 0, 256)
                    if t == NT - 1:
                        near = (192, 0, 192)
                    cols = x[0:w, W - near[0]:W]
                    v.tensor_tensor(cols, cols, bias[0:w, e, near[1]:near[2]], ALU.add).then_inc(s["biased"], 1)
                    dve.wait_ge(s["biased"], N * hp + n + 1)
                v.tensor_reduce(neg_max[0:w, n:n + 1], x[0:w, 0:W], AX_X, ALU.max, negate=True).then_inc(s["maxed"], 1)

            def norm(hp, n):
                t, e = n // 2, n % 2
                w = tile_width(t)
                dve.wait_ge(s["summed"], N * hp + n + 3)
                v.reciprocal(inv[0:w, n:n + 1], total[0:w, n:n + 1]).then_inc(s["inverted"], 1)
                dve.wait_ge(s["inverted"], (N + NC) * hp + NC + n + 1 if mla else N * hp + n + 1)
                dve.wait_ge(s["o_turned"], NT * hp + t + 1)
                v.tensor_scalar(o[0:w, t % 2, e * H:(e + 1) * H], pO[0:w, 0:H],
                                inv[0:w, n:n + 1], None, ALU.mult).then_inc(s["normed"], 1)

            def low(hp, t):
                w = tile_width(t)
                dve.wait_ge(s["hi"], NT * hp + t + 1)
                hi_, lo_ = head_out(t, hp)
                v.tensor_tensor(lo_, pOT[:, 0:w], hi_, ALU.subtract).then_inc(s["lo"], 1)

            with dve.Fori(0, pairs) as hp:
                prepare(hp)
                for n in range(-1, N + 3):
                    if n + 1 < N:
                        maximum(hp, n + 1)
                    if 0 <= n - 1 < N:
                        norm(hp, n - 1)
                    if n >= 4 and n % 2 == 0:
                        low(hp, (n - 4) // 2)

        if not mla:
            @block.gpsimd
            def _(pool):
                with pool.Fori(0, pairs) as hp:
                    pool.wait_ge(s["loaded"], 80 * hp + 80)
                    pool.wait_ge(s["summed"], N * hp + 2)
                    pool.sem_inc(s["apart"], 1)
                    nc.gpsimd.tensor_scalar(qT[:], qin[:], C_SCALE, None, ALU.mult).then_inc(s["pool_kept"], 1)
                    nc.gpsimd.tensor_copy(kT[:, 0:T], kin[:]).then_inc(s["pool_kept"], 1)


def build(nc, D):
    with ExitStack() as ctx:
        def sb(name, shape, dt=F32):
            return ctx.enter_context(nc.sbuf_tensor(name, shape, dt))
        S = {"ident": sb("ident", [P, P]), "ones": sb("ones", [P, P]), "gains": sb("gains", [P, G_COLS]),
             "halves": sb("halves", [1, 2 * P + CHUNK]),
             "xT": sb("xT", [P, KT, T]), "hhi": sb("hhi", [P, KT, T], F32R), "hlo": sb("hlo", [P, KT, T], F32R)}
        load_stage(nc, S, D)
        norm_stage(nc, S, "mix0", G_MIX0)
        project_stage(nc, S, "in0", D["w_in"], Z_ROWS // UNIT, D["z"])
        with Stage(nc, "recur") as st:
            S["aT"], S["enm"], S["wk"], S["decay"] = (st.sb(x, [P, R]) for x in ("aT", "enm", "wk", "decay"))
            S["upper"], S["lower"] = st.sb("upper", [P, P]), st.sb("lower", [P, P])
            gate_stage(nc, S, D)
            mlstm_stage(nc, S, D)
        with Stage(nc, "latents") as st:
            S["cqT"], S["ckvT"] = st.sb("cqT", [P, Q_RANK // P, T]), st.sb("ckvT", [P, KV_RANK // P, KEYS])
            S["kT"] = st.sb("kT", [B_NOPE + B_ROPE, 2, KEYS])
            latent_stage(nc, S, D)
            attention_stage(nc, S, D, "mla")
        project_stage(nc, S, "out0", D["w_out0"], D_MODEL // UNIT)
        norm_stage(nc, S, "ffn0n", G_FFN0)
        ffn_stage(nc, S, "ffn0", D["w_gate"][0], D["w_up"][0], D["w_down"][0])
        norm_stage(nc, S, "mix1", G_MIX1)
        project_stage(nc, S, "in1", D["w_qkv"], 3 * D_MODEL // UNIT, D["z"])
        attention_stage(nc, S, D, "band")
        project_stage(nc, S, "out1", D["w_out1"], D_MODEL // UNIT)
        norm_stage(nc, S, "ffn1n", G_FFN1)
        ffn_stage(nc, S, "ffn1", D["w_gate"][1], D["w_up"][1], D["w_down"][1])
        final_stage(nc, S, D)


_OUTS = [("y_prompt", (1024, 1024), (1, 1024, 1024)), ("y_sample", (64, 1024), (1, 64, 1024)),
         ("p_ckv", (1024, 256), (1, 1, 1024, 256)), ("p_krope", (1024, 32), (1, 1, 1024, 32)),
         ("p_C", (4, 128, 128), (1, 1, 4, 128, 128)), ("p_n", (4, 128, 1), (1, 1, 4, 128)), ("p_m", (1, 4), (1, 1, 4)),
         ("p_bk", (512, 1024), (1, 1, 512, 16, 64)), ("p_bv", (512, 1024), (1, 1, 512, 16, 64)),
         ("s_ckv", (64, 256), (1, 1, 64, 256)), ("s_krope", (64, 32), (1, 1, 64, 32)),
         ("s_C", (4, 128, 128), (1, 1, 4, 128, 128)), ("s_n", (4, 128, 1), (1, 1, 4, 128)), ("s_m", (1, 4), (1, 1, 4)),
         ("s_bk", (512, 1024), (1, 1, 512, 16, 64)), ("s_bv", (512, 1024), (1, 1, 512, 16, 64))]
_SCRATCH = [("z", (3072, T)), ("gates", (2, A_HEADS, NT * P)), ("u", (A_HEADS, NT * P)), ("w", (A_HEADS, NT * P)),
            ("bias", (C_HEADS, P, 2 * P))]


def _rope_tables():
    half = B_ROPE // 2
    inv = np.float32(10000.0) ** (-np.arange(half, dtype=np.float32) / np.float32(half))
    pos = np.concatenate([np.arange(SEQ), PAST_LEN + np.arange(DEC_SEQ)]).astype(np.float32)
    ang = (pos[:, None] * inv[None, :]).astype(np.float32)
    cos, sin = np.cos(ang).T, np.sin(ang).T
    return np.stack([np.concatenate([cos, cos]), np.concatenate([-sin, sin])], 1).astype(np.float32)


def _layout(i):
    def cols(g):
        return g.reshape(-1, P).T

    w = i["w_in_ab"][0]
    a = 4 * A_HEADS * A_DIM
    b = a + 2 * A_HEADS
    kr = w[:, b + Q_RANK + KV_RANK:]
    pad = np.zeros((D_MODEL, 32 - A_HEADS), np.float32)
    w_in = np.concatenate([w[:, :a], w[:, b:], kr[:, 16:], kr[:, :16], w[:, a:a + A_HEADS], pad,
                           w[:, a + A_HEADS:b], pad], 1)
    uq = i["mla_w_uq"][0].reshape(Q_RANK, B_HEADS, B_NOPE + B_ROPE)
    rot = uq[:, :, B_NOPE:]
    rel = i["rel_bias_c"][0]
    gains = [i["norm_mix"][0], i["norm_ffn"][0], i["norm_mix"][1], i["norm_ffn"][1], i["norm_final"],
             i["mla_q_norm"][0], i["mla_kv_norm"][0], i["mlstm_hnorm"][0]]
    table = _rope_tables()
    halves = np.concatenate([np.repeat([1, 0, 0, 1], CHUNK), np.full(CHUNK, NEG)]).astype(np.float32)
    return {
        "x_prompt": i["x_prompt"][0], "x_sample": i["x_sample"][0], "w_in": w_in,
        "gains": np.concatenate([cols(g) for g in gains], 1),
        "b_gates": i["b_gates"].reshape(2, A_HEADS).T,
        "s_C0": i["state_mlstm_C"][0, 0], "s_n0": i["state_mlstm_n"].reshape(A_HEADS, A_DIM, 1),
        "s_m0": i["state_mlstm_m"].reshape(1, A_HEADS),
        "c_ckv": i["cache_mla_ckv"][0, 0], "c_krope": i["cache_mla_krope"][0, 0],
        "w_qn": uq[:, :, :B_NOPE].reshape(Q_RANK, -1), "w_qr": rot.reshape(Q_RANK, -1),
        "w_qs": np.concatenate([rot[:, :, 16:], rot[:, :, :16]], 2).reshape(Q_RANK, -1),
        "w_uk": i["mla_w_uk"][0].reshape(KV_RANK, -1), "w_uv": i["mla_w_uv"][0].reshape(KV_RANK, -1),
        "w_out0": i["w_out_ab"][0], "w_qkv": i["w_qkv_c"][0], "w_out1": i["w_out_c"][0],
        "c_k": i["cache_band_k"].reshape(PAST_LEN, -1), "c_v": i["cache_band_v"].reshape(PAST_LEN, -1),
        "rel": np.concatenate([np.repeat(rel[:, 2 * MAX_REL:], P - 1, 1), rel[:, :0:-1]], 1),
        "w_gate": i["w_gate"], "w_up": i["w_up"], "w_down": i["w_down"],
        "rope_k": table, "rope_q": np.concatenate([table, table]) * np.float32(MLA_SCALE), "halves": halves[None],
        "ident": np.eye(P, dtype=np.float32), "ones": np.ones((P, P), np.float32),
        "upper": np.triu(np.ones((P, P), np.float32)), "lower": np.tril(np.full((P, P), NEG, np.float32), -1),
    }


def kernel(**inputs):
    import concourse.bacc as _bacc
    from concourse.bass_utils import run_bass_kernel_spmd as _run

    nc = _bacc.Bacc("TRN2", target_bir_lowering=False, num_devices=1)
    arrays = {"in_" + n: np.ascontiguousarray(v) for n, v in _layout(inputs).items()}
    D = {n[3:]: nc.dram_tensor(n, a.shape, F32, kind="ExternalInput").ap() for n, a in arrays.items()}
    for n, shape, _ in _OUTS:
        D[n] = nc.dram_tensor("out_" + n, shape, F32, kind="ExternalOutput").ap()
    for n, shape in _SCRATCH:
        D[n] = nc.dram_tensor("park_" + n, shape, F32, kind="Internal").ap()
    build(nc, D)
    r = _run(nc, [arrays], core_ids=[0])
    return tuple(r.results[0]["out_" + n].reshape(shape) for n, _, shape in _OUTS)
```

```python
from contextlib import ExitStack

import numpy as np

import concourse.bass as bass
from concourse import mybir

ALU = mybir.AluOpType
ACT = mybir.ActivationFunctionType
AX_X = mybir.AxisListType.X
F32 = mybir.dt.float32
F32R = mybir.dt.float32r

D_MODEL, SEQ, DEC_SEQ, PAST_LEN = 1024, 1024, 64, 512
A_HEADS, A_DIM = 4, 128
B_HEADS, B_NOPE, B_ROPE, B_VDIM = 8, 64, 32, 64
Q_RANK, KV_RANK = 384, 256
CHUNK = 64
C_HEADS, C_DIM, MAX_REL = 16, 64, 128
D_FF = ((8 * D_MODEL + 767) // 768) * 256
MLA_SCALE = (B_NOPE + B_ROPE) ** -0.5
C_SCALE = C_DIM ** -0.5
EPS = 1e-6
NEG = -1e30

P = 128
KT = D_MODEL // P
T = SEQ + DEC_SEQ
NT = (T + P - 1) // P
CHUNKS = [(0, 384), (384, 384), (768, T - 768)]
NC = len(CHUNKS)
UNIT = 2 * P
KEYS = T + PAST_LEN

Z_Q, Z_K, Z_V, Z_O = 0, 512, 1024, 1536
Z_CQ, Z_CKV, Z_MISC = 2048, 2432, 2688
Z_KR, Z_KRS, Z_I, Z_F = Z_MISC, Z_MISC + 32, Z_MISC + 64, Z_MISC + 96
Z_ROWS = Z_MISC + P
G_MIX0, G_FFN0, G_MIX1, G_FFN1, G_Q, G_KV, G_H = 0, 8, 16, 24, 32, 35, 37
G_COLS = 41


def tile_width(t):
    return min(P, T - t * P)


class Stage:

    def __init__(self, nc, name):
        self.nc, self.name, self.ctx, self.sems = nc, name, ExitStack(), []

    def __enter__(self):
        self.ctx.__enter__()
        return self

    def __exit__(self, *a):
        self.ctx.__exit__(*a)
        if self.sems and a[0] is None:
            self.nc.clear_and_free_semaphores(self.sems)
            self.nc.all_engine_barrier()

    def sb(self, name, shape, dt=F32):
        return self.ctx.enter_context(self.nc.sbuf_tensor(f"{self.name}_{name}", shape, dt))

    def ps(self, name, shape, dt=F32):
        return self.ctx.enter_context(self.nc.psum_tensor(f"{self.name}_{name}", shape, dt))

    def sem(self, name):
        self.sems.append(self.nc.alloc_semaphore(name=f"{self.name}_{name}"))
        return self.sems[-1]

    def block(self):
        return self.ctx.enter_context(self.nc.Block())


def load_stage(nc, S, D):
    with Stage(nc, "load") as st:
        xin = st.sb("xin", [P, 3, D_MODEL])
        banks = st.ps("banks", [P, 8, 512])
        ident_in, const_in = st.sem("ident_in"), st.sem("const_in")
        row_in = [st.sem(f"row_in{i}") for i in range(3)]
        turned, act_out, dve_out = st.sem("turned"), st.sem("act_out"), st.sem("dve_out")
        block = st.block()

        @block.sync
        def _(sp):
            sp.dma_start(S["ident"][:], D["ident"]).then_inc(ident_in, 16)
            sp.dma_start(S["ones"][:], D["ones"]).then_inc(const_in, 16)
            sp.dma_start(S["gains"][:], D["gains"]).then_inc(const_in, 16)
            sp.dma_start(S["halves"][:], D["halves"]).then_inc(const_in, 16)
            for t in range(NT):
                w = tile_width(t)
                if t >= 3:
                    sp.wait_ge(turned, 2 * (t - 2))
                src = D["x_prompt"][t * P:t * P + w, :] if t < SEQ // P else D["x_sample"]
                sp.dma_start(xin[0:w, t % 3, :], src).then_inc(row_in[t % 3], 16)
            rel = D["rel"]
            width = rel.shape[1]
            rows = bass.AP(rel.tensor, P - 1, [[width, C_HEADS], [-1, P], [1, 2 * P]])
            sp.dma_start(D["bias"], rows).then_inc(const_in, 16)
            sp.wait_ge(const_in, 64)

        @block.tensor
        def _(pe):
            pe.wait_ge(ident_in, 16)
            for t in range(NT):
                w = tile_width(t)
                pe.wait_ge(row_in[t % 3], 16 * (t // 3 + 1))
                for j in range(2):
                    if t >= 4:
                        pe.wait_ge(dve_out if j else act_out, t - 3)
                    for q in range(4):
                        k = 4 * j + q
                        last = nc.tensor.transpose(banks[:, (2 * t + j) % 8, q * P:q * P + w],
                                                   xin[0:w, t % 3, k * P:(k + 1) * P], S["ident"][0:w, 0:w])
                    last.then_inc(turned, 1)

        def empty(t, j):
            w = tile_width(t)
            src = banks[:, (2 * t + j) % 8, :].rearrange("p (q n) -> p q n", q=4)[:, :, 0:w]
            return S["xT"][:, 4 * j:4 * j + 4, t * P:t * P + w], src

        @block.scalar
        def _(act):
            for t in range(NT):
                act.wait_ge(turned, 2 * t + 1)
                nc.scalar.activation(*empty(t, 0), ACT.Copy).then_inc(act_out, 1)

        @block.vector
        def _(dve):
            for t in range(NT):
                dve.wait_ge(turned, 2 * t + 2)
                nc.vector.tensor_copy(*empty(t, 1)).then_inc(dve_out, 1)


class Norm:

    HALF = KT // 2

    def __init__(self, nc, S, st, g0, sq, hf, var, means, roots):
        self.nc, self.S, self.g0 = nc, S, g0
        self.sq, self.hf, self.var, self.means, self.roots = sq, hf, var, means, roots
        self.squared, self.summed, self.eps_added, self.recip, self.rooted, self.scaled, self.hi_done, self.lo_done = (
            st.sem("n_" + n) for n in ("squared", "summed", "eps_added", "recip", "rooted", "scaled", "hi", "lo"))

    def square(self, act, c):
        c0, w = CHUNKS[c]
        for j in range(2):
            n = 2 * c + j
            if n >= 2:
                act.wait_ge(self.summed, n - 1)
            src = self.S["xT"][:, j * self.HALF:(j + 1) * self.HALF, c0:c0 + w]
            self.nc.scalar.activation(self.sq[j][:, :, 0:w], src, ACT.Square).then_inc(self.squared, 1)

    def root(self, act, c):
        w = CHUNKS[c][1]
        act.wait_ge(self.recip, c + 1)
        n = len(self.roots)
        if c >= n:
            act.wait_ge(self.scaled, KT * (c - n + 1))
        self.nc.scalar.activation(self.roots[c % n][:, 0:w], self.var[:, 0:w], ACT.Sqrt).then_inc(self.rooted, 1)

    def high(self, act, c):
        c0, w = CHUNKS[c]
        for k in range(KT):
            act.wait_ge(self.scaled, c * KT + k + 1)
            self.nc.scalar.activation(self.S["hhi"][:, k, c0:c0 + w], self.hf[k % 4][:, 0:w], ACT.Copy)\
                .then_inc(self.hi_done, 1)

    def total(self, pe, c):
        w = CHUNKS[c][1]
        n = len(self.means)
        if c >= n:
            pe.wait_ge(self.eps_added, c - n + 1)
        for k in range(KT):
            if k % self.HALF == 0:
                pe.wait_ge(self.squared, 2 * c + k // self.HALF + 1)
            last = self.nc.tensor.matmul(self.means[c % len(self.means)][:, 0:w], self.S["ones"][:],
                                         self.sq[k // self.HALF][:, k % self.HALF, 0:w], start=(k == 0), stop=(k == KT - 1))
            if k % self.HALF == self.HALF - 1:
                last.then_inc(self.summed, 1)

    def reciprocal(self, dve, c):
        w = CHUNKS[c][1]
        dve.wait_ge(self.summed, 2 * c + 2)
        if c:
            dve.wait_ge(self.rooted, c)
        self.nc.vector.tensor_scalar(self.var[:, 0:w], self.means[c % len(self.means)][:, 0:w], 1.0 / D_MODEL, EPS, ALU.mult,
                                     ALU.add).then_inc(self.eps_added, 1)
        dve.wait_ge(self.eps_added, c + 1)
        self.nc.vector.reciprocal(self.var[:, 0:w], self.var[:, 0:w]).then_inc(self.recip, 1)

    def scale(self, dve, c):
        c0, w = CHUNKS[c]
        dve.wait_ge(self.rooted, c + 1)
        for k in range(KT):
            n = c * KT + k
            if n >= 4:
                dve.wait_ge(self.lo_done, n - 3)
            self.nc.vector.scalar_tensor_tensor(
                out=self.hf[k % 4][:, 0:w], in0=self.S["xT"][:, k, c0:c0 + w],
                scalar=self.S["gains"][:, self.g0 + k:self.g0 + k + 1], in1=self.roots[c % len(self.roots)][:, 0:w],
                op0=ALU.mult, op1=ALU.mult).then_inc(self.scaled, 1)

    def low(self, pool, c):
        c0, w = CHUNKS[c]
        for k in range(KT):
            pool.wait_ge(self.hi_done, c * KT + k + 1)
            self.nc.gpsimd.tensor_tensor(self.S["hlo"][:, k, c0:c0 + w], self.hf[k % 4][:, 0:w],
                                         self.S["hhi"][:, k, c0:c0 + w], ALU.subtract).then_inc(self.lo_done, 1)

    def on_vector(self, dve):
        for c in range(NC):
            self.reciprocal(dve, c)
            if c:
                self.scale(dve, c - 1)
        self.scale(dve, NC - 1)

    def ready(self, pe, c):
        pe.wait_ge(self.lo_done, (c + 1) * KT)


def three_pass(nc, out, whi, wlo, hhi, hlo, kts, c0, w):
    for k in range(kts):
        nc.tensor.matmul(out, whi[:, k, :], hhi[:, k, c0:c0 + w], start=(k == 0), stop=False)
        nc.tensor.matmul(out, whi[:, k, :], hlo[:, k, c0:c0 + w], start=False, stop=False)
        last = nc.tensor.matmul(out, wlo[:, k, :], hhi[:, k, c0:c0 + w], start=False, stop=(k == kts - 1))
    return last


def project_stage(nc, S, name, weights, units, out_rows=None, g0=None):
    xT, hhi, hlo = S["xT"], S["hhi"], S["hlo"]
    w_view = weights.rearrange("(k p) n -> p k n", p=P)
    with Stage(nc, name) as st:
        stage = st.sb("stage", [P, KT, UNIT])
        whi = st.sb("whi", [P, 2, KT, P], F32R)
        wlo = st.sb("wlo", [P, 2, KT, P], F32R)
        rows = st.sb("rows", [P, 2, T]) if out_rows is not None else None
        banks = st.ps("banks", [P, 2 * NC, 512])
        w_in, hi_done, lo_done = st.sem("w_in"), st.sem("hi_done"), st.sem("lo_done")
        summed = st.sem("summed")
        emptied = st.sem("emptied")
        stored = [st.sem(f"stored{h}") for h in range(2)]
        if g0 is None:
            norm = None
        else:
            W = CHUNKS[0][1]
            norm = Norm(nc, S, st, g0, [st.sb(f"sq{j}", [P, KT // 2, W]) for j in range(2)],
                        [st.sb(f"hf{j}", [P, W]) for j in range(4)], st.sb("var", [P, W]),
                        [st.ps("means", [P, 512])], [st.ps("roots", [P, 512])])
        block = st.block()

        @block.sync
        def _(sp):
            def load(u):
                sp.dma_start(stage[:], w_view[:, :, bass.ds(u * UNIT, UNIT)]).then_inc(w_in, 16)

            def store(u):
                for h in range(2):
                    sp.wait_ge(emptied, u * 2 * NC + (h + 1) * NC + 2 * NC)
                    sp.dma_start(out_rows[bass.ds(u * UNIT + h * P, P), :], rows[:, h, :]).then_inc(stored[h], 16)

            load(0)
            if out_rows is not None:
                for h in range(2):
                    sp.sem_inc(stored[h], 16)
            with sp.Fori(0, units - 1) as u:
                sp.wait_ge(lo_done, 2 * u + 2)
                load(u + 1)
                if out_rows is not None:
                    store(u)
            if out_rows is not None:
                store(units - 1)
                for h in range(2):
                    sp.wait_ge(stored[h], 16 * (units + 1))

        @block.scalar
        def _(act):
            def split(u):
                act.wait_ge(w_in, 16 * u + 16)
                for h in range(2):
                    act.wait_ge(summed, 2 * NC * u + (h + 1) * NC)
                    nc.scalar.activation(whi[:, h], stage[:, :, h * P:(h + 1) * P], ACT.Copy).then_inc(hi_done, 1)

            if norm:
                norm.square(act, 0)
                norm.square(act, 1)
                norm.root(act, 0)
                norm.square(act, 2)
            split(0)
            if norm:
                norm.high(act, 0)
                norm.root(act, 1)
                norm.high(act, 1)
                norm.root(act, 2)
                norm.high(act, 2)
            with act.Fori(1, units) as u:
                split(u)

        @block.gpsimd
        def _(pool):
            def split(u):
                for h in range(2):
                    pool.wait_ge(hi_done, 2 * u + h + 1)
                    nc.gpsimd.tensor_tensor(wlo[:, h], stage[:, :, h * P:(h + 1) * P], whi[:, h],
                                            ALU.subtract).then_inc(lo_done, 1)

            split(0)
            if norm:
                for c in range(NC):
                    norm.low(pool, c)
            with pool.Fori(1, units) as u:
                split(u)

        @block.tensor
        def _(pe):
            pe.sem_inc(summed, 2 * NC)

            def products(u, first=False):
                for h in range(2):
                    pe.wait_ge(lo_done, 2 * u + h + 1)
                    for c, (c0, w) in enumerate(CHUNKS):
                        b = h * NC + c
                        if first and h == 0:
                            norm.ready(pe, c)
                        pe.wait_ge(emptied, 2 * NC * u + b + 1)
                        last = three_pass(nc, banks[:, b, 0:w], whi[:, h], wlo[:, h], hhi, hlo, KT, c0, w)
                        last.then_inc(summed, 1)

            if norm:
                for c in range(NC):
                    norm.total(pe, c)
                products(0, first=True)
            with pe.Fori(1 if norm else 0, units) as u:
                products(u)

        @block.vector
        def _(dve):
            dve.sem_inc(emptied, 2 * NC)
            if norm:
                norm.on_vector(dve)
            with dve.Fori(0, units) as u:
                for h in range(2):
                    if out_rows is not None:
                        dve.wait_ge(stored[h], 16 * u + 16)
                    for c, (c0, w) in enumerate(CHUNKS):
                        b = h * NC + c
                        dve.wait_ge(summed, 2 * NC * u + b + 1 + 2 * NC)
                        if out_rows is not None:
                            nc.vector.tensor_copy(rows[:, h, c0:c0 + w], banks[:, b, 0:w]).then_inc(emptied, 1)
                        else:
                            x = xT[:, bass.ds(2 * u + h, 1), c0:c0 + w].rearrange("p a n -> p (a n)")
                            nc.vector.tensor_tensor(x, x, banks[:, b, 0:w], ALU.add).then_inc(emptied, 1)




R = A_HEADS * NT


def gate_stage(nc, S, D):
    PROMPT = SEQ // P
    with Stage(nc, "gate") as st:
        gi = st.sb("gi", [A_HEADS, NT * P])
        gf = st.sb("gf", [A_HEADS, NT * P])
        e1 = st.sb("e1", [A_HEADS, T])
        bias = st.sb("bias", [A_HEADS, 2])
        ig = st.sb("ig", [R, P])
        lf = st.sb("lf", [R, P])
        lfT = st.sb("lfT", [P, R])
        b = st.sb("b", [R, P])
        a = st.sb("a", [R, P])
        amax = st.sb("amax", [R, P])
        rows = st.sb("rows", [1, 4, A_HEADS, NT])
        logs = st.sb("logs", [1, 2, R])
        m_in = st.sb("m_in", [R, 1])
        u = st.sb("u", [R, P])
        w = st.sb("w", [R, P])
        nm = st.sb("nm", [R, P])
        wk = st.sb("wk", [P, R])
        m0 = st.sb("m0", [1, A_HEADS])
        m_out = st.sb("m_out", [1, 2, A_HEADS])
        ps = st.ps("ps", [P, 8, 512])
        z_in, dve, act, pe = st.sem("z_in"), st.sem("dve"), st.sem("act"), st.sem("pe")
        parked, back, out = st.sem("parked"), st.sem("back"), st.sem("out")
        block = st.block()
        r_b, r_a, r_min, r_mout = (rows[:, i] for i in range(4))
        flat = lambda x: x.rearrange("p h c -> p (h c)")

        done = {}

        @block.vector
        def _(eng):
            n = [0]

            def step(ins):
                ins.then_inc(dve, 1)
                n[0] += 1
                eng.wait_ge(dve, n[0])

            v = nc.vector
            step(v.memset(gi[:, T:], NEG))
            step(v.memset(gf[:, T:], 0.0))
            step(v.memset(r_min[:, :, 0], 0.0))
            eng.wait_ge(z_in, 96)
            step(v.tensor_scalar(gi[:, 0:T], gi[:, 0:T], bias[:, 0:1], None, ALU.add))
            step(v.tensor_scalar(gf[:, 0:T], gf[:, 0:T], bias[:, 1:2], None, ALU.add))
            step(v.scalar_tensor_tensor(out=e1[:], in0=gf[:, 0:T], scalar=-1.0, in1=gf[:, 0:T], op0=ALU.mult,
                                        op1=ALU.min))
            step(v.tensor_scalar(gf[:, 0:T], gf[:, 0:T], 0.0, None, ALU.min))
            eng.wait_ge(act, 2)
            step(v.tensor_tensor(gf[:, 0:T], gf[:, 0:T], e1[:], ALU.subtract))
            eng.wait_ge(pe, 1)
            step(v.tensor_copy(lfT[:], ps[:, 0, 0:R]))
            eng.wait_ge(pe, 2)
            step(v.tensor_copy(b[:], ps[0:R, 1, 0:P]))
            eng.wait_ge(back, 32)
            step(v.tensor_tensor(a[:], ig[:], b[:], ALU.subtract))
            eng.wait_ge(pe, 3)
            step(v.tensor_copy(S["aT"][:], ps[:, 2, 0:R]))
            step(v.tensor_tensor_scan(amax[:], a[:], a[:], NEG, ALU.max, ALU.max))
            eng.wait_ge(pe, 4)
            step(v.tensor_copy(rows[:, 0:2].rearrange("p i h c -> p (i h c)"), ps[0:1, 3, 0:2 * R]))
            step(v.tensor_copy(r_min[:, :, NT - 1], m0[:]))
            for c in list(range(PROMPT)) + [NT - 1]:
                step(v.tensor_tensor(r_mout[:, :, c], r_min[:, :, c], r_a[:, :, c], ALU.max))
                step(v.tensor_tensor(r_mout[:, :, c], r_mout[:, :, c], r_b[:, :, c], ALU.add))
                if c + 1 < PROMPT:
                    step(v.tensor_copy(r_min[:, :, c + 1], r_mout[:, :, c]))
            step(v.tensor_copy(m_out[:, 0, :], r_mout[:, :, PROMPT - 1]))
            step(v.tensor_copy(m_out[:, 1, :], r_mout[:, :, NT - 1]))
            done["m"] = n[0]
            step(v.tensor_tensor(logs[:, 1, :], flat(r_b), flat(r_mout), ALU.subtract))
            step(v.tensor_tensor(logs[:, 0, :], logs[:, 1, :], flat(r_min), ALU.add))
            done["logs"] = n[0]
            eng.wait_ge(pe, 5)
            step(v.tensor_copy(m_in[:], ps[0:R, 4, 0:1]))
            step(v.tensor_scalar(u[:], amax[:], m_in[:], -1.0, ALU.max, ALU.mult))
            done["u"] = n[0]
            step(v.tensor_tensor(nm[:], u[:], b[:], ALU.subtract))
            done["nm"] = n[0]
            eng.wait_ge(pe, 7)
            step(v.tensor_tensor(wk[:], S["aT"][:], ps[:, 7, 0:R], ALU.add))
            done["wk"] = n[0]

        @block.sync
        def _(sp):
            sp.dma_start(gi[:, 0:T], D["z"][Z_I:Z_I + A_HEADS, :]).then_inc(z_in, 16)
            sp.dma_start(gf[:, 0:T], D["z"][Z_F:Z_F + A_HEADS, :]).then_inc(z_in, 16)
            sp.dma_start(bias[:], D["b_gates"]).then_inc(z_in, 16)
            sp.dma_start(S["upper"][:], D["upper"]).then_inc(z_in, 16)
            sp.dma_start(S["lower"][:], D["lower"]).then_inc(z_in, 16)
            sp.dma_start(m0[:], D["s_m0"]).then_inc(z_in, 16)
            sp.wait_ge(dve, 8)
            sp.dma_start(D["gates"][0], gi[:]).then_inc(parked, 16)
            sp.dma_start(D["gates"][1], gf[:]).then_inc(parked, 16)
            sp.wait_ge(parked, 32)
            sp.dma_start(ig[:], D["gates"][0].rearrange("h (c t) -> (h c) t", t=P)).then_inc(back, 16)
            sp.dma_start(lf[:], D["gates"][1].rearrange("h (c t) -> (h c) t", t=P)).then_inc(back, 16)
            sp.wait_ge(dve, done["m"])
            sp.dma_start(D["p_m"], m_out[:, 0, :]).then_inc(out, 16)
            sp.dma_start(D["s_m"], m_out[:, 1, :]).then_inc(out, 16)
            sp.wait_ge(dve, done["u"])
            sp.dma_start(D["u"].rearrange("h (c t) -> (h c) t", t=P), u[:]).then_inc(out, 16)
            sp.wait_ge(act, 4)
            sp.dma_start(D["w"].rearrange("h (c t) -> (h c) t", t=P), w[:]).then_inc(out, 16)
            sp.wait_ge(out, 64)

        @block.scalar
        def _(eng):
            eng.wait_ge(dve, 6)
            nc.scalar.activation(e1[:], e1[:], ACT.Exp).then_inc(act, 1)
            eng.wait_ge(act, 1)
            nc.scalar.activation(e1[:], e1[:], ACT.Ln, bias=1.0).then_inc(act, 1)
            eng.wait_ge(pe, 6)
            nc.scalar.activation(S["decay"][:], ps[:, 6, 0:R], ACT.Exp).then_inc(act, 1)
            eng.wait_ge(dve, done["u"])
            nc.scalar.activation(w[:], u[:], ACT.Exp, bias=m_in[:]).then_inc(act, 1)
            eng.wait_ge(dve, done["wk"])
            nc.scalar.activation(S["wk"][:], wk[:], ACT.Exp).then_inc(act, 1)
            eng.wait_ge(pe, 8)
            nc.scalar.activation(S["enm"][:], ps[:, 0, 0:R], ACT.Exp).then_inc(act, 1)

        @block.tensor
        def _(eng):
            eng.wait_ge(back, 32)
            nc.tensor.transpose(ps[:, 0, 0:R], lf[:], S["ident"][0:R, 0:R]).then_inc(pe, 1)
            eng.wait_ge(dve, 9)
            nc.tensor.matmul(ps[0:R, 1, 0:P], lfT[:], S["upper"][:], start=True, stop=True).then_inc(pe, 1)
            eng.wait_ge(dve, 11)
            nc.tensor.transpose(ps[:, 2, 0:R], a[:], S["ident"][0:R, 0:R]).then_inc(pe, 1)
            eng.wait_ge(dve, 13)
            nc.tensor.transpose(ps[0:1, 3, 0:R], b[:, P - 1:P], S["ident"][0:R, 0:R])
            nc.tensor.transpose(ps[0:1, 3, R:2 * R], amax[:, P - 1:P], S["ident"][0:R, 0:R]).then_inc(pe, 1)
            eng.wait_ge(dve, done["m"])
            nc.tensor.matmul(ps[0:R, 4, 0:1], flat(r_min), S["ones"][0:1, 0:1], start=True, stop=True).then_inc(pe, 1)
            eng.wait_ge(dve, done["logs"])
            nc.tensor.matmul(ps[:, 6, 0:R], S["ones"][0:1, :], logs[:, 0, :], start=True, stop=True).then_inc(pe, 1)
            nc.tensor.matmul(ps[:, 7, 0:R], S["ones"][0:1, :], logs[:, 1, :], start=True, stop=True).then_inc(pe, 1)
            eng.wait_ge(dve, done["nm"])
            nc.tensor.transpose(ps[:, 0, 0:R], nm[:], S["ident"][0:R, 0:R]).then_inc(pe, 1)


def mlstm_stage(nc, S, D):
    PROMPT = SEQ // P
    N = 2 * NT
    E1 = A_DIM + 1
    hhi, hlo = S["hhi"], S["hlo"]
    with Stage(nc, "mlstm") as st:
        qT, kT, vT, oT = (st.sb(x, [P, 2, T]) for x in ("qT", "kT", "vT", "oT"))
        dm = st.sb("dm", [P, 2, NT, P])
        qw = st.sb("qw", [P, 2, NT * P])
        cols = st.sb("cols", [P, 4, N])
        kw = st.sb("kw", [P, N, A_DIM])
        v1 = st.sb("v1", [P, 2, NT, E1])
        state = st.sb("state", [P, 2, 2, E1])
        sd = st.sb("sd", [P, 2, P])
        h = st.sb("h", [P, N, A_DIM])
        den = st.sb("den", [P, N])
        ssq = st.sb("ssq", [P, N])
        junk = st.sb("junk", [P, 2, A_DIM])
        gated = st.sb("gated", [P, 4, P])
        pS = st.ps("pS", [P, 2, 512])
        pU = st.ps("pU", [P, 2, 512])
        pT = st.ps("pT", [P, 4, 512])
        pN = pT[:, 2:4, :]
        names = ("kv_in", "zin", "uin", "set_up", "dadd", "dexp", "turned", "kw_set", "v_set", "sm", "sdm", "nm", "um",
                 "upd", "dn", "rd", "hs", "sq", "mv", "rt", "hn", "ht", "gt", "hi", "lo", "stored", "ones", "sg", "apart", "cleared")
        s = {x: st.sem(x) for x in names}
        block = st.block()
        TR = 2 * N

        @block.sync
        def _(sp):
            for hp in range(2):
                if hp:
                    sp.wait_ge(s["sdm"], N * hp)
                for e in range(2):
                    src = D["u"][2 * hp + e:2 * hp + e + 1, :].to_broadcast([P, NT * P])
                    sp.dma_start(dm[:, e].rearrange("p c t -> p (c t)"), src).then_inc(s["uin"], 16)
                if hp:
                    sp.wait_ge(s["nm"], N * hp)
                for e in range(2):
                    for dst, row in ((kT, Z_K), (vT, Z_V)):
                        row += (2 * hp + e) * P
                        sp.dma_start(dst[:, e, :], D["z"][row:row + P, :]).then_inc(s["kv_in"], 16)
                for e in range(2):
                    src = D["w"][2 * hp + e:2 * hp + e + 1, :].to_broadcast([P, NT * P])
                    sp.dma_start(qw[:, e], src).then_inc(s["zin"], 16)
                    row = Z_Q + (2 * hp + e) * P
                    sp.dma_start(qT[:, e, :], D["z"][row:row + P, :]).then_inc(s["zin"], 16)
                if hp:
                    sp.wait_ge(s["stored"], 128 * hp)
                for e in range(2):
                    sp.dma_start(state[:, e, 1, 0:A_DIM], D["s_C0"][2 * hp + e]).then_inc(s["zin"], 16)
                    sp.dma_start(state[:, e, 1, A_DIM:E1], D["s_n0"][2 * hp + e]).then_inc(s["zin"], 16)
                if hp:
                    sp.wait_ge(s["gt"], N * hp)
                for e in range(2):
                    row = Z_O + (2 * hp + e) * P
                    sp.dma_start(oT[:, e, :], D["z"][row:row + P, :]).then_inc(s["zin"], 16)
                for g, (c_out, n_out) in enumerate((("p_C", "p_n"), ("s_C", "s_n"))):
                    for e in range(2):
                        sp.wait_ge(s["upd"], N * hp + 2 * (PROMPT - 1 + g) + e + 1)
                        sp.dma_start(D[c_out][2 * hp + e], state[:, e, g, 0:A_DIM]).then_inc(s["stored"], 16)
                        sp.dma_start(D[n_out][2 * hp + e], state[:, e, g, A_DIM:E1]).then_inc(s["stored"], 16)
            sp.wait_ge(s["stored"], 128 * 2)

        @block.gpsimd
        def _(pool):
            nc.gpsimd.memset(v1[:], 1.0).then_inc(s["ones"], 1)
            pool.sem_inc(s["lo"], 4)
            with pool.Fori(0, 2) as hp:
                for n in range(N):
                    c, e = n // 2, n % 2
                    w = tile_width(c)
                    pool.wait_ge(s["hi"], N * hp + n + 1)
                    dst = slice(c * P, c * P + w)
                    ht = bass.ds(2 * hp + e, 1)
                    nc.gpsimd.tensor_tensor(hlo[:, ht, dst].rearrange("p a n -> p (a n)"), gated[:, n % 4, 0:w],
                                            hhi[:, ht, dst].rearrange("p a n -> p (a n)"), ALU.subtract)\
                      .then_inc(s["lo"], 1)

        @block.scalar
        def _(act):
            with act.Fori(0, 2) as hp:
                for e in range(2):
                    act.wait_ge(s["dadd"], 4 * hp + 2 * e + 2)
                    nc.scalar.activation(dm[:, e], dm[:, e], ACT.Exp).then_inc(s["dexp"], 1)
                for n in range(N):
                    c, e = n // 2, n % 2
                    w = tile_width(c)
                    act.wait_ge(s["turned"], TR * hp + 2 * n + 2)
                    nc.scalar.activation(v1[0:w, e, c, 0:A_DIM], pT[0:w, (2 * n + 1) % 4, 0:P], ACT.Copy).then_inc(s["v_set"], 1)
                act.wait_ge(s["zin"], 160 * hp + 160)
                nc.scalar.activation(oT[:], oT[:], ACT.Sigmoid).then_inc(s["sg"], 1)
                for n in range(N):
                    w = tile_width(n // 2)
                    act.wait_ge(s["hs"], N * hp + n + 1)
                    if n >= 2:
                        act.wait_ge(s["sq"], N * hp + n - 1)
                    nc.scalar.activation(junk[0:w, n % 2], h[0:w, n, :], ACT.Square, accum_out=ssq[0:w, n:n + 1])\
                      .then_inc(s["sq"], 1)
                act.wait_ge(s["mv"], 2 * hp + 2)
                nc.scalar.activation(ssq[:], ssq[:], ACT.Sqrt).then_inc(s["rt"], 1)
                for n in range(N):
                    c, e = n // 2, n % 2
                    w = tile_width(c)
                    act.wait_ge(s["gt"], N * hp + n + 1)
                    dst = hhi[:, bass.ds(2 * hp + e, 1), c * P:c * P + w].rearrange("p a n -> p (a n)")
                    nc.scalar.activation(dst, gated[:, n % 4, 0:w], ACT.Copy).then_inc(s["hi"], 1)

        @block.tensor
        def _(pe):
            with pe.Fori(0, 2) as hp:
                pe.wait_ge(s["kv_in"], 64 * hp + 64)
                for n in range(N):
                    c, e = n // 2, n % 2
                    w = tile_width(c)
                    for j, src in enumerate((kT, vT)):
                        m = 2 * n + j
                        if n >= 2:
                            pe.wait_ge(s[("kw_set", "v_set")[j]], N * hp + n - 1)
                        if w < P:
                            pe.sem_inc(s["apart"], 1)
                        nc.tensor.transpose(pT[0:w, m % 4, 0:P], src[:, e, c * P:c * P + w], S["ident"][:])\
                          .then_inc(s["turned"], 1)

                def scores(n):
                    c, e = n // 2, n % 2
                    w = tile_width(c)
                    if n >= 2:
                        pe.wait_ge(s["sdm"], N * hp + n - 1)
                    nc.tensor.matmul(pS[0:w, n % 2, 0:w], kT[:, e, c * P:c * P + w], qT[:, e, c * P:c * P + w],
                                     start=True, stop=True).then_inc(s["sm"], 1)

                pe.wait_ge(s["zin"], 160 * hp + 160)
                scores(0)
                pe.wait_ge(s["kw_set"], N * hp + N)
                pe.wait_ge(s["v_set"], N * hp + N)
                pe.wait_ge(s["set_up"], 2 * hp + 2)
                for n in range(N):
                    c, e = n // 2, n % 2
                    w = tile_width(c)
                    g = int(c == NT - 1)
                    if n + 1 < N:
                        scores(n + 1)
                    if n >= 2:
                        pe.wait_ge(s["upd"], N * hp + n - 1)
                    nc.tensor.matmul(pU[:, n % 2, 0:E1], kw[0:w, n, :], v1[0:w, e, c, :], start=True, stop=True)\
                      .then_inc(s["um"], 1)
                    pe.wait_ge(s["sdm"], N * hp + n + 1)
                    if n >= 2:
                        pe.wait_ge(s["hs"], N * hp + n - 1)
                    nc.tensor.matmul(pN[0:w, n % 2, 0:E1], qw[:, e, c * P:c * P + w], state[:, e, g, :],
                                     start=True, stop=False)
                    nc.tensor.matmul(pN[0:w, n % 2, 0:E1], sd[0:w, n % 2, 0:w], v1[0:w, e, c, :],
                                     start=False, stop=True).then_inc(s["nm"], 1)
                for n in range(N):
                    c, e = n // 2, n % 2
                    w = tile_width(c)
                    pe.wait_ge(s["hn"], N * hp + n + 1)
                    if n >= 4:
                        pe.wait_ge(s["gt"], N * hp + n - 3)
                    if w < P:
                        pe.sem_inc(s["apart"], 1)
                    nc.tensor.transpose(pT[:, n % 4, 0:w], h[0:w, n, :], S["ident"][0:w, 0:w]).then_inc(s["ht"], 1)
                pe.wait_ge(s["gt"], N * hp + N)

        @block.vector
        def _(dve):
            v = nc.vector
            dve.wait_ge(s["ones"], 1)
            v.memset(ssq[:], 1.0).then_inc(s["cleared"], 1)
            with dve.Fori(0, 2) as hp:
                dve.wait_ge(s["uin"], 32 * hp + 32)
                pair = bass.ds(hp * N, N)
                for i, src in enumerate(("aT", "enm", "wk", "decay")):
                    v.tensor_copy(cols[:, i, :], S[src][:, pair]).then_inc(s["rd"], 1)
                dve.wait_ge(s["rd"], (4 + N) * hp + 4)
                mask = S["lower"][:].rearrange("p (a t) -> p a t", a=1).to_broadcast([P, NT, P])
                for e in range(2):
                    a = cols[:, 0, e * NT:(e + 1) * NT].rearrange("p (c a) -> p c a", a=1).to_broadcast([P, NT, P])
                    v.tensor_tensor(dm[:, e], dm[:, e], a, ALU.add).then_inc(s["dadd"], 1)
                    dve.wait_ge(s["dadd"], 4 * hp + 2 * e + 1)
                    v.tensor_tensor(dm[:, e], dm[:, e], mask, ALU.add).then_inc(s["dadd"], 1)
                for n in range(N):
                    c, e = n // 2, n % 2
                    w = tile_width(c)
                    dve.wait_ge(s["turned"], TR * hp + 2 * n + 1)
                    i = e * NT + c
                    v.tensor_scalar(kw[0:w, n, :], pT[0:w, 2 * n % 4, 0:P], A_DIM ** -0.5, cols[0:w, 2, i:i + 1],
                                    ALU.mult, ALU.mult).then_inc(s["kw_set"], 1)
                dve.wait_ge(s["zin"], 160 * hp + 160)
                v.tensor_tensor(qw[:, :, 0:T], qw[:, :, 0:T], qT[:], ALU.mult).then_inc(s["set_up"], 1)
                v.memset(state[:, :, 0, :], 0.0).then_inc(s["set_up"], 1)
                dve.wait_ge(s["set_up"], 2 * hp + 2)
                dve.wait_ge(s["dexp"], 2 * hp + 2)

                def decayed(n):
                    c, e = n // 2, n % 2
                    w = tile_width(c)
                    dve.wait_ge(s["sm"], N * hp + n + 1)
                    if n >= 2:
                        dve.wait_ge(s["nm"], N * hp + n - 1)
                    v.scalar_tensor_tensor(out=sd[0:w, n % 2, 0:w], in0=pS[0:w, n % 2, 0:w], scalar=A_DIM ** -0.5,
                                           in1=dm[0:w, e, c, 0:w], op0=ALU.mult, op1=ALU.mult).then_inc(s["sdm"], 1)

                decayed(0)
                for n in range(N):
                    c, e = n // 2, n % 2
                    w = tile_width(c)
                    g = int(c == NT - 1)
                    i = e * NT + c
                    if n + 1 < N:
                        decayed(n + 1)
                    dve.wait_ge(s["nm"], N * hp + n + 1)
                    dve.wait_ge(s["um"], N * hp + n + 1)
                    if n >= 2:
                        dve.wait_ge(s["upd"], N * hp + n - 1)
                    v.scalar_tensor_tensor(out=state[:, e, g, :], in0=state[:, e, g, :], scalar=cols[:, 3, i:i + 1],
                                           in1=pU[:, n % 2, 0:E1], op0=ALU.mult, op1=ALU.add).then_inc(s["upd"], 1)
                    v.tensor_scalar(den[0:w, n:n + 1], pN[0:w, n % 2, A_DIM:E1], -1.0, cols[0:w, 1, i:i + 1],
                                    ALU.mult, ALU.max).then_inc(s["dn"], 1)
                    dve.wait_ge(s["dn"], 2 * N * hp + 2 * n + 1)
                    v.tensor_tensor(den[0:w, n:n + 1], pN[0:w, n % 2, A_DIM:E1], den[0:w, n:n + 1], ALU.max)\
                     .then_inc(s["dn"], 1)
                    dve.wait_ge(s["dn"], 2 * N * hp + 2 * n + 2)
                    v.reciprocal(den[0:w, n:n + 1], den[0:w, n:n + 1]).then_inc(s["rd"], 1)
                    dve.wait_ge(s["rd"], (4 + N) * hp + 4 + n + 1)
                    v.tensor_scalar(h[0:w, n, :], pN[0:w, n % 2, 0:A_DIM], den[0:w, n:n + 1], None, ALU.mult)\
                     .then_inc(s["hs"], 1)
                dve.wait_ge(s["sq"], N * hp + N)
                v.tensor_scalar(ssq[:], ssq[:], 1.0 / A_DIM, EPS, ALU.mult, ALU.add).then_inc(s["mv"], 1)
                dve.wait_ge(s["mv"], 2 * hp + 1)
                v.reciprocal(ssq[:], ssq[:]).then_inc(s["mv"], 1)
                dve.wait_ge(s["rt"], hp + 1)
                for n in range(N):
                    w = tile_width(n // 2)
                    v.tensor_scalar(h[0:w, n, :], h[0:w, n, :], ssq[0:w, n:n + 1], None, ALU.mult).then_inc(s["hn"], 1)
                dve.wait_ge(s["sg"], hp + 1)
                for n in range(N):
                    c, e = n // 2, n % 2
                    w = tile_width(c)
                    dve.wait_ge(s["ht"], N * hp + n + 1)
                    if n == 0:
                        dve.wait_ge(s["lo"], N * hp + 4)
                    elif n >= 4:
                        dve.wait_ge(s["lo"], N * hp + n + 1)
                    g = bass.ds(2 * hp + G_H + e, 1)
                    v.scalar_tensor_tensor(out=gated[:, n % 4, 0:w], in0=pT[:, n % 4, 0:w], scalar=S["gains"][:, g],
                                           in1=oT[:, e, c * P:c * P + w], op0=ALU.mult, op1=ALU.mult)\
                     .then_inc(s["gt"], 1)


def ffn_stage(nc, S, name, g0, w_gate, w_up, w_down):
    xT, hhi, hlo = S["xT"], S["hhi"], S["hlo"]
    parts = D_FF // UNIT
    F = UNIT // P
    srcs = [w_gate.rearrange("(k p) n -> p k n", p=P), w_up.rearrange("(k p) n -> p k n", p=P),
            w_down.rearrange("(a f p) n -> a p f n", f=F, p=P)]
    W = CHUNKS[0][1]
    with Stage(nc, name) as st:
        stage = [st.sb(f"stage{m}", [P, KT * UNIT]) for m in range(3)]
        whi = [st.sb(f"whi{m}", [P, KT * UNIT], F32R) for m in range(3)]
        wlo = [st.sb(f"wlo{m}", [P, KT * UNIT], F32R) for m in range(3)]
        ahi = st.sb("ahi", [P, F, T], F32R)
        alo = st.sb("alo", [P, F, T], F32R)
        silu = st.sb("silu", [P, F, W])
        act32 = st.sb("act32", [P, F, W])
        banks = st.ps("banks", [P, 8, 512])
        w_in = [st.sem(f"w_in{m}") for m in range(3)]
        w_hi = [st.sem(f"w_hi{m}") for m in range(3)]
        w_lo = [st.sem(f"w_lo{m}") for m in range(3)]
        gate_sum, up_sum, silu_done, product = (st.sem(n) for n in ("gate_sum", "up_sum", "silu_done", "product"))
        a_hi, a_lo = st.sem("a_hi"), st.sem("a_lo")
        out_sum, added = st.sem("out_sum"), st.sem("added")
        sq = [stage[2][:, 0:KT // 2 * W].rearrange("p (k n) -> p k n", n=W), st.sb("sq", [P, KT // 2, W])]
        norm = Norm(nc, S, st, g0, sq, [x[:, f, :] for x in (silu, act32) for f in range(F)], st.sb("var", [P, W]),
                    [banks[:, 4], banks[:, 5]], [banks[:, 6], banks[:, 7]])
        G = NC * F
        O = NC * KT

        block = st.block()

        def cols(m, tiles):
            return tiles[m][:].rearrange("p (k f n) -> p f k n", k=KT, f=F)

        @block.sync
        def _(sp):
            def load(i, m):
                src = srcs[m][:, :, bass.ds(i * UNIT, UNIT)] if m < 2 else \
                    srcs[m][bass.ds(i, 1), :, :, :].rearrange("a p f n -> p (a f) n")
                dst = stage[m][:].rearrange("p (a n) -> p a n", a=KT if m < 2 else F)
                sp.dma_start(dst, src).then_inc(w_in[m], 16)

            for m in range(3):
                if m == 2:
                    sp.wait_ge(norm.summed, 2 * NC)
                load(0, m)
            with sp.Fori(1, parts) as i:
                for m in range(3):
                    sp.wait_ge(w_lo[m], i)
                    load(i, m)

        @block.scalar
        def _(act):
            def split(i, m):
                act.wait_ge(w_in[m], 16 * i + 16)
                if m < 2:
                    act.wait_ge(up_sum, G * i + G)
                else:
                    act.wait_ge(out_sum, O * i + O)
                nc.scalar.activation(whi[m][:], stage[m][:], ACT.Copy).then_inc(w_hi[m], 1)

            def hidden(i):
                for c, (c0, w) in enumerate(CHUNKS):
                    for f in range(F):
                        n = G * i + c * F + f
                        act.wait_ge(gate_sum, n + 1)
                        act.wait_ge(product, n + 1)
                        nc.scalar.activation(silu[:, f, 0:w], banks[:, 2 * f, 0:w], ACT.Silu).then_inc(silu_done, 1)
                    for f in range(F):
                        n = G * i + c * F + f
                        act.wait_ge(product, n + 1 + F)
                        nc.scalar.activation(ahi[:, f, c0:c0 + w], act32[:, f, 0:w], ACT.Copy).then_inc(a_hi, 1)

            norm.square(act, 0)
            norm.square(act, 1)
            norm.root(act, 0)
            norm.square(act, 2)
            split(0, 0)
            split(0, 1)
            norm.high(act, 0)
            norm.root(act, 1)
            norm.high(act, 1)
            norm.root(act, 2)
            norm.high(act, 2)
            act.wait_ge(norm.lo_done, NC * KT)
            with act.Fori(0, parts - 1) as i:
                split(i, 2)
                hidden(i)
                split(i + 1, 0)
                split(i + 1, 1)
            split(parts - 1, 2)
            hidden(parts - 1)

        @block.gpsimd
        def _(pool):
            pool.sem_inc(a_lo, F)

            def split(i, m):
                pool.wait_ge(w_hi[m], i + 1)
                nc.gpsimd.tensor_tensor(wlo[m][:], stage[m][:], whi[m][:], ALU.subtract).then_inc(w_lo[m], 1)

            def hidden(i):
                for c, (c0, w) in enumerate(CHUNKS):
                    for f in range(F):
                        n = G * i + c * F + f
                        pool.wait_ge(a_hi, n + 1)
                        nc.gpsimd.tensor_tensor(alo[:, f, c0:c0 + w], act32[:, f, 0:w], ahi[:, f, c0:c0 + w],
                                                ALU.subtract).then_inc(a_lo, 1)

            split(0, 0)
            split(0, 1)
            for c in range(NC):
                norm.low(pool, c)
            with pool.Fori(0, parts - 1) as i:
                split(i, 2)
                hidden(i)
                split(i + 1, 0)
                split(i + 1, 1)
            split(parts - 1, 2)
            hidden(parts - 1)

        @block.tensor
        def _(pe):
            pe.sem_inc(up_sum, G)
            pe.sem_inc(out_sum, O)

            def part(i, first=False):
                pe.wait_ge(w_lo[0], i + 1)
                pe.wait_ge(w_lo[1], i + 1)
                for c, (c0, w) in enumerate(CHUNKS):
                    if first:
                        norm.ready(pe, c)
                    for f in range(F):
                        pe.wait_ge(product, G * i + c * F + f + 1)
                        for m, done in ((0, gate_sum), (1, up_sum)):
                            three_pass(nc, banks[:, 2 * f + m, 0:w], cols(m, whi)[:, f], cols(m, wlo)[:, f],
                                       hhi, hlo, KT, c0, w).then_inc(done, 1)
                pe.wait_ge(w_lo[2], i + 1)
                down = [t[2][:].rearrange("p (f k n) -> p k f n", f=F, k=KT) for t in (whi, wlo)]
                for c, (c0, w) in enumerate(CHUNKS):
                    pe.wait_ge(a_lo, G * i + (c + 2) * F)
                    for k in range(KT):
                        pe.wait_ge(added, O * i + c * KT + k + 1)
                        three_pass(nc, banks[:, 4 + k % 4, 0:w], down[0][:, k], down[1][:, k],
                                   ahi, alo, F, c0, w).then_inc(out_sum, 1)

            for c in range(NC):
                norm.total(pe, c)
            part(0, first=True)
            with pe.Fori(1, parts) as i:
                part(i)

        @block.vector
        def _(dve):
            dve.sem_inc(product, F)
            norm.on_vector(dve)
            dve.sem_inc(added, 4)
            dve.wait_ge(norm.lo_done, NC * KT)
            with dve.Fori(0, parts) as i:
                for c, (c0, w) in enumerate(CHUNKS):
                    for f in range(F):
                        n = G * i + c * F + f
                        dve.wait_ge(silu_done, n + 1)
                        dve.wait_ge(up_sum, n + 1 + G)
                        dve.wait_ge(a_lo, n + 1)
                        nc.vector.tensor_tensor(act32[:, f, 0:w], silu[:, f, 0:w], banks[:, 2 * f + 1, 0:w],
                                                ALU.mult).then_inc(product, 1)
                for c, (c0, w) in enumerate(CHUNKS):
                    for k in range(KT):
                        dve.wait_ge(out_sum, O * i + c * KT + k + 1 + O)
                        x = xT[:, k, c0:c0 + w]
                        nc.vector.tensor_tensor(x, x, banks[:, 4 + k % 4, 0:w], ALU.add).then_inc(added, 1)


def final_stage(nc, S, D):
    xT = S["xT"]
    with Stage(nc, "final") as st:
        gain = st.sb("gain", [P, D_MODEL])
        sq = st.sb("sq", [P, 2, D_MODEL])
        var = st.sb("var", [P, NT])
        out = st.sb("out", [P, 3, D_MODEL])
        banks = st.ps("banks", [P, 3, 2, 512])
        gain_in, turned, squared, eps_added, recip, rooted, scaled = (
            st.sem(x) for x in ("gain_in", "turned", "squared", "eps_added", "recip", "rooted", "scaled"))
        stored = [st.sem(f"stored{i}") for i in range(3)]
        block = st.block()

        def rows_of(t):
            return banks[0:tile_width(t), t % 3].rearrange("p b n -> p (b n)")

        @block.tensor
        def _(pe):
            for t in range(NT):
                w = tile_width(t)
                if t >= 3:
                    pe.wait_ge(scaled, t - 2)
                for k in range(KT):
                    last = nc.tensor.transpose(banks[0:w, t % 3, k // 4, k % 4 * P:(k % 4 + 1) * P],
                                               xT[:, k, t * P:t * P + w], S["ident"][:])
                last.then_inc(turned, 1)

        @block.scalar
        def _(act):
            for t in range(NT + 1):
                if t < NT:
                    w = tile_width(t)
                    act.wait_ge(turned, t + 1)
                    if t >= 2:
                        act.wait_ge(squared, t - 1)
                    nc.scalar.activation(sq[0:w, t % 2, :], rows_of(t), ACT.Square, accum_out=var[0:w, t:t + 1])\
                        .then_inc(squared, 1)
                if t:
                    w = tile_width(t - 1)
                    act.wait_ge(recip, t)
                    nc.scalar.activation(var[0:w, t - 1:t], var[0:w, t - 1:t], ACT.Sqrt).then_inc(rooted, 1)

        @block.vector
        def _(dve):
            v = nc.vector
            dve.wait_ge(gain_in, 16)

            def reciprocal(t):
                w = tile_width(t)
                dve.wait_ge(squared, t + 1)
                v.tensor_scalar(var[0:w, t:t + 1], var[0:w, t:t + 1], 1.0 / D_MODEL, EPS, ALU.mult, ALU.add)\
                    .then_inc(eps_added, 1)
                dve.wait_ge(eps_added, t + 1)
                v.reciprocal(var[0:w, t:t + 1], var[0:w, t:t + 1]).then_inc(recip, 1)

            reciprocal(0)
            for t in range(NT):
                w = tile_width(t)
                if t + 1 < NT:
                    reciprocal(t + 1)
                dve.wait_ge(rooted, t + 1)
                if t >= 3:
                    dve.wait_ge(stored[t % 3], 16 * (t // 3))
                v.scalar_tensor_tensor(out=out[0:w, t % 3, :], in0=rows_of(t), scalar=var[0:w, t:t + 1],
                                       in1=gain[0:w, :], op0=ALU.mult, op1=ALU.mult).then_inc(scaled, 1)

        @block.sync
        def _(sp):
            sp.dma_start(gain[:], D["g_final"].to_broadcast([P, D_MODEL])).then_inc(gain_in, 16)
            for t in range(NT):
                w = tile_width(t)
                sp.wait_ge(scaled, t + 1)
                dst = D["y_prompt"][t * P:t * P + w, :] if t < SEQ // P else D["y_sample"]
                sp.dma_start(dst, out[0:w, t % 3, :]).then_inc(stored[t % 3], 16)
            for i in range(3):
                sp.wait_ge(stored[i], 16 * ((NT - i + 2) // 3))


def latent_stage(nc, S, D):
    RQ, RK = Q_RANK // P, KV_RANK // P
    CT = PAST_LEN // P
    cqT, ckvT, kT = S["cqT"], S["ckvT"], S["kT"]
    lo, hi = B_NOPE, B_NOPE + B_ROPE
    with Stage(nc, "latent") as st:
        sq = st.sb("sq", [P, RQ, T])
        var = st.sb("var", [P, 2, T])
        krs = st.sb("krs", [P, T])
        cs = st.sb("cs", [P, 2, T])
        cache = st.sb("cache", [P, CT, KV_RANK])
        rcache = st.sb("rcache", [P, CT, B_ROPE])
        rows = st.sb("rows", [P, NT, KV_RANK])
        rrows = st.sb("rrows", [P, NT, B_ROPE])
        mean = st.ps("mean", [P, 2, NC, 512])
        turn = st.ps("turn", [P, 2, 512])
        z_in, c_in = st.sem("z_in"), st.sem("c_in")
        squared, summed, var_done, rooted, normed = (st.sem(x) for x in ("squared", "summed", "var_done", "rooted", "normed"))
        dve_step, turned, copied, out, krope = (st.sem(x) for x in ("dve_step", "turned", "copied", "out", "krope"))
        block = st.block()
        lat = [(cqT, RQ, G_Q, Q_RANK), (ckvT, RK, G_KV, KV_RANK)]

        @block.sync
        def _(sp):
            sp.dma_start(cqT[:], D["z"][Z_CQ:Z_CKV, :].rearrange("(k p) t -> p k t", p=P)).then_inc(z_in, 16)
            sp.dma_start(ckvT[:, :, 0:T], D["z"][Z_CKV:Z_MISC, :].rearrange("(k p) t -> p k t", p=P)).then_inc(z_in, 16)
            sp.dma_start(kT[lo:hi, 0, 0:T], D["z"][Z_KR:Z_KR + B_ROPE, :]).then_inc(c_in, 16)
            sp.dma_start(krs[lo:hi, :], D["z"][Z_KRS:Z_KRS + B_ROPE, :]).then_inc(c_in, 16)
            sp.dma_start(cs[lo:hi], D["rope_k"]).then_inc(c_in, 16)
            sp.dma_start(cache[:], D["c_ckv"].rearrange("(c p) r -> p c r", p=P)).then_inc(c_in, 16)
            sp.dma_start(rcache[:], D["c_krope"].rearrange("(c p) r -> p c r", p=P)).then_inc(c_in, 16)
            sp.wait_ge(copied, 2 * CT + 2 * NT)
            for dst, src in (("ckv", rows), ("krope", rrows)):
                sp.dma_start(D["p_" + dst].rearrange("(c p) r -> p c r", p=P), src[:, 0:NT - 1, :]).then_inc(out, 16)
                sp.dma_start(D["s_" + dst], src[0:DEC_SEQ, NT - 1, :]).then_inc(out, 16)
            sp.wait_ge(out, 64)

        @block.scalar
        def _(act):
            for i, (x, kts, _, _) in enumerate(lat):
                act.wait_ge(z_in, 32)
                if i:
                    act.wait_ge(summed, NC)
                nc.scalar.activation(sq[:, 0:kts, :], x[:, :, 0:T], ACT.Square).then_inc(squared, 1)
            for i in range(2):
                act.wait_ge(var_done, 2 * NC * (i + 1))
                nc.scalar.activation(var[:, i], var[:, i], ACT.Sqrt).then_inc(rooted, 1)

        @block.tensor
        def _(pe):
            for i, (_, kts, _, _) in enumerate(lat):
                pe.wait_ge(squared, i + 1)
                for c, (c0, w) in enumerate(CHUNKS):
                    for k in range(kts):
                        last = nc.tensor.matmul(mean[:, i, c, 0:w], S["ones"][:], sq[:, k, c0:c0 + w],
                                                start=(k == 0), stop=(k == kts - 1))
                    last.then_inc(summed, 1)
            pe.wait_ge(c_in, 16 * 5)
            m = 0
            for c in range(CT):
                if m >= 2:
                    pe.wait_ge(copied, m - 1)
                for k in range(RK):
                    last = nc.tensor.transpose(turn[:, m % 2, k * P:(k + 1) * P], cache[:, c, k * P:(k + 1) * P], S["ident"][:])
                last.then_inc(turned, 1)
                m += 1
            for c in range(CT):
                pe.wait_ge(copied, m - 1)
                nc.tensor.transpose(turn[0:B_ROPE, m % 2, 0:P], rcache[:, c, :], S["ident"][:]).then_inc(turned, 1)
                m += 1
            pe.wait_ge(normed, RQ + RK)
            pe.wait_ge(krope, 3)
            for c in range(NT):
                w = tile_width(c)
                pe.wait_ge(copied, m - 1)
                for k in range(RK):
                    last = nc.tensor.transpose(turn[0:w, m % 2, k * P:(k + 1) * P], ckvT[:, k, c * P:c * P + w], S["ident"][:])
                last.then_inc(turned, 1)
                m += 1
            for c in range(NT):
                w = tile_width(c)
                pe.wait_ge(copied, m - 1)
                nc.tensor.transpose(turn[0:w, m % 2, 0:B_ROPE], kT[lo:hi, 0, c * P:c * P + w],
                                    S["ident"][lo:hi, lo:hi]).then_inc(turned, 1)
                m += 1

        @block.vector
        def _(dve):
            v = nc.vector
            dve.wait_ge(c_in, 16 * 5)
            kr = kT[lo:hi, 0, 0:T]
            v.tensor_tensor(kr, kr, cs[lo:hi, 0], ALU.mult).then_inc(dve_step, 1)
            v.tensor_tensor(krs[lo:hi], krs[lo:hi], cs[lo:hi, 1], ALU.mult).then_inc(dve_step, 1)
            dve.wait_ge(dve_step, 2)
            v.tensor_tensor(kr, kr, krs[lo:hi], ALU.add).then_inc(krope, 1)
            m = 0
            for c in range(CT):
                dve.wait_ge(turned, m + 1)
                v.tensor_copy(ckvT[:, :, T + c * P:T + (c + 1) * P],
                              turn[:, m % 2, 0:RK * P].rearrange("p (k n) -> p k n", k=RK)).then_inc(copied, 1)
                m += 1
            for c in range(CT):
                dve.wait_ge(turned, m + 1)
                v.tensor_copy(kT[lo:hi, 0, T + c * P:T + (c + 1) * P], turn[0:B_ROPE, m % 2, 0:P]).then_inc(copied, 1)
                m += 1
            dve.wait_ge(krope, 1)
            dve.wait_ge(copied, m)
            v.tensor_copy(kT[lo:hi, 1, :], kT[lo:hi, 0, :]).then_inc(krope, 2)
            n = 0
            for i, (x, kts, g0, rank) in enumerate(lat):
                for c, (c0, w) in enumerate(CHUNKS):
                    dve.wait_ge(summed, NC * i + c + 1)
                    v.tensor_scalar(var[:, i, c0:c0 + w], mean[:, i, c, 0:w], 1.0 / rank, EPS, ALU.mult, ALU.add)\
                     .then_inc(var_done, 1)
                    n += 1
                    dve.wait_ge(var_done, n)
                    v.reciprocal(var[:, i, c0:c0 + w], var[:, i, c0:c0 + w]).then_inc(var_done, 1)
                    n += 1
            for i, (x, kts, g0, rank) in enumerate(lat):
                dve.wait_ge(rooted, i + 1)
                for k in range(kts):
                    v.scalar_tensor_tensor(out=x[:, k, 0:T], in0=x[:, k, 0:T], scalar=S["gains"][:, g0 + k:g0 + k + 1],
                                           in1=var[:, i], op0=ALU.mult, op1=ALU.mult).then_inc(normed, 1)
            for c in range(NT):
                w = tile_width(c)
                dve.wait_ge(turned, m + 1)
                v.tensor_copy(rows[0:w, c, :], turn[0:w, m % 2, 0:KV_RANK]).then_inc(copied, 1)
                m += 1
            for c in range(NT):
                w = tile_width(c)
                dve.wait_ge(turned, m + 1)
                v.tensor_copy(rrows[0:w, c, :], turn[0:w, m % 2, 0:B_ROPE]).then_inc(copied, 1)
                m += 1


def attention_stage(nc, S, D, kind):
    mla = kind == "mla"
    pairs = (B_HEADS if mla else C_HEADS) // 2
    cat0 = (A_HEADS * A_DIM // P) if mla else 0
    N = 2 * NT
    CT = PAST_LEN // P
    VT = NT + CT
    H = 64
    RQ, RK = Q_RANK // P, KV_RANK // P
    hhi, hlo = S["hhi"], S["hlo"]

    def key_tiles(t):
        if t == NT - 1:
            return [(T + c * P, P, NT + c) for c in range(CT)] + [(SEQ, DEC_SEQ, NT - 1)]
        first = 0 if mla else max(0, t - 4)
        return [(j * P, P, j) for j in range(first, t + 1)]

    if mla:
        KC = [(c, 400) for c in range(0, KEYS, 400)]
        items = [("knope", i, 1, 1) for i in range(len(KC))] + [("qnope", i, 1, 1) for i in range(NC)]
        for i in range(NC):
            items += [("qrope", i, 0, 1), ("qswap", i, 0, 1)]
        items += [("v", i, 0, 1) for i in range(4)]
    else:
        items = [("kcache", 0, 0, 1), ("v", 0, 0, 1), ("k", 0, 1, 0), ("v", 1, 0, 1), ("k", 1, 1, 0), ("v", 2, 0, 1)]
    NI = len(items)
    act_before = [sum(x[2] for x in items[:m]) for m in range(NI + 1)]
    dve_before = [sum(x[3] for x in items[:m]) for m in range(NI + 1)]
    NA, ND = act_before[-1], dve_before[-1]

    with Stage(nc, kind) as st:
        V = st.sb("V", [P, VT, P])
        p = st.sb("p", [P, 2, 1024])
        pT = st.sb("pT", [P, 2, 1024])
        neg_max, total, inv = (st.sb(x, [P, N]) for x in ("neg_max", "total", "inv"))
        o = st.sb("o", [P, 2, P])
        if mla:
            kT = S["kT"]
            qT = st.sb("qT", [B_NOPE + B_ROPE, 2, T])
            w_nope, w_rope, w_swap = st.sb("w_nope", [P, RQ, P]), st.sb("w_rope", [P, RQ, 64]), st.sb("w_swap", [P, RQ, 64])
            w_uk, w_uv = st.sb("w_uk", [P, RK, P]), st.sb("w_uv", [P, RK, P])
            rope = st.sb("rope", [64, 2, T])
            t1, t2 = st.sb("t1", [64, T]), st.sb("t2", [64, T])
        else:
            qin, kin, vin = (st.sb(x, [P, T]) for x in ("qin", "kin", "vin"))
            cin = st.sb("cin", [P, CT, P])
            bin_ = st.sb("bin", [P, 2, 256])
            qT, kT = st.sb("qT", [P, T]), st.sb("kT", [P, KEYS])
            ktok = st.sb("ktok", [P, 5, P])
            far = st.sb("far", [P, 2])
            bias = st.sb("bias", [P, 2, 256])
        pS = st.ps("pS", [P, 4, 512])
        pP = st.ps("pP", [P, 2, 512])
        pO = st.ps("pO", [P, 512])
        pOT = st.ps("pOT", [P, 512])
        names = ("loaded", "prepped", "act_kept", "dve_kept", "pool_kept", "tables", "scored", "biased", "maxed",
                 "exped", "turned", "p_kept", "summed", "inverted", "normed", "o_turned", "hi", "lo", "apart",
                 "stored", "far_done", "bias_done", "v_loaded")
        s = {x: st.sem(x) for x in names}
        block = st.block()

        def value_tiles(i):
            tiles = [(j * P, tile_width(j), j) for j in range(NT)] + [(T + c * P, P, NT + c) for c in range(CT)]
            return [tiles[j] for j in (range(0, 4), range(4, 8), range(NT, VT), range(8, 9))[i]]

        def q_of(t, e):
            w = tile_width(t)
            return qT[:, e, t * P:t * P + w] if mla else qT[H * e:H * e + H, t * P:t * P + w]

        def k_of(e, c0, w):
            return kT[:, e, c0:c0 + w] if mla else kT[H * e:H * e + H, c0:c0 + w]

        def scores_of(n):
            return pS[:, 2 * (n % 2):2 * (n % 2) + 2, :].rearrange("p b n -> p (b n)")

        turned_of = pP[:].rearrange("p b n -> p (b n)")

        def head_out(t, hp):
            w = tile_width(t)
            cols = slice(t * P, t * P + w)
            return [x[:, bass.ds(hp + cat0, 1), cols].rearrange("p a n -> p (a n)") for x in (hhi, hlo)]

        @block.sync
        def _(sp):
            def load(hp):
                if mla:
                    for dst, name, width in ((w_nope, "w_qn", P), (w_rope, "w_qr", 64), (w_swap, "w_qs", 64),
                                             (w_uk, "w_uk", P), (w_uv, "w_uv", P)):
                        src = D[name].rearrange("(k p) n -> p k n", p=P)[:, :, bass.ds(hp * width, width)]
                        sp.dma_start(dst[:], src).then_inc(s["loaded"], 16)
                else:
                    for i, dst in enumerate((qin, kin, vin)):
                        sp.dma_start(dst[:], D["z"][bass.ds(hp * P + i * D_MODEL, P), :]).then_inc(s["loaded"], 16)
                    src = D["c_k"].rearrange("(c p) n -> p c n", p=P)[:, :, bass.ds(hp * P, P)]
                    sp.dma_start(cin[:], src).then_inc(s["loaded"], 16)
                    sp.dma_start(bin_[:], D["bias"][bass.ds(2 * hp, 2), :, :].rearrange("h p j -> p h j"))\
                      .then_inc(s["loaded"], 16)

            def store(hp):
                col = bass.ds(hp * P, P)
                sp.wait_ge(s["act_kept"], NA * hp + NA)
                sp.sem_inc(s["apart"], 1)
                sp.wait_ge(s["dve_kept"], ND * hp + ND)
                sp.sem_inc(s["apart"], 1)
                for src, new, kv in ((ktok[:, 0:4, :], ktok[0:DEC_SEQ, 4, :], "bk"), (V[:, 4:8, :], V[0:DEC_SEQ, 8, :], "bv")):
                    sp.dma_start(D["p_" + kv].rearrange("(c p) n -> p c n", p=P)[:, :, col], src).then_inc(s["stored"], 16)
                    sp.dma_start(D["s_" + kv][PAST_LEN - DEC_SEQ:PAST_LEN, col], new).then_inc(s["stored"], 16)

            def load_v(hp):
                src = D["c_v"].rearrange("(c p) n -> p c n", p=P)[:, :, bass.ds(hp * P, P)]
                sp.dma_start(V[:, NT:VT, :], src).then_inc(s["v_loaded"], 16)

            if mla:
                sp.dma_start(rope[:], D["rope_q"]).then_inc(s["tables"], 16)
            load(0)
            if not mla:
                load_v(0)
                for kv in ("k", "v"):
                    sp.dma_start(D["s_b" + kv][0:PAST_LEN - DEC_SEQ, :], D["c_" + kv][DEC_SEQ:PAST_LEN, :])\
                      .then_inc(s["tables"], 16)
            with sp.Fori(1, pairs) as hp:
                sp.wait_ge(s["prepped"], NI * hp)
                if not mla:
                    sp.sem_inc(s["apart"], 1)
                    sp.wait_ge(s["pool_kept"], 2 * hp)
                    sp.wait_ge(s["far_done"], 2 * hp)
                sp.sem_inc(s["apart"], 1)
                load(hp)
                if not mla:
                    store(hp - 1)
                    sp.wait_ge(s["summed"], N * hp + 2)
                    sp.sem_inc(s["apart"], 1)
                    load_v(hp)
            if not mla:
                store(pairs - 1)
                sp.wait_ge(s["stored"], 64 * pairs + 64)
                sp.wait_ge(s["tables"], 32)

        @block.tensor
        def _(pe):
            pe.sem_inc(s["summed"], 2)
            pe.sem_inc(s["o_turned"], 2)

            def start_item(hp, m):
                if m >= 4:
                    if act_before[m - 3] > 0:
                        pe.wait_ge(s["act_kept"], NA * hp + act_before[m - 3])
                    if dve_before[m - 3] > 0:
                        pe.wait_ge(s["dve_kept"], ND * hp + dve_before[m - 3])

            def prepare(hp):
                pe.wait_ge(s["exped"], N * hp + 2)
                pe.wait_ge(s["loaded"], 80 * hp + 80)
                for m, (name, i, _, _) in enumerate(items):
                    start_item(hp, m)
                    bank = pS[:, m % 4, :]
                    if name == "knope":
                        c0, w = KC[i]
                        parts = [(bank[:, 0:w], w_uk[:, k, :], S["ckvT"][:, k, c0:c0 + w], k, RK) for k in range(RK)]
                    elif name in ("qnope", "qrope", "qswap"):
                        c0, w = CHUNKS[i]
                        wt = {"qnope": w_nope, "qrope": w_rope, "qswap": w_swap}[name]
                        M = P if name == "qnope" else 64
                        parts = [(bank[0:M, 0:w], wt[:, k, :], S["cqT"][:, k, c0:c0 + w], k, RQ) for k in range(RQ)]
                    elif mla:
                        parts = []
                        for q, (c0, w, _) in enumerate(value_tiles(i)):
                            parts += [(bank[0:w, q * P:(q + 1) * P], S["ckvT"][:, k, c0:c0 + w], w_uv[:, k, :], k, RK)
                                      for k in range(RK)]
                    else:
                        parts = None
                        src = {"kcache": None, "v": vin, "k": kin}[name]
                        tiles = range(4) if name == "kcache" else {"v": (range(0, 4), range(4, 8), range(8, 9)),
                                                                   "k": (range(4, 8), range(8, 9))}[name][i]
                        for q, c in enumerate(tiles):
                            if src is None:
                                last = nc.tensor.transpose(bank[:, q * P:(q + 1) * P], cin[:, c, :], S["ident"][:])
                            else:
                                w = tile_width(c)
                                if w < P:
                                    pe.sem_inc(s["apart"], 1)
                                last = nc.tensor.transpose(bank[0:w, q * P:(q + 1) * P], src[:, c * P:c * P + w],
                                                           S["ident"][:])
                    for out, lhsT, rhs, k, kts in parts or []:
                        last = nc.tensor.matmul(out, lhsT, rhs, start=(k == 0), stop=(k == kts - 1))
                    last.then_inc(s["prepped"], 1)
                pe.wait_ge(s["act_kept"], NA * hp + NA)
                pe.wait_ge(s["dve_kept"], ND * hp + ND)
                if not mla:
                    pe.wait_ge(s["pool_kept"], 2 * hp + 2)
                    pe.wait_ge(s["v_loaded"], 16 * hp + 16)

            def score(hp, n):
                t, e = n // 2, n % 2
                w = tile_width(t)
                tiles = key_tiles(t)
                W = sum(x[1] for x in tiles)
                pe.wait_ge(s["exped"], N * hp + n + 1)
                if w < P:
                    pe.sem_inc(s["apart"], 1)
                out = scores_of(n)
                masks = []
                if t < NT - 1 and mla:
                    masks.append((0, W - CHUNK))
                if t >= 4 and t < NT - 1 and not mla:
                    masks.append((1, 0))
                runs = []
                c = 0
                for k0, kw, _ in tiles:
                    if runs and runs[-1][1] + runs[-1][2] == k0 and runs[-1][2] + kw <= 512 and c % 512:
                        runs[-1][2] += kw
                    else:
                        runs.append([c, k0, kw])
                    c += kw
                for r, (c, k0, kw) in enumerate(runs):
                    here = [m for m in masks if c <= m[1] < c + kw]
                    last = nc.tensor.matmul(out[0:w, c:c + kw], q_of(t, e), k_of(e, k0, kw), start=True, stop=not here)
                    for half, mc in here:
                        last = nc.tensor.matmul(out[0:w, mc:mc + CHUNK], S["halves"][0:1, half * P:half * P + w],
                                                S["halves"][0:1, 2 * P:2 * P + CHUNK], start=False, stop=True)
                last.then_inc(s["scored"], 1)

            def turn(hp, n):
                t = n // 2
                w = tile_width(t)
                pe.wait_ge(s["exped"], N * hp + n + 3)
                pe.wait_ge(s["p_kept"], N * hp + n + 1)
                if w < P:
                    pe.sem_inc(s["apart"], 1)
                c = 0
                for b, (_, kw, _) in enumerate(key_tiles(t)):
                    last = nc.tensor.transpose(turned_of[0:kw, b * P:b * P + w], p[0:w, n % 2, c:c + kw], S["ident"][0:w, 0:w])
                    c += kw
                last.then_inc(s["turned"], 1)

            def weigh(hp, n):
                t, e = n // 2, n % 2
                w = tile_width(t)
                tiles = key_tiles(t)
                pe.wait_ge(s["p_kept"], N * hp + n + 2)
                pe.wait_ge(s["normed"], N * hp + n + 1)
                if w < P:
                    pe.sem_inc(s["apart"], 1)
                for b, (_, kw, vt) in enumerate(tiles):
                    last = nc.tensor.matmul(pO[0:w, 0:H], pT[0:kw, n % 2, b * P:b * P + w],
                                            V[0:kw, vt, e * H:(e + 1) * H], start=(b == 0), stop=(b == len(tiles) - 1))
                last.then_inc(s["summed"], 1)

            def turn_out(hp, t):
                w = tile_width(t)
                pe.wait_ge(s["normed"], N * hp + 2 * t + 2 + 1)
                pe.wait_ge(s["lo"], NT * hp + t + 1)
                if w < P:
                    pe.sem_inc(s["apart"], 1)
                nc.tensor.transpose(pOT[:, 0:w], o[0:w, t % 2, :], S["ident"][0:w, 0:w]).then_inc(s["o_turned"], 1)

            with pe.Fori(0, pairs) as hp:
                prepare(hp)
                for n in range(-1, N + 3):
                    if n + 1 < N:
                        score(hp, n + 1)
                    if 0 <= n < N:
                        turn(hp, n)
                    if 0 <= n - 1 < N:
                        weigh(hp, n - 1)
                    if n >= 4 and n % 2 == 0:
                        turn_out(hp, (n - 4) // 2)

        @block.scalar
        def _(act):
            act.sem_inc(s["exped"], 2)
            act.sem_inc(s["p_kept"], 1)

            def exp(hp, n):
                t = n // 2
                w = tile_width(t)
                W = sum(x[1] for x in key_tiles(t))
                act.wait_ge(s["maxed"], N * hp + n + 1)
                nc.scalar.activation(p[0:w, n % 2, 0:W], scores_of(n)[0:w, 0:W], ACT.Exp, bias=neg_max[0:w, n:n + 1],
                                     accum_out=total[0:w, n:n + 1]).then_inc(s["exped"], 1)

            def keep(hp, n):
                t = n // 2
                w = tile_width(t)
                tiles = key_tiles(t)
                act.wait_ge(s["turned"], N * hp + n + 1)
                act.wait_ge(s["summed"], N * hp + n + 1)
                if w == P:
                    cols = len(tiles) * P
                    nc.scalar.activation(pT[:, n % 2, 0:cols], turned_of[:, 0:cols], ACT.Copy).then_inc(s["p_kept"], 1)
                else:
                    wide = lambda x: x.rearrange("p (b n) -> p b n", n=P)[:, 0:CT, 0:w]
                    nc.scalar.activation(wide(pT[:, n % 2, :]), wide(turned_of), ACT.Copy)
                    nc.scalar.activation(pT[0:DEC_SEQ, n % 2, CT * P:CT * P + w], turned_of[0:DEC_SEQ, CT * P:CT * P + w],
                                         ACT.Copy).then_inc(s["p_kept"], 1)

            def high(hp, t):
                w = tile_width(t)
                act.wait_ge(s["o_turned"], NT * hp + t + 3)
                nc.scalar.activation(head_out(t, hp)[0], pOT[:, 0:w], ACT.Copy).then_inc(s["hi"], 1)

            with act.Fori(0, pairs) as hp:
                for m, (name, i, mine, _) in enumerate(items):
                    if not mine:
                        continue
                    act.wait_ge(s["prepped"], NI * hp + m + 1)
                    bank = pS[:, m % 4, :]
                    if name == "knope":
                        c0, w = KC[i]
                        nc.scalar.activation(kT[0:B_NOPE, 0, c0:c0 + w], bank[0:B_NOPE, 0:w], ACT.Copy).then_inc(s["act_kept"], 1)
                    elif name == "qnope":
                        c0, w = CHUNKS[i]
                        nc.scalar.activation(qT[0:B_NOPE, 0, c0:c0 + w], bank[0:B_NOPE, 0:w], ACT.Copy, scale=MLA_SCALE)\
                          .then_inc(s["act_kept"], 1)
                    else:
                        if hp is not None and i == 0:
                            act.wait_ge(s["stored"], 64 * hp + 64)
                        w = P if i == 0 else DEC_SEQ
                        dst = ktok[:, 0:4, :].rearrange("p c n -> p (c n)") if i == 0 else ktok[0:w, 4, :]
                        nc.scalar.activation(dst, bank[0:w, 0:512 if i == 0 else P], ACT.Copy).then_inc(s["act_kept"], 1)
                for n in range(-1, N + 3):
                    if n + 1 < N:
                        exp(hp, n + 1)
                    if 0 <= n < N:
                        keep(hp, n)
                    if n >= 4 and n % 2 == 0:
                        high(hp, (n - 4) // 2)

        @block.vector
        def _(dve):
            v = nc.vector
            dve.sem_inc(s["normed"], 1)
            dve.sem_inc(s["lo"], 1)
            if mla:
                dve.wait_ge(s["tables"], 16)
            else:
                dve.sem_inc(s["stored"], 64)

            def kept(name, i, bank, hp):
                if name == "knope":
                    c0, w = KC[i]
                    return v.tensor_copy(kT[0:B_NOPE, 1, c0:c0 + w], bank[B_NOPE:2 * B_NOPE, 0:w])
                if name == "qnope":
                    c0, w = CHUNKS[i]
                    return v.tensor_scalar(qT[0:B_NOPE, 1, c0:c0 + w], bank[B_NOPE:2 * B_NOPE, 0:w], MLA_SCALE, None, ALU.mult)
                if name in ("qrope", "qswap"):
                    c0, w = CHUNKS[i]
                    dst, table = (t1, 0) if name == "qrope" else (t2, 1)
                    return v.tensor_tensor(dst[:, c0:c0 + w], rope[:, table, c0:c0 + w], bank[0:64, 0:w], ALU.mult)
                if name == "kcache":
                    return v.tensor_copy(kT[:, T:KEYS], bank)
                if mla:
                    tiles = value_tiles(i)
                    w, first, count = tiles[0][1], tiles[0][2], len(tiles)
                else:
                    w, first, count = (P, 4 * i, 4) if i < 2 else (DEC_SEQ, 8, 1)
                return v.tensor_copy(V[0:w, first:first + count, :].rearrange("p c n -> p (c n)"), bank[0:w, 0:count * P])

            def prepare(hp):
                if not mla:
                    dve.wait_ge(s["loaded"], 80 * hp + 80)
                    v.tensor_copy(far[:], bin_[:, :, 0]).then_inc(s["far_done"], 1)
                    dve.wait_ge(s["far_done"], 2 * hp + 1)
                    for e in range(2):
                        last = v.tensor_scalar(bias[:, e, :], bin_[:, e, :], far[:, e:e + 1], None, ALU.subtract)
                    last.then_inc(s["far_done"], 1)
                    dve.wait_ge(s["far_done"], 2 * hp + 2)
                    v.memset(bias[0:CHUNK, :, 256 - CHUNK:256], NEG).then_inc(s["bias_done"], 1)
                    dve.wait_ge(s["bias_done"], hp + 1)
                    dve.wait_ge(s["stored"], 64 * hp + 64)
                for m, (name, i, _, mine) in enumerate(items):
                    if not mine:
                        continue
                    dve.wait_ge(s["prepped"], NI * hp + m + 1)
                    ins = kept(name, i, pS[:, m % 4, :], hp)
                    if name == "qswap":
                        ins.then_inc(s["inverted"], 1)
                        dve.wait_ge(s["inverted"], (N + NC) * hp + i + 1)
                        c0, w = CHUNKS[i]
                        for e in range(2):
                            ins = v.tensor_tensor(qT[B_NOPE:B_NOPE + B_ROPE, e, c0:c0 + w],
                                                  t1[e * B_ROPE:(e + 1) * B_ROPE, c0:c0 + w],
                                                  t2[e * B_ROPE:(e + 1) * B_ROPE, c0:c0 + w], ALU.add)
                    ins.then_inc(s["dve_kept"], 1)

            def maximum(hp, n):
                t, e = n // 2, n % 2
                w = tile_width(t)
                W = sum(x[1] for x in key_tiles(t))
                x = scores_of(n)
                dve.wait_ge(s["scored"], N * hp + n + 1)
                if not mla:
                    near = (P, 128, 256) if t == 0 else (256, 0, 256)
                    if t == NT - 1:
                        near = (192, 0, 192)
                    cols = x[0:w, W - near[0]:W]
                    v.tensor_tensor(cols, cols, bias[0:w, e, near[1]:near[2]], ALU.add).then_inc(s["biased"], 1)
                    dve.wait_ge(s["biased"], N * hp + n + 1)
                v.tensor_reduce(neg_max[0:w, n:n + 1], x[0:w, 0:W], AX_X, ALU.max, negate=True).then_inc(s["maxed"], 1)

            def norm(hp, n):
                t, e = n // 2, n % 2
                w = tile_width(t)
                dve.wait_ge(s["summed"], N * hp + n + 3)
                v.reciprocal(inv[0:w, n:n + 1], total[0:w, n:n + 1]).then_inc(s["inverted"], 1)
                dve.wait_ge(s["inverted"], (N + NC) * hp + NC + n + 1 if mla else N * hp + n + 1)
                dve.wait_ge(s["o_turned"], NT * hp + t + 1)
                v.tensor_scalar(o[0:w, t % 2, e * H:(e + 1) * H], pO[0:w, 0:H],
                                inv[0:w, n:n + 1], None, ALU.mult).then_inc(s["normed"], 1)

            def low(hp, t):
                w = tile_width(t)
                dve.wait_ge(s["hi"], NT * hp + t + 1)
                hi_, lo_ = head_out(t, hp)
                v.tensor_tensor(lo_, pOT[:, 0:w], hi_, ALU.subtract).then_inc(s["lo"], 1)

            with dve.Fori(0, pairs) as hp:
                prepare(hp)
                for n in range(-1, N + 3):
                    if n + 1 < N:
                        maximum(hp, n + 1)
                    if 0 <= n - 1 < N:
                        norm(hp, n - 1)
                    if n >= 4 and n % 2 == 0:
                        low(hp, (n - 4) // 2)

        if not mla:
            @block.gpsimd
            def _(pool):
                with pool.Fori(0, pairs) as hp:
                    pool.wait_ge(s["loaded"], 80 * hp + 80)
                    pool.wait_ge(s["summed"], N * hp + 2)
                    pool.sem_inc(s["apart"], 1)
                    nc.gpsimd.tensor_scalar(qT[:], qin[:], C_SCALE, None, ALU.mult).then_inc(s["pool_kept"], 1)
                    nc.gpsimd.tensor_copy(kT[:, 0:T], kin[:]).then_inc(s["pool_kept"], 1)


def band_stage(nc, S, D):
    H = C_DIM
    TILES = [4, 0, 5, 1, 6, 2, 7, 3, NT - 1]
    N = len(TILES)
    CT = PAST_LEN // P
    VT = NT + CT
    pairs = C_HEADS // 2
    TURNS = 3
    STAGE_AT = {2: 0, 4: 1, 6: 2}
    LOADS, STORES = 8, 4
    hhi, hlo = S["hhi"], S["hlo"]

    def key_tiles(t):
        if t == NT - 1:
            return [(T + c * P, P, NT + c) for c in range(CT)] + [(SEQ, DEC_SEQ, NT - 1)]
        return [(j * P, P, j) for j in range(max(0, t - 4), t + 1)]

    def score_cols(t):
        W = sum(x[1] for x in key_tiles(t))
        c0 = 2 * P if W > 512 else 0
        return c0, c0 + W

    with Stage(nc, "band") as st:
        q_in, k_in, v_in = st.sb("q_in", [P, T]), st.sb("k_in", [P, T]), st.sb("v_in", [H, T])
        c_in = st.sb("c_in", [P, CT, 2, H])
        b_in = st.sb("b_in", [P, 2 * P])
        q2, k2 = st.sb("q2", [P, 2, NT * P], F32R), st.sb("k2", [P, 2, KEYS], F32R)
        klo = st.sb("klo", [H, 2, KEYS], F32R)
        V = st.sb("V", [P, 2, VT, P])
        ktok = st.sb("ktok", [P, 5, H])
        near = st.sb("near", [P, 2 * P])
        bias = st.sb("bias", [P, 2, 2, 2 * P], F32R)
        ident = st.sb("ident", [P, P], F32R)
        p, pT = st.sb("p", [P, 2, 640]), st.sb("pT", [P, 2, 640])
        neg_max, total, inv = (st.sb(x, [P, 2 * N]) for x in ("neg_max", "total", "inv"))
        diag = st.sb("diag", [P, 2, P])
        halves = st.sb("halves", [1, 2 * P + CHUNK], F32R)
        pS = st.ps("pS", [P, 2, 2, 512])
        pP = st.ps("pP", [P, 1024])
        pO = st.ps("pO", [P, 512])
        spare = st.ps("spare", [P, 512])
        names = ("loaded", "cv_in", "q_hi", "k_hi", "q_lo", "k_lo", "kc_hi", "turned_in", "taken", "scored",
                 "maxed", "exped", "inverted", "diag_set", "turned", "p_kept", "summed", "hi", "lo", "apart", "stored",
                 "near_set", "bias_hi", "bias_lo", "rolled", "set_up")
        s = {x: st.sem(x) for x in names}
        block = st.block()

        def own(e):
            return slice(H * e, H * e + H)

        def step_of(hp, m):
            return 2 * N * hp + m, (m // N) % 2, TILES[m % N]

        def waits_apart(eng, *waits):
            for name, count in waits:
                eng.wait_ge(s[name], count)
                eng.sem_inc(s["apart"], 1)

        @block.sync
        def _(sp):
            def load(h):
                for half in range(2):
                    rows = slice(half * H, half * H + H)
                    sp.dma_start(q_in[rows, :], D["z"][bass.ds(h * H, H), :]).then_inc(s["loaded"], 16)
                    sp.dma_start(k_in[rows, :], D["z"][bass.ds(h * H + D_MODEL, H), :]).then_inc(s["loaded"], 16)
                    sp.dma_start(c_in[:, :, half, :], D["c_k"].rearrange("(c p) n -> p c n", p=P)[:, :, bass.ds(h * H, H)])\
                      .then_inc(s["loaded"], 16)
                sp.dma_start(v_in[:], D["z"][bass.ds(h * H + 2 * D_MODEL, H), :]).then_inc(s["loaded"], 16)
                sp.dma_start(b_in[:], D["bias"][bass.ds(h, 1), :, :].rearrange("h p j -> p (h j)")).then_inc(s["loaded"], 16)

            def load_cv(h, e):
                sp.dma_start(V[:, e, NT:VT, own(e)], D["c_v"].rearrange("(c p) n -> p c n", p=P)[:, :, bass.ds(h * H, H)])\
                  .then_inc(s["cv_in"], 16)

            def wait_used(h):
                waits_apart(sp, ("q_lo", h + 1), ("k_lo", 2 * h + 2), ("taken", TURNS * h + TURNS), ("bias_lo", h + 1))

            def store(h, e):
                col = bass.ds(h * H, H)
                for src, new, kv in ((ktok[:, 0:4, :], ktok[0:DEC_SEQ, 4, :], "bk"),
                                     (V[:, e, 4:8, own(e)], V[0:DEC_SEQ, e, 8, own(e)], "bv")):
                    sp.dma_start(D["p_" + kv].rearrange("(c p) n -> p c n", p=P)[:, :, col], src).then_inc(s["stored"], 16)
                    sp.dma_start(D["s_" + kv][PAST_LEN - DEC_SEQ:PAST_LEN, col], new).then_inc(s["stored"], 16)

            def head(hp, e, last):
                h = 2 * hp + e
                if not (last and e == 1):
                    waits_apart(sp, ("summed", N * h + 1))
                    load_cv(h + 1, 1 - e)
                    wait_used(h + 1)
                    if not last:
                        load(h + 2)
                    store(h + 1, 1 - e)

            load(0)
            load_cv(0, 0)
            for kv in ("k", "v"):
                sp.dma_start(D["s_b" + kv][0:PAST_LEN - DEC_SEQ, :], D["c_" + kv][DEC_SEQ:PAST_LEN, :]).then_inc(s["rolled"], 16)
            wait_used(0)
            load(1)
            store(0, 0)
            with sp.Fori(0, pairs - 1) as hp:
                for e in range(2):
                    head(hp, e, False)
            for e in range(2):
                head(pairs - 1, e, True)
            sp.wait_ge(s["stored"], 16 * STORES * (C_HEADS + 1))
            sp.wait_ge(s["rolled"], 32)

        @block.tensor
        def _(pe):
            def turn_in(h, which):
                if not (isinstance(h, int) and h == 0 and which == 0):
                    pe.wait_ge(s["taken"], TURNS * h + which)
                pe.sem_inc(s["apart"], 1)
                if which == 0:
                    pe.wait_ge(s["loaded"], 16 * LOADS * (h + 1))
                    pe.sem_inc(s["apart"], 1)
                    for c in range(8):
                        ins = nc.tensor.transpose(spare[:, c * H:(c + 1) * H], v_in[:, c * P:(c + 1) * P], S["ident"][0:H, 0:H])
                elif which == 1:
                    for q, c in enumerate(range(4, NT)):
                        w = tile_width(c)
                        nc.tensor.transpose(spare[0:w, q * H:(q + 1) * H], k_in[0:H, c * P:c * P + w], S["ident"][0:H, 0:H])
                    ins = nc.tensor.transpose(spare[0:DEC_SEQ, 5 * H:6 * H], v_in[:, SEQ:T], S["ident"][0:H, 0:H])
                else:
                    for c in range(CT):
                        ins = nc.tensor.transpose(spare[:, c * P:(c + 1) * P], c_in[:, c].rearrange("p a n -> p (a n)"),
                                                  S["ident"][:])
                ins.then_inc(s["turned_in"], 1)

            def score(hp, m):
                g, e, t = step_of(hp, m)
                tiles = key_tiles(t)
                if m % N == 0:
                    h = 2 * hp + m // N
                    waits_apart(pe, ("q_lo", h + 1), ("k_lo", 2 * h + 2), ("taken", TURNS * h + TURNS), ("bias_lo", h + 1))
                pe.wait_ge(s["exped"], g + 1)
                out = pS[:, m % 2].rearrange("p b n -> p (b n)")
                end = score_cols(t)[1]
                runs, c = [], score_cols(t)[0]
                for k0, kw, _ in tiles:
                    if runs and runs[-1][1] + runs[-1][2] == k0 and c % 512:
                        runs[-1][2] += kw
                    else:
                        runs.append([c, k0, kw])
                    c += kw
                qs = slice(t * P, t * P + P)
                width, b0 = (P, P) if t == 0 else (192, 0) if t == NT - 1 else (2 * P, 0)
                for r, (c, k0, kw) in enumerate(runs):
                    cols, keys = out[:, c:c + kw], slice(k0, k0 + kw)
                    parts = [(cols, q2[:, e, qs], k2[:, e, keys]), (cols, q2[0:H, e, qs], klo[:, e, keys])]
                    if r == 0 and 4 <= t < NT - 1:
                        parts.append((out[:, c:c + CHUNK], halves[0:1, P:2 * P], halves[0:1, 2 * P:2 * P + CHUNK]))
                    lo_, hi_ = max(c, end - width), c + kw
                    if lo_ < hi_:
                        b = b0 + lo_ - (end - width)
                        parts += [(out[:, lo_:hi_], ident[:], bias[:, e, part, b:b + hi_ - lo_]) for part in range(2)]
                    for q, (dst, lhsT, rhs) in enumerate(parts):
                        ins = nc.tensor.matmul(dst, lhsT, rhs, start=(q == 0), stop=(q == len(parts) - 1))
                ins.then_inc(s["scored"], 1)

            def turn(hp, m):
                g, _, t = step_of(hp, m)
                w = tile_width(t)
                pe.wait_ge(s["p_kept"], g + 1)
                pe.wait_ge(s["diag_set"], g + 1)
                if w < P:
                    pe.sem_inc(s["apart"], 1)
                c = 0
                for b, (_, kw, _) in enumerate(key_tiles(t)):
                    ins = nc.tensor.matmul(pP[0:kw, b * P:b * P + w], p[0:w, m % 2, c:c + kw], diag[0:w, m % 2, 0:w],
                                           start=True, stop=True)
                    c += kw
                ins.then_inc(s["turned"], 1)

            def weigh(hp, m):
                g, e, t = step_of(hp, m)
                w = tile_width(t)
                tiles = key_tiles(t)
                if m % N == 0:
                    waits_apart(pe, ("cv_in", 16 * (2 * hp + m // N + 1)))
                pe.wait_ge(s["lo"], g + 1)
                pe.wait_ge(s["p_kept"], g + 2)
                if w < P:
                    pe.sem_inc(s["apart"], 1)
                for b, (_, kw, vt) in enumerate(tiles):
                    ins = nc.tensor.matmul(pO[:, 0:w], V[0:kw, e, vt, :], pT[0:kw, m % 2, b * P:b * P + w],
                                           start=(b == 0), stop=(b == len(tiles) - 1))
                ins.then_inc(s["summed"], 1)

            def steps(hp, first, last):
                for m in range(2 * N):
                    if not (last and m == 2 * N - 1):
                        score(hp, m + 1)
                    turn(hp, m)
                    if not (first and m == 0):
                        weigh(hp, m - 1)
                    if m % N in STAGE_AT and not (last and m >= N):
                        turn_in(2 * hp + m // N + 1, STAGE_AT[m % N])

            for which in range(TURNS):
                turn_in(0, which)
            pe.wait_ge(s["set_up"], 6)
            score(0, 0)
            steps(0, True, False)
            with pe.Fori(1, pairs - 1) as hp:
                steps(hp, False, False)
            steps(pairs - 1, False, True)
            weigh(pairs - 1, 2 * N - 1)

        @block.scalar
        def _(act):
            act.sem_inc(s["exped"], 2)
            act.sem_inc(s["p_kept"], 1)
            act.sem_inc(s["stored"], 16 * STORES)

            def split_q(h, e):
                act.wait_ge(s["loaded"], 16 * LOADS * (h + 1))
                act.activation(q2[:, e, 0:T], q_in[:], ACT.Copy, scale=C_SCALE).then_inc(s["q_hi"], 1)

            def split_k(h, e):
                act.activation(k2[:, e, 0:T], k_in[:], ACT.Copy).then_inc(s["k_hi"], 1)

            def split_bias(h, e):
                act.wait_ge(s["near_set"], 2 * h + 2)
                act.activation(bias[:, e, 0, :], near[:], ACT.Copy).then_inc(s["bias_hi"], 1)

            def take(h, e, which):
                act.wait_ge(s["turned_in"], TURNS * h + which + 1)
                if which == 1:
                    act.wait_ge(s["stored"], 16 * STORES * (h + 1))
                    act.activation(ktok[:, 0:4, :].rearrange("p c n -> p (c n)"), spare[:, 0:4 * H], ACT.Copy)
                    act.activation(ktok[0:DEC_SEQ, 4, :], spare[0:DEC_SEQ, 4 * H:5 * H], ACT.Copy)
                    act.activation(V[0:DEC_SEQ, e, NT - 1, own(e)], spare[0:DEC_SEQ, 5 * H:6 * H], ACT.Copy)\
                       .then_inc(s["taken"], 1)
                elif which == 2:
                    act.activation(k2[:, e, T:KEYS], spare[:], ACT.Copy).then_inc(s["kc_hi"], 1)

            def exp(hp, m):
                g, _, t = step_of(hp, m)
                w = tile_width(t)
                c0, c1 = score_cols(t)
                act.wait_ge(s["maxed"], g + 1)
                act.activation(p[0:w, m % 2, 0:c1 - c0], pS[0:w, m % 2].rearrange("p b n -> p (b n)")[:, c0:c1], ACT.Exp,
                               bias=neg_max[0:w, m % (2 * N):m % (2 * N) + 1],
                               accum_out=total[0:w, m % (2 * N):m % (2 * N) + 1]).then_inc(s["exped"], 1)

            def keep(hp, m):
                g, _, t = step_of(hp, m)
                w = tile_width(t)
                n = len(key_tiles(t))
                act.wait_ge(s["turned"], g + 1)
                if w == P:
                    act.activation(pT[:, m % 2, 0:n * P], pP[:, 0:n * P], ACT.Copy).then_inc(s["p_kept"], 1)
                else:
                    wide = lambda x: x.rearrange("p (b n) -> p b n", n=P)[:, 0:CT, 0:w]
                    act.activation(wide(pT[:, m % 2, :]), wide(pP[:, 0:640]), ACT.Copy)
                    act.activation(pT[0:DEC_SEQ, m % 2, CT * P:CT * P + w], pP[0:DEC_SEQ, CT * P:CT * P + w],
                                   ACT.Copy).then_inc(s["p_kept"], 1)

            def high(hp, m):
                g, e, t = step_of(hp, m)
                w = tile_width(t)
                pair = hp if m >= 0 else hp - 1
                act.wait_ge(s["summed"], g + 1)
                act.activation(hhi[own(e), bass.ds(pair, 1), t * P:t * P + w].rearrange("p a n -> p (a n)"),
                               pO[own(e), 0:w], ACT.Copy).then_inc(s["hi"], 1)

            def steps(hp, first, last):
                for m in range(2 * N):
                    keep(hp, m)
                    if not (last and m == 2 * N - 1):
                        exp(hp, m + 1)
                    if not (first and m == 0):
                        high(hp, m - 1)
                    if not (last and m >= N):
                        h, e, i = 2 * hp + m // N + 1, 1 - m // N, m % N
                        if i == 0:
                            split_q(h, e)
                        if i == 1:
                            split_k(h, e)
                        if i in STAGE_AT:
                            take(h, e, STAGE_AT[i])
                        if i == 5:
                            split_bias(h, e)

            split_q(0, 0)
            split_k(0, 0)
            split_bias(0, 0)
            for which in range(TURNS):
                take(0, 0, which)
            exp(0, 0)
            steps(0, True, False)
            with act.Fori(1, pairs - 1) as hp:
                steps(hp, False, False)
            steps(pairs - 1, False, True)
            high(pairs - 1, 2 * N - 1)

        @block.vector
        def _(dve):
            dve.sem_inc(s["lo"], 1)
            for e in range(2):
                dve.memset(V[:, e, :, own(1 - e)], 0.0).then_inc(s["set_up"], 1)
                dve.tensor_scalar(q2[:, e, T:NT * P], S["ones"][:, 0:NT * P - T], 0.0, None, ALU.mult)\
                   .then_inc(s["set_up"], 1)
            dve.tensor_copy(halves[:], S["halves"][:]).then_inc(s["set_up"], 1)
            dve.tensor_copy(ident[:], S["ident"][:]).then_inc(s["set_up"], 1)

            def split_q(h, e):
                dve.wait_ge(s["q_hi"], h + 1)
                dve.scalar_tensor_tensor(out=q2[H:P, e, 0:T], in0=q_in[H:P, :], scalar=C_SCALE, in1=q2[H:P, e, 0:T],
                                         op0=ALU.mult, op1=ALU.subtract).then_inc(s["q_lo"], 1)

            def set_bias(h, e):
                dve.wait_ge(s["loaded"], 16 * LOADS * (h + 1))
                dve.tensor_scalar(near[:], b_in[:], b_in[:, 0:1], None, ALU.subtract).then_inc(s["near_set"], 1)
                dve.wait_ge(s["near_set"], 2 * h + 1)
                dve.memset(near[0:CHUNK, 2 * P - CHUNK:2 * P], NEG).then_inc(s["near_set"], 1)

            def split_bias(h, e):
                dve.wait_ge(s["bias_hi"], h + 1)
                dve.tensor_tensor(bias[:, e, 1, :], near[:], bias[:, e, 0, :], ALU.subtract).then_inc(s["bias_lo"], 1)

            def take(h, e, which):
                if which == 0:
                    dve.wait_ge(s["turned_in"], TURNS * h + 1)
                    if not (isinstance(h, int) and h == 0):
                        dve.wait_ge(s["stored"], 16 * STORES * h)
                    dve.tensor_copy(V[:, e, 0:8, own(e)], spare[:].rearrange("p (c n) -> p c n", n=H))\
                       .then_inc(s["taken"], 1)
                elif which == 2:
                    dve.wait_ge(s["kc_hi"], h + 1)
                    dve.tensor_tensor(klo[:, e, T:KEYS], spare[0:H, :], k2[0:H, e, T:KEYS], ALU.subtract)\
                       .then_inc(s["taken"], 1)

            def maximum(hp, m):
                g, e, t = step_of(hp, m)
                w = tile_width(t)
                c0, c1 = score_cols(t)
                dve.wait_ge(s["scored"], g + 1)
                dve.tensor_reduce(neg_max[0:w, m % (2 * N):m % (2 * N) + 1], pS[0:w, m % 2].rearrange("p b n -> p (b n)")[:, c0:c1],
                                  AX_X, ALU.max, negate=True).then_inc(s["maxed"], 1)

            def inverse(hp, m):
                g, _, t = step_of(hp, m)
                w = tile_width(t)
                col = slice(m % (2 * N), m % (2 * N) + 1)
                dve.wait_ge(s["exped"], g + 3)
                dve.reciprocal(inv[0:w, col], total[0:w, col]).then_inc(s["inverted"], 1)
                dve.wait_ge(s["inverted"], g + 1)
                dve.tensor_scalar(diag[0:w, m % 2, 0:w], S["ident"][0:w, 0:w], inv[0:w, col], None, ALU.mult)\
                   .then_inc(s["diag_set"], 1)

            def low(hp, m):
                g, e, t = step_of(hp, m)
                w = tile_width(t)
                pair = bass.ds(hp if m >= 0 else hp - 1, 1)
                part = [x[own(e), pair, t * P:t * P + w].rearrange("p a n -> p (a n)") for x in (hhi, hlo)]
                dve.wait_ge(s["hi"], g + 1)
                dve.tensor_tensor(part[1], pO[own(e), 0:w], part[0], ALU.subtract).then_inc(s["lo"], 1)

            def steps(hp, first, last):
                for m in range(2 * N):
                    if not (last and m == 2 * N - 1):
                        maximum(hp, m + 1)
                        inverse(hp, m + 1)
                    if not (first and m == 0):
                        low(hp, m - 1)
                    if not (last and m >= N):
                        h, e, i = 2 * hp + m // N + 1, 1 - m // N, m % N
                        if i == 1:
                            split_q(h, e)
                        if i in STAGE_AT:
                            take(h, e, STAGE_AT[i])
                        if i == 3:
                            set_bias(h, e)
                        if i == 5:
                            split_bias(h, e)

            set_bias(0, 0)
            split_q(0, 0)
            split_bias(0, 0)
            for which in range(TURNS):
                take(0, 0, which)
            maximum(0, 0)
            inverse(0, 0)
            steps(0, True, False)
            with dve.Fori(1, pairs - 1) as hp:
                steps(hp, False, False)
            steps(pairs - 1, False, True)
            low(pairs - 1, 2 * N - 1)

        @block.gpsimd
        def _(pool):
            def split_k(h, e, half):
                pool.wait_ge(s["k_hi"], h + 1)
                pool.sem_inc(s["apart"], 1)
                cols = slice(half * (T // 2), (half + 1) * (T // 2))
                pool.tensor_tensor(klo[:, e, cols], k_in[0:H, cols], k2[0:H, e, cols], ALU.subtract).then_inc(s["k_lo"], 1)

            for half in range(2):
                split_k(0, 0, half)
            split_k(1, 1, 0)
            split_k(1, 1, 1)
            with pool.Fori(1, pairs) as hp:
                for e in range(2):
                    for half in range(2):
                        split_k(2 * hp + e, e, half)


def build(nc, D):
    with ExitStack() as ctx:
        def sb(name, shape, dt=F32):
            return ctx.enter_context(nc.sbuf_tensor(name, shape, dt))
        S = {"ident": sb("ident", [P, P]), "ones": sb("ones", [P, P]), "gains": sb("gains", [P, G_COLS]),
             "halves": sb("halves", [1, 2 * P + CHUNK]),
             "xT": sb("xT", [P, KT, T]), "hhi": sb("hhi", [P, KT, T], F32R), "hlo": sb("hlo", [P, KT, T], F32R)}
        load_stage(nc, S, D)
        project_stage(nc, S, "in0", D["w_in"], Z_ROWS // UNIT, D["z"], G_MIX0)
        with Stage(nc, "recur") as st:
            S["aT"], S["enm"], S["wk"], S["decay"] = (st.sb(x, [P, R]) for x in ("aT", "enm", "wk", "decay"))
            S["upper"], S["lower"] = st.sb("upper", [P, P]), st.sb("lower", [P, P])
            gate_stage(nc, S, D)
            mlstm_stage(nc, S, D)
        with Stage(nc, "latents") as st:
            S["cqT"], S["ckvT"] = st.sb("cqT", [P, Q_RANK // P, T]), st.sb("ckvT", [P, KV_RANK // P, KEYS])
            S["kT"] = st.sb("kT", [B_NOPE + B_ROPE, 2, KEYS])
            latent_stage(nc, S, D)
            attention_stage(nc, S, D, "mla")
        project_stage(nc, S, "out0", D["w_out0"], D_MODEL // UNIT)
        ffn_stage(nc, S, "ffn0", G_FFN0, D["w_gate"][0], D["w_up"][0], D["w_down"][0])
        project_stage(nc, S, "in1", D["w_qkv"], 3 * D_MODEL // UNIT, D["z"], G_MIX1)
        band_stage(nc, S, D)
        project_stage(nc, S, "out1", D["w_out1"], D_MODEL // UNIT)
        ffn_stage(nc, S, "ffn1", G_FFN1, D["w_gate"][1], D["w_up"][1], D["w_down"][1])
        final_stage(nc, S, D)


_OUTS = [("y_prompt", (1024, 1024), (1, 1024, 1024)), ("y_sample", (64, 1024), (1, 64, 1024)),
         ("p_ckv", (1024, 256), (1, 1, 1024, 256)), ("p_krope", (1024, 32), (1, 1, 1024, 32)),
         ("p_C", (4, 128, 128), (1, 1, 4, 128, 128)), ("p_n", (4, 128, 1), (1, 1, 4, 128)), ("p_m", (1, 4), (1, 1, 4)),
         ("p_bk", (512, 1024), (1, 1, 512, 16, 64)), ("p_bv", (512, 1024), (1, 1, 512, 16, 64)),
         ("s_ckv", (64, 256), (1, 1, 64, 256)), ("s_krope", (64, 32), (1, 1, 64, 32)),
         ("s_C", (4, 128, 128), (1, 1, 4, 128, 128)), ("s_n", (4, 128, 1), (1, 1, 4, 128)), ("s_m", (1, 4), (1, 1, 4)),
         ("s_bk", (512, 1024), (1, 1, 512, 16, 64)), ("s_bv", (512, 1024), (1, 1, 512, 16, 64))]
_SCRATCH = [("z", (3072, T)), ("gates", (2, A_HEADS, NT * P)), ("u", (A_HEADS, NT * P)), ("w", (A_HEADS, NT * P)),
            ("bias", (C_HEADS, P, 2 * P))]


def _rope_tables():
    half = B_ROPE // 2
    inv = np.float32(10000.0) ** (-np.arange(half, dtype=np.float32) / np.float32(half))
    pos = np.concatenate([np.arange(SEQ), PAST_LEN + np.arange(DEC_SEQ)]).astype(np.float32)
    ang = (pos[:, None] * inv[None, :]).astype(np.float32)
    cos, sin = np.cos(ang).T, np.sin(ang).T
    return np.stack([np.concatenate([cos, cos]), np.concatenate([-sin, sin])], 1).astype(np.float32)


def _layout(i):
    def cols(g):
        return g.reshape(-1, P).T

    w = i["w_in_ab"][0]
    a = 4 * A_HEADS * A_DIM
    b = a + 2 * A_HEADS
    kr = w[:, b + Q_RANK + KV_RANK:]
    pad = np.zeros((D_MODEL, 32 - A_HEADS), np.float32)
    w_in = np.concatenate([w[:, :a], w[:, b:], kr[:, 16:], kr[:, :16], w[:, a:a + A_HEADS], pad,
                           w[:, a + A_HEADS:b], pad], 1)
    uq = i["mla_w_uq"][0].reshape(Q_RANK, B_HEADS, B_NOPE + B_ROPE)
    rot = uq[:, :, B_NOPE:]
    rel = i["rel_bias_c"][0]
    gains = [i["norm_mix"][0], i["norm_ffn"][0], i["norm_mix"][1], i["norm_ffn"][1],
             i["mla_q_norm"][0], i["mla_kv_norm"][0], i["mlstm_hnorm"][0]]
    table = _rope_tables()
    halves = np.concatenate([np.repeat([1, 0, 0, 1], CHUNK), np.full(CHUNK, NEG)]).astype(np.float32)
    return {
        "x_prompt": i["x_prompt"][0], "x_sample": i["x_sample"][0], "w_in": w_in,
        "gains": np.concatenate([cols(g) for g in gains], 1),
        "g_final": i["norm_final"].reshape(1, -1),
        "b_gates": i["b_gates"].reshape(2, A_HEADS).T,
        "s_C0": i["state_mlstm_C"][0, 0], "s_n0": i["state_mlstm_n"].reshape(A_HEADS, A_DIM, 1),
        "s_m0": i["state_mlstm_m"].reshape(1, A_HEADS),
        "c_ckv": i["cache_mla_ckv"][0, 0], "c_krope": i["cache_mla_krope"][0, 0],
        "w_qn": uq[:, :, :B_NOPE].reshape(Q_RANK, -1), "w_qr": rot.reshape(Q_RANK, -1),
        "w_qs": np.concatenate([rot[:, :, 16:], rot[:, :, :16]], 2).reshape(Q_RANK, -1),
        "w_uk": i["mla_w_uk"][0].reshape(KV_RANK, -1), "w_uv": i["mla_w_uv"][0].reshape(KV_RANK, -1),
        "w_out0": i["w_out_ab"][0], "w_qkv": i["w_qkv_c"][0], "w_out1": i["w_out_c"][0],
        "c_k": i["cache_band_k"].reshape(PAST_LEN, -1), "c_v": i["cache_band_v"].reshape(PAST_LEN, -1),
        "rel": np.concatenate([np.repeat(rel[:, 2 * MAX_REL:], P - 1, 1), rel[:, :0:-1]], 1),
        "w_gate": i["w_gate"], "w_up": i["w_up"], "w_down": i["w_down"],
        "rope_k": table, "rope_q": np.concatenate([table, table]) * np.float32(MLA_SCALE), "halves": halves[None],
        "ident": np.eye(P, dtype=np.float32), "ones": np.ones((P, P), np.float32),
        "upper": np.triu(np.ones((P, P), np.float32)), "lower": np.tril(np.full((P, P), NEG, np.float32), -1),
    }


def kernel(**inputs):
    import concourse.bacc as _bacc
    from concourse.bass_utils import run_bass_kernel_spmd as _run

    nc = _bacc.Bacc("TRN2", target_bir_lowering=False, num_devices=1)
    arrays = {"in_" + n: np.ascontiguousarray(v) for n, v in _layout(inputs).items()}
    D = {n[3:]: nc.dram_tensor(n, a.shape, F32, kind="ExternalInput").ap() for n, a in arrays.items()}
    for n, shape, _ in _OUTS:
        D[n] = nc.dram_tensor("out_" + n, shape, F32, kind="ExternalOutput").ap()
    for n, shape in _SCRATCH:
        D[n] = nc.dram_tensor("park_" + n, shape, F32, kind="Internal").ap()
    build(nc, D)
    r = _run(nc, [arrays], core_ids=[0])
    return tuple(r.results[0]["out_" + n].reshape(shape) for n, _, shape in _OUTS)
```

```python
from contextlib import ExitStack

import numpy as np

import concourse.bass as bass
from concourse import mybir

ALU = mybir.AluOpType
ACT = mybir.ActivationFunctionType
AX_X = mybir.AxisListType.X
F32 = mybir.dt.float32
F32R = mybir.dt.float32r

D_MODEL, SEQ, DEC_SEQ, PAST_LEN = 1024, 1024, 64, 512
A_HEADS, A_DIM = 4, 128
B_HEADS, B_NOPE, B_ROPE, B_VDIM = 8, 64, 32, 64
Q_RANK, KV_RANK = 384, 256
CHUNK = 64
C_HEADS, C_DIM, MAX_REL = 16, 64, 128
D_FF = ((8 * D_MODEL + 767) // 768) * 256
MLA_SCALE = (B_NOPE + B_ROPE) ** -0.5
C_SCALE = C_DIM ** -0.5
EPS = 1e-6
NEG = -1e30

P = 128
KT = D_MODEL // P
T = SEQ + DEC_SEQ
NT = (T + P - 1) // P
CHUNKS = [(0, 384), (384, 384), (768, T - 768)]
NC = len(CHUNKS)
UNIT = 2 * P
KEYS = T + PAST_LEN

Z_Q, Z_K, Z_V, Z_O = 0, 512, 1024, 1536
Z_CQ, Z_CKV, Z_MISC = 2048, 2432, 2688
Z_KR, Z_KRS, Z_I, Z_F = Z_MISC, Z_MISC + 32, Z_MISC + 64, Z_MISC + 96
Z_ROWS = Z_MISC + P
G_MIX0, G_FFN0, G_MIX1, G_FFN1, G_Q, G_KV, G_H = 0, 8, 16, 24, 32, 35, 37
G_COLS = 41


def tile_width(t):
    return min(P, T - t * P)


class Stage:

    def __init__(self, nc, name):
        self.nc, self.name, self.ctx, self.sems = nc, name, ExitStack(), []

    def __enter__(self):
        self.ctx.__enter__()
        return self

    def __exit__(self, *a):
        self.ctx.__exit__(*a)
        if self.sems and a[0] is None:
            self.nc.clear_and_free_semaphores(self.sems)
            self.nc.all_engine_barrier()

    def sb(self, name, shape, dt=F32):
        return self.ctx.enter_context(self.nc.sbuf_tensor(f"{self.name}_{name}", shape, dt))

    def ps(self, name, shape, dt=F32):
        return self.ctx.enter_context(self.nc.psum_tensor(f"{self.name}_{name}", shape, dt))

    def sem(self, name):
        self.sems.append(self.nc.alloc_semaphore(name=f"{self.name}_{name}"))
        return self.sems[-1]

    def block(self):
        return self.ctx.enter_context(self.nc.Block())


def load_stage(nc, S, D):
    with Stage(nc, "load") as st:
        xin = st.sb("xin", [P, 3, D_MODEL])
        banks = st.ps("banks", [P, 8, 512])
        ident_in, const_in = st.sem("ident_in"), st.sem("const_in")
        row_in = [st.sem(f"row_in{i}") for i in range(3)]
        turned, act_out, dve_out = st.sem("turned"), st.sem("act_out"), st.sem("dve_out")
        block = st.block()

        @block.sync
        def _(sp):
            sp.dma_start(S["ident"][:], D["ident"]).then_inc(ident_in, 16)
            sp.dma_start(S["ones"][:], D["ones"]).then_inc(const_in, 16)
            sp.dma_start(S["gains"][:], D["gains"]).then_inc(const_in, 16)
            sp.dma_start(S["halves"][:], D["halves"]).then_inc(const_in, 16)
            for t in range(NT):
                w = tile_width(t)
                if t >= 3:
                    sp.wait_ge(turned, 2 * (t - 2))
                src = D["x_prompt"][t * P:t * P + w, :] if t < SEQ // P else D["x_sample"]
                sp.dma_start(xin[0:w, t % 3, :], src).then_inc(row_in[t % 3], 16)
            rel = D["rel"]
            width = rel.shape[1]
            rows = bass.AP(rel.tensor, P - 1, [[width, C_HEADS], [-1, P], [1, 2 * P]])
            sp.dma_start(D["bias"], rows).then_inc(const_in, 16)
            sp.wait_ge(const_in, 64)

        @block.tensor
        def _(pe):
            pe.wait_ge(ident_in, 16)
            for t in range(NT):
                w = tile_width(t)
                pe.wait_ge(row_in[t % 3], 16 * (t // 3 + 1))
                for j in range(2):
                    if t >= 4:
                        pe.wait_ge(dve_out if j else act_out, t - 3)
                    for q in range(4):
                        k = 4 * j + q
                        last = nc.tensor.transpose(banks[:, (2 * t + j) % 8, q * P:q * P + w],
                                                   xin[0:w, t % 3, k * P:(k + 1) * P], S["ident"][0:w, 0:w])
                    last.then_inc(turned, 1)

        def empty(t, j):
            w = tile_width(t)
            src = banks[:, (2 * t + j) % 8, :].rearrange("p (q n) -> p q n", q=4)[:, :, 0:w]
            return S["xT"][:, 4 * j:4 * j + 4, t * P:t * P + w], src

        @block.scalar
        def _(act):
            for t in range(NT):
                act.wait_ge(turned, 2 * t + 1)
                nc.scalar.activation(*empty(t, 0), ACT.Copy).then_inc(act_out, 1)

        @block.vector
        def _(dve):
            for t in range(NT):
                dve.wait_ge(turned, 2 * t + 2)
                nc.vector.tensor_copy(*empty(t, 1)).then_inc(dve_out, 1)


class Norm:

    HALF = KT // 2

    def __init__(self, nc, S, st, g0, sq, hf, var, means, roots):
        self.nc, self.S, self.g0 = nc, S, g0
        self.sq, self.hf, self.var, self.means, self.roots = sq, hf, var, means, roots
        self.squared, self.summed, self.eps_added, self.recip, self.rooted, self.scaled, self.hi_done, self.lo_done = (
            st.sem("n_" + n) for n in ("squared", "summed", "eps_added", "recip", "rooted", "scaled", "hi", "lo"))

    def square(self, act, c):
        c0, w = CHUNKS[c]
        for j in range(2):
            n = 2 * c + j
            if n >= 2:
                act.wait_ge(self.summed, n - 1)
            src = self.S["xT"][:, j * self.HALF:(j + 1) * self.HALF, c0:c0 + w]
            self.nc.scalar.activation(self.sq[j][:, :, 0:w], src, ACT.Square).then_inc(self.squared, 1)

    def root(self, act, c):
        w = CHUNKS[c][1]
        act.wait_ge(self.recip, c + 1)
        n = len(self.roots)
        if c >= n:
            act.wait_ge(self.scaled, KT * (c - n + 1))
        self.nc.scalar.activation(self.roots[c % n][:, 0:w], self.var[:, 0:w], ACT.Sqrt).then_inc(self.rooted, 1)

    def high(self, act, c):
        c0, w = CHUNKS[c]
        for k in range(KT):
            act.wait_ge(self.scaled, c * KT + k + 1)
            self.nc.scalar.activation(self.S["hhi"][:, k, c0:c0 + w], self.hf[k % 4][:, 0:w], ACT.Copy)\
                .then_inc(self.hi_done, 1)

    def total(self, pe, c):
        w = CHUNKS[c][1]
        n = len(self.means)
        if c >= n:
            pe.wait_ge(self.eps_added, c - n + 1)
        for k in range(KT):
            if k % self.HALF == 0:
                pe.wait_ge(self.squared, 2 * c + k // self.HALF + 1)
            last = self.nc.tensor.matmul(self.means[c % len(self.means)][:, 0:w], self.S["ones"][:],
                                         self.sq[k // self.HALF][:, k % self.HALF, 0:w], start=(k == 0), stop=(k == KT - 1))
            if k % self.HALF == self.HALF - 1:
                last.then_inc(self.summed, 1)

    def reciprocal(self, dve, c):
        w = CHUNKS[c][1]
        dve.wait_ge(self.summed, 2 * c + 2)
        if c:
            dve.wait_ge(self.rooted, c)
        self.nc.vector.tensor_scalar(self.var[:, 0:w], self.means[c % len(self.means)][:, 0:w], 1.0 / D_MODEL, EPS, ALU.mult,
                                     ALU.add).then_inc(self.eps_added, 1)
        dve.wait_ge(self.eps_added, c + 1)
        self.nc.vector.reciprocal(self.var[:, 0:w], self.var[:, 0:w]).then_inc(self.recip, 1)

    def scale(self, dve, c):
        c0, w = CHUNKS[c]
        dve.wait_ge(self.rooted, c + 1)
        for k in range(KT):
            n = c * KT + k
            if n >= 4:
                dve.wait_ge(self.lo_done, n - 3)
            self.nc.vector.scalar_tensor_tensor(
                out=self.hf[k % 4][:, 0:w], in0=self.S["xT"][:, k, c0:c0 + w],
                scalar=self.S["gains"][:, self.g0 + k:self.g0 + k + 1], in1=self.roots[c % len(self.roots)][:, 0:w],
                op0=ALU.mult, op1=ALU.mult).then_inc(self.scaled, 1)

    def low(self, pool, c):
        c0, w = CHUNKS[c]
        for k in range(KT):
            pool.wait_ge(self.hi_done, c * KT + k + 1)
            self.nc.gpsimd.tensor_tensor(self.S["hlo"][:, k, c0:c0 + w], self.hf[k % 4][:, 0:w],
                                         self.S["hhi"][:, k, c0:c0 + w], ALU.subtract).then_inc(self.lo_done, 1)

    def on_vector(self, dve):
        for c in range(NC):
            self.reciprocal(dve, c)
            if c:
                self.scale(dve, c - 1)
        self.scale(dve, NC - 1)

    def ready(self, pe, c):
        pe.wait_ge(self.lo_done, (c + 1) * KT)


def three_pass(nc, out, whi, wlo, hhi, hlo, kts, c0, w):
    for k in range(kts):
        nc.tensor.matmul(out, whi[:, k, :], hhi[:, k, c0:c0 + w], start=(k == 0), stop=False)
        nc.tensor.matmul(out, whi[:, k, :], hlo[:, k, c0:c0 + w], start=False, stop=False)
        last = nc.tensor.matmul(out, wlo[:, k, :], hhi[:, k, c0:c0 + w], start=False, stop=(k == kts - 1))
    return last


def project_stage(nc, S, name, weights, units, out_rows=None, g0=None):
    xT, hhi, hlo = S["xT"], S["hhi"], S["hlo"]
    w_view = weights.rearrange("(k p) n -> p k n", p=P)
    with Stage(nc, name) as st:
        stage = st.sb("stage", [P, KT, UNIT])
        whi = st.sb("whi", [P, 2, KT, P], F32R)
        wlo = st.sb("wlo", [P, 2, KT, P], F32R)
        rows = st.sb("rows", [P, 2, T]) if out_rows is not None else None
        banks = st.ps("banks", [P, 2 * NC, 512])
        w_in, hi_done, lo_done = st.sem("w_in"), st.sem("hi_done"), st.sem("lo_done")
        summed = st.sem("summed")
        emptied = st.sem("emptied")
        stored = [st.sem(f"stored{h}") for h in range(2)]
        if g0 is None:
            norm = None
        else:
            W = CHUNKS[0][1]
            norm = Norm(nc, S, st, g0, [st.sb(f"sq{j}", [P, KT // 2, W]) for j in range(2)],
                        [st.sb(f"hf{j}", [P, W]) for j in range(4)], st.sb("var", [P, W]),
                        [st.ps("means", [P, 512])], [st.ps("roots", [P, 512])])
        block = st.block()

        @block.sync
        def _(sp):
            def load(u):
                sp.dma_start(stage[:], w_view[:, :, bass.ds(u * UNIT, UNIT)]).then_inc(w_in, 16)

            def store(u):
                for h in range(2):
                    sp.wait_ge(emptied, u * 2 * NC + (h + 1) * NC + 2 * NC)
                    sp.dma_start(out_rows[bass.ds(u * UNIT + h * P, P), :], rows[:, h, :]).then_inc(stored[h], 16)

            load(0)
            if out_rows is not None:
                for h in range(2):
                    sp.sem_inc(stored[h], 16)
            with sp.Fori(0, units - 1) as u:
                sp.wait_ge(lo_done, 2 * u + 2)
                load(u + 1)
                if out_rows is not None:
                    store(u)
            if out_rows is not None:
                store(units - 1)
                for h in range(2):
                    sp.wait_ge(stored[h], 16 * (units + 1))

        @block.scalar
        def _(act):
            def split(u):
                act.wait_ge(w_in, 16 * u + 16)
                for h in range(2):
                    act.wait_ge(summed, 2 * NC * u + (h + 1) * NC)
                    nc.scalar.activation(whi[:, h], stage[:, :, h * P:(h + 1) * P], ACT.Copy).then_inc(hi_done, 1)

            if norm:
                norm.square(act, 0)
            split(0)
            if norm:
                norm.square(act, 1)
                norm.root(act, 0)
                norm.square(act, 2)
                norm.high(act, 0)
                norm.root(act, 1)
                norm.high(act, 1)
                norm.root(act, 2)
                norm.high(act, 2)
            with act.Fori(1, units) as u:
                split(u)

        @block.gpsimd
        def _(pool):
            def split(u):
                for h in range(2):
                    pool.wait_ge(hi_done, 2 * u + h + 1)
                    nc.gpsimd.tensor_tensor(wlo[:, h], stage[:, :, h * P:(h + 1) * P], whi[:, h],
                                            ALU.subtract).then_inc(lo_done, 1)

            split(0)
            if norm:
                for c in range(NC):
                    norm.low(pool, c)
            with pool.Fori(1, units) as u:
                split(u)

        @block.tensor
        def _(pe):
            pe.sem_inc(summed, 2 * NC)

            def products(u, first=False):
                for h in range(2):
                    pe.wait_ge(lo_done, 2 * u + h + 1)
                    for c, (c0, w) in enumerate(CHUNKS):
                        b = h * NC + c
                        if first and h == 0:
                            norm.ready(pe, c)
                        pe.wait_ge(emptied, 2 * NC * u + b + 1)
                        last = three_pass(nc, banks[:, b, 0:w], whi[:, h], wlo[:, h], hhi, hlo, KT, c0, w)
                        last.then_inc(summed, 1)

            if norm:
                for c in range(NC):
                    norm.total(pe, c)
                products(0, first=True)
            with pe.Fori(1 if norm else 0, units) as u:
                products(u)

        @block.vector
        def _(dve):
            dve.sem_inc(emptied, 2 * NC)
            if norm:
                norm.on_vector(dve)
            with dve.Fori(0, units) as u:
                for h in range(2):
                    if out_rows is not None:
                        dve.wait_ge(stored[h], 16 * u + 16)
                    for c, (c0, w) in enumerate(CHUNKS):
                        b = h * NC + c
                        dve.wait_ge(summed, 2 * NC * u + b + 1 + 2 * NC)
                        if out_rows is not None:
                            nc.vector.tensor_copy(rows[:, h, c0:c0 + w], banks[:, b, 0:w]).then_inc(emptied, 1)
                        else:
                            x = xT[:, bass.ds(2 * u + h, 1), c0:c0 + w].rearrange("p a n -> p (a n)")
                            nc.vector.tensor_tensor(x, x, banks[:, b, 0:w], ALU.add).then_inc(emptied, 1)




R = A_HEADS * NT


def gate_stage(nc, S, D):
    PROMPT = SEQ // P
    with Stage(nc, "gate") as st:
        gi = st.sb("gi", [A_HEADS, NT * P])
        gf = st.sb("gf", [A_HEADS, NT * P])
        e1 = st.sb("e1", [A_HEADS, T])
        bias = st.sb("bias", [A_HEADS, 2])
        ig = st.sb("ig", [R, P])
        lf = st.sb("lf", [R, P])
        lfT = st.sb("lfT", [P, R])
        b = st.sb("b", [R, P])
        a = st.sb("a", [R, P])
        amax = st.sb("amax", [R, P])
        rows = st.sb("rows", [1, 4, A_HEADS, NT])
        logs = st.sb("logs", [1, 2, R])
        m_in = st.sb("m_in", [R, 1])
        u = st.sb("u", [R, P])
        w = st.sb("w", [R, P])
        nm = st.sb("nm", [R, P])
        wk = st.sb("wk", [P, R])
        m0 = st.sb("m0", [1, A_HEADS])
        m_out = st.sb("m_out", [1, 2, A_HEADS])
        ps = st.ps("ps", [P, 8, 512])
        z_in, dve, act, pe = st.sem("z_in"), st.sem("dve"), st.sem("act"), st.sem("pe")
        parked, back, out, ahead = st.sem("parked"), st.sem("back"), st.sem("out"), st.sem("ahead")
        block = st.block()
        r_b, r_a, r_min, r_mout = (rows[:, i] for i in range(4))
        flat = lambda x: x.rearrange("p h c -> p (h c)")

        done = {}

        @block.vector
        def _(eng):
            n = [0]

            def step(ins):
                ins.then_inc(dve, 1)
                n[0] += 1
                eng.wait_ge(dve, n[0])

            v = nc.vector
            step(v.memset(gi[:, T:], NEG))
            step(v.memset(gf[:, T:], 0.0))
            step(v.memset(r_min[:, :, 0], 0.0))
            eng.wait_ge(z_in, 96)
            step(v.tensor_scalar(gi[:, 0:T], gi[:, 0:T], bias[:, 0:1], None, ALU.add))
            step(v.tensor_scalar(gf[:, 0:T], gf[:, 0:T], bias[:, 1:2], None, ALU.add))
            step(v.scalar_tensor_tensor(out=e1[:], in0=gf[:, 0:T], scalar=-1.0, in1=gf[:, 0:T], op0=ALU.mult,
                                        op1=ALU.min))
            step(v.tensor_scalar(gf[:, 0:T], gf[:, 0:T], 0.0, None, ALU.min))
            eng.wait_ge(act, 2)
            step(v.tensor_tensor(gf[:, 0:T], gf[:, 0:T], e1[:], ALU.subtract))
            eng.wait_ge(pe, 1)
            step(v.tensor_copy(lfT[:], ps[:, 0, 0:R]))
            eng.wait_ge(pe, 2)
            step(v.tensor_copy(b[:], ps[0:R, 1, 0:P]))
            eng.wait_ge(back, 32)
            step(v.tensor_tensor(a[:], ig[:], b[:], ALU.subtract))
            eng.wait_ge(pe, 3)
            step(v.tensor_copy(S["aT"][:], ps[:, 2, 0:R]))
            step(v.tensor_tensor_scan(amax[:], a[:], a[:], NEG, ALU.max, ALU.max))
            eng.wait_ge(pe, 4)
            step(v.tensor_copy(rows[:, 0:2].rearrange("p i h c -> p (i h c)"), ps[0:1, 3, 0:2 * R]))
            step(v.tensor_copy(r_min[:, :, NT - 1], m0[:]))
            for c in list(range(PROMPT)) + [NT - 1]:
                step(v.tensor_tensor(r_mout[:, :, c], r_min[:, :, c], r_a[:, :, c], ALU.max))
                step(v.tensor_tensor(r_mout[:, :, c], r_mout[:, :, c], r_b[:, :, c], ALU.add))
                if c + 1 < PROMPT:
                    step(v.tensor_copy(r_min[:, :, c + 1], r_mout[:, :, c]))
            step(v.tensor_copy(m_out[:, 0, :], r_mout[:, :, PROMPT - 1]))
            step(v.tensor_copy(m_out[:, 1, :], r_mout[:, :, NT - 1]))
            done["m"] = n[0]
            step(v.tensor_tensor(logs[:, 1, :], flat(r_b), flat(r_mout), ALU.subtract))
            step(v.tensor_tensor(logs[:, 0, :], logs[:, 1, :], flat(r_min), ALU.add))
            done["logs"] = n[0]
            eng.wait_ge(pe, 5)
            step(v.tensor_copy(m_in[:], ps[0:R, 4, 0:1]))
            step(v.tensor_scalar(u[:], amax[:], m_in[:], -1.0, ALU.max, ALU.mult))
            done["u"] = n[0]
            step(v.tensor_tensor(nm[:], u[:], b[:], ALU.subtract))
            done["nm"] = n[0]
            eng.wait_ge(pe, 7)
            step(v.tensor_tensor(wk[:], S["aT"][:], ps[:, 7, 0:R], ALU.add))
            done["wk"] = n[0]

        @block.sync
        def _(sp):
            sp.dma_start(gi[:, 0:T], D["z"][Z_I:Z_I + A_HEADS, :]).then_inc(z_in, 16)
            sp.dma_start(gf[:, 0:T], D["z"][Z_F:Z_F + A_HEADS, :]).then_inc(z_in, 16)
            sp.dma_start(bias[:], D["b_gates"]).then_inc(z_in, 16)
            sp.dma_start(S["upper"][:], D["upper"]).then_inc(z_in, 16)
            sp.dma_start(S["lower"][:], D["lower"]).then_inc(z_in, 16)
            sp.dma_start(m0[:], D["s_m0"]).then_inc(z_in, 16)
            sp.wait_ge(dve, 8)
            sp.dma_start(D["gates"][0], gi[:]).then_inc(parked, 16)
            sp.dma_start(D["gates"][1], gf[:]).then_inc(parked, 16)
            sp.wait_ge(parked, 32)
            sp.dma_start(ig[:], D["gates"][0].rearrange("h (c t) -> (h c) t", t=P)).then_inc(back, 16)
            sp.dma_start(lf[:], D["gates"][1].rearrange("h (c t) -> (h c) t", t=P)).then_inc(back, 16)
            for e in range(2):
                for name, row in (("k", Z_K), ("v", Z_V), ("q", Z_Q), ("o", Z_O)):
                    sp.dma_start(S[name][:, e, :], D["z"][row + e * P:row + (e + 1) * P, :]).then_inc(ahead, 16)
            sp.wait_ge(dve, done["m"])
            sp.dma_start(D["p_m"], m_out[:, 0, :]).then_inc(out, 16)
            sp.dma_start(D["s_m"], m_out[:, 1, :]).then_inc(out, 16)
            sp.wait_ge(dve, done["u"])
            sp.dma_start(D["u"].rearrange("h (c t) -> (h c) t", t=P), u[:]).then_inc(out, 16)
            sp.wait_ge(act, 4)
            sp.dma_start(D["w"].rearrange("h (c t) -> (h c) t", t=P), w[:]).then_inc(out, 16)
            sp.wait_ge(out, 64)
            sp.wait_ge(ahead, 128)

        @block.scalar
        def _(eng):
            eng.wait_ge(dve, 6)
            nc.scalar.activation(e1[:], e1[:], ACT.Exp).then_inc(act, 1)
            eng.wait_ge(act, 1)
            nc.scalar.activation(e1[:], e1[:], ACT.Ln, bias=1.0).then_inc(act, 1)
            eng.wait_ge(pe, 6)
            nc.scalar.activation(S["decay"][:], ps[:, 6, 0:R], ACT.Exp).then_inc(act, 1)
            eng.wait_ge(dve, done["u"])
            nc.scalar.activation(w[:], u[:], ACT.Exp, bias=m_in[:]).then_inc(act, 1)
            eng.wait_ge(dve, done["wk"])
            nc.scalar.activation(S["wk"][:], wk[:], ACT.Exp).then_inc(act, 1)
            eng.wait_ge(pe, 8)
            nc.scalar.activation(S["enm"][:], ps[:, 0, 0:R], ACT.Exp).then_inc(act, 1)

        @block.tensor
        def _(eng):
            eng.wait_ge(back, 32)
            nc.tensor.transpose(ps[:, 0, 0:R], lf[:], S["ident"][0:R, 0:R]).then_inc(pe, 1)
            eng.wait_ge(dve, 9)
            nc.tensor.matmul(ps[0:R, 1, 0:P], lfT[:], S["upper"][:], start=True, stop=True).then_inc(pe, 1)
            eng.wait_ge(dve, 11)
            nc.tensor.transpose(ps[:, 2, 0:R], a[:], S["ident"][0:R, 0:R]).then_inc(pe, 1)
            eng.wait_ge(dve, 13)
            nc.tensor.transpose(ps[0:1, 3, 0:R], b[:, P - 1:P], S["ident"][0:R, 0:R])
            nc.tensor.transpose(ps[0:1, 3, R:2 * R], amax[:, P - 1:P], S["ident"][0:R, 0:R]).then_inc(pe, 1)
            eng.wait_ge(dve, done["m"])
            nc.tensor.matmul(ps[0:R, 4, 0:1], flat(r_min), S["ones"][0:1, 0:1], start=True, stop=True).then_inc(pe, 1)
            eng.wait_ge(dve, done["logs"])
            nc.tensor.matmul(ps[:, 6, 0:R], S["ones"][0:1, :], logs[:, 0, :], start=True, stop=True).then_inc(pe, 1)
            nc.tensor.matmul(ps[:, 7, 0:R], S["ones"][0:1, :], logs[:, 1, :], start=True, stop=True).then_inc(pe, 1)
            eng.wait_ge(dve, done["nm"])
            nc.tensor.transpose(ps[:, 0, 0:R], nm[:], S["ident"][0:R, 0:R]).then_inc(pe, 1)


def mlstm_stage(nc, S, D):
    PROMPT = SEQ // P
    N = 2 * NT
    E1 = A_DIM + 1
    hhi, hlo = S["hhi"], S["hlo"]
    with Stage(nc, "mlstm") as st:
        qT, kT, vT, oT = (S[x] for x in "qkvo")
        dm = st.sb("dm", [P, 2, NT, P])
        qw = st.sb("qw", [P, 2, NT * P])
        cols = st.sb("cols", [P, 4, N])
        kw = st.sb("kw", [P, N, A_DIM])
        v1 = st.sb("v1", [P, 2, NT, E1])
        state = st.sb("state", [P, 2, 2, E1])
        sd = st.sb("sd", [P, 2, P])
        h = st.sb("h", [P, N, A_DIM])
        den = st.sb("den", [P, N])
        ssq = st.sb("ssq", [P, N])
        junk = st.sb("junk", [P, 2, A_DIM])
        gated = st.sb("gated", [P, 4, P])
        pS = st.ps("pS", [P, 2, 512])
        pU = st.ps("pU", [P, 2, 512])
        pT = st.ps("pT", [P, 4, 512])
        pN = pT[:, 2:4, :]
        names = ("kv_in", "zin", "uin", "set_up", "dadd", "dexp", "turned", "kw_set", "v_set", "sm", "sdm", "nm", "um",
                 "upd", "dn", "rd", "hs", "sq", "mv", "rt", "hn", "ht", "gt", "hi", "lo", "stored", "ones", "sg", "apart", "cleared")
        s = {x: st.sem(x) for x in names}
        block = st.block()
        TR = 2 * N

        @block.sync
        def _(sp):
            for hp in range(2):
                if hp:
                    sp.wait_ge(s["sdm"], N * hp)
                for e in range(2):
                    src = D["u"][2 * hp + e:2 * hp + e + 1, :].to_broadcast([P, NT * P])
                    sp.dma_start(dm[:, e].rearrange("p c t -> p (c t)"), src).then_inc(s["uin"], 16)
                if hp:
                    sp.wait_ge(s["nm"], N * hp)
                    for e in range(2):
                        for dst, row in ((kT, Z_K), (vT, Z_V)):
                            row += (2 * hp + e) * P
                            sp.dma_start(dst[:, e, :], D["z"][row:row + P, :]).then_inc(s["kv_in"], 16)
                else:
                    sp.sem_inc(s["kv_in"], 16 * 4)
                    sp.sem_inc(s["zin"], 16 * 4)
                for e in range(2):
                    src = D["w"][2 * hp + e:2 * hp + e + 1, :].to_broadcast([P, NT * P])
                    sp.dma_start(qw[:, e], src).then_inc(s["zin"], 16)
                    if hp:
                        row = Z_Q + (2 * hp + e) * P
                        sp.dma_start(qT[:, e, :], D["z"][row:row + P, :]).then_inc(s["zin"], 16)
                if hp:
                    sp.wait_ge(s["stored"], 128 * hp)
                for e in range(2):
                    sp.dma_start(state[:, e, 1, 0:A_DIM], D["s_C0"][2 * hp + e]).then_inc(s["zin"], 16)
                    sp.dma_start(state[:, e, 1, A_DIM:E1], D["s_n0"][2 * hp + e]).then_inc(s["zin"], 16)
                if hp:
                    sp.wait_ge(s["gt"], N * hp)
                    for e in range(2):
                        row = Z_O + (2 * hp + e) * P
                        sp.dma_start(oT[:, e, :], D["z"][row:row + P, :]).then_inc(s["zin"], 16)
                for g, (c_out, n_out) in enumerate((("p_C", "p_n"), ("s_C", "s_n"))):
                    for e in range(2):
                        sp.wait_ge(s["upd"], N * hp + 2 * (PROMPT - 1 + g) + e + 1)
                        sp.dma_start(D[c_out][2 * hp + e], state[:, e, g, 0:A_DIM]).then_inc(s["stored"], 16)
                        sp.dma_start(D[n_out][2 * hp + e], state[:, e, g, A_DIM:E1]).then_inc(s["stored"], 16)
            sp.wait_ge(s["stored"], 128 * 2)

        @block.gpsimd
        def _(pool):
            nc.gpsimd.memset(v1[:], 1.0).then_inc(s["ones"], 1)
            pool.sem_inc(s["lo"], 4)
            with pool.Fori(0, 2) as hp:
                for n in range(N):
                    c, e = n // 2, n % 2
                    w = tile_width(c)
                    pool.wait_ge(s["hi"], N * hp + n + 1)
                    dst = slice(c * P, c * P + w)
                    ht = bass.ds(2 * hp + e, 1)
                    nc.gpsimd.tensor_tensor(hlo[:, ht, dst].rearrange("p a n -> p (a n)"), gated[:, n % 4, 0:w],
                                            hhi[:, ht, dst].rearrange("p a n -> p (a n)"), ALU.subtract)\
                      .then_inc(s["lo"], 1)

        @block.scalar
        def _(act):
            act.wait_ge(s["ones"], 1)
            with act.Fori(0, 2) as hp:
                for n in range(N):
                    c, e = n // 2, n % 2
                    w = tile_width(c)
                    act.wait_ge(s["turned"], TR * hp + 2 * n + 2)
                    nc.scalar.activation(v1[0:w, e, c, 0:A_DIM], pT[0:w, (2 * n + 1) % 4, 0:P], ACT.Copy).then_inc(s["v_set"], 1)
                for e in range(2):
                    act.wait_ge(s["dadd"], 4 * hp + 2 * e + 2)
                    nc.scalar.activation(dm[:, e], dm[:, e], ACT.Exp).then_inc(s["dexp"], 1)
                act.wait_ge(s["zin"], 160 * hp + 160)
                nc.scalar.activation(oT[:], oT[:], ACT.Sigmoid).then_inc(s["sg"], 1)
                for n in range(N):
                    w = tile_width(n // 2)
                    act.wait_ge(s["hs"], N * hp + n + 1)
                    if n >= 2:
                        act.wait_ge(s["sq"], N * hp + n - 1)
                    nc.scalar.activation(junk[0:w, n % 2], h[0:w, n, :], ACT.Square, accum_out=ssq[0:w, n:n + 1])\
                      .then_inc(s["sq"], 1)
                act.wait_ge(s["mv"], 2 * hp + 2)
                nc.scalar.activation(ssq[:], ssq[:], ACT.Sqrt).then_inc(s["rt"], 1)
                for n in range(N):
                    c, e = n // 2, n % 2
                    w = tile_width(c)
                    act.wait_ge(s["gt"], N * hp + n + 1)
                    dst = hhi[:, bass.ds(2 * hp + e, 1), c * P:c * P + w].rearrange("p a n -> p (a n)")
                    nc.scalar.activation(dst, gated[:, n % 4, 0:w], ACT.Copy).then_inc(s["hi"], 1)

        @block.tensor
        def _(pe):
            with pe.Fori(0, 2) as hp:
                pe.wait_ge(s["kv_in"], 64 * hp + 64)
                for n in range(N):
                    c, e = n // 2, n % 2
                    w = tile_width(c)
                    for j, src in enumerate((kT, vT)):
                        m = 2 * n + j
                        if n >= 2:
                            pe.wait_ge(s[("kw_set", "v_set")[j]], N * hp + n - 1)
                        if w < P:
                            pe.sem_inc(s["apart"], 1)
                        nc.tensor.transpose(pT[0:w, m % 4, 0:P], src[:, e, c * P:c * P + w], S["ident"][:])\
                          .then_inc(s["turned"], 1)

                def scores(n):
                    c, e = n // 2, n % 2
                    w = tile_width(c)
                    if n >= 2:
                        pe.wait_ge(s["sdm"], N * hp + n - 1)
                    nc.tensor.matmul(pS[0:w, n % 2, 0:w], kT[:, e, c * P:c * P + w], qT[:, e, c * P:c * P + w],
                                     start=True, stop=True).then_inc(s["sm"], 1)

                pe.wait_ge(s["zin"], 160 * hp + 160)
                scores(0)
                pe.wait_ge(s["kw_set"], N * hp + N)
                pe.wait_ge(s["v_set"], N * hp + N)
                pe.wait_ge(s["set_up"], 2 * hp + 2)
                for n in range(N):
                    c, e = n // 2, n % 2
                    w = tile_width(c)
                    g = int(c == NT - 1)
                    if n + 1 < N:
                        scores(n + 1)
                    if n >= 2:
                        pe.wait_ge(s["upd"], N * hp + n - 1)
                    nc.tensor.matmul(pU[:, n % 2, 0:E1], kw[0:w, n, :], v1[0:w, e, c, :], start=True, stop=True)\
                      .then_inc(s["um"], 1)
                    pe.wait_ge(s["sdm"], N * hp + n + 1)
                    if n >= 2:
                        pe.wait_ge(s["hs"], N * hp + n - 1)
                    nc.tensor.matmul(pN[0:w, n % 2, 0:E1], qw[:, e, c * P:c * P + w], state[:, e, g, :],
                                     start=True, stop=False)
                    nc.tensor.matmul(pN[0:w, n % 2, 0:E1], sd[0:w, n % 2, 0:w], v1[0:w, e, c, :],
                                     start=False, stop=True).then_inc(s["nm"], 1)
                for n in range(N):
                    c, e = n // 2, n % 2
                    w = tile_width(c)
                    pe.wait_ge(s["hn"], N * hp + n + 1)
                    if n >= 4:
                        pe.wait_ge(s["gt"], N * hp + n - 3)
                    if w < P:
                        pe.sem_inc(s["apart"], 1)
                    nc.tensor.transpose(pT[:, n % 4, 0:w], h[0:w, n, :], S["ident"][0:w, 0:w]).then_inc(s["ht"], 1)
                pe.wait_ge(s["gt"], N * hp + N)

        @block.vector
        def _(dve):
            v = nc.vector
            dve.wait_ge(s["ones"], 1)
            v.memset(ssq[:], 1.0).then_inc(s["cleared"], 1)
            with dve.Fori(0, 2) as hp:
                pair = bass.ds(hp * N, N)
                for i, src in enumerate(("aT", "enm", "wk", "decay")):
                    v.tensor_copy(cols[:, i, :], S[src][:, pair]).then_inc(s["rd"], 1)
                dve.wait_ge(s["rd"], (4 + N) * hp + 4)
                for n in range(N):
                    c, e = n // 2, n % 2
                    w = tile_width(c)
                    dve.wait_ge(s["turned"], TR * hp + 2 * n + 1)
                    i = e * NT + c
                    v.tensor_scalar(kw[0:w, n, :], pT[0:w, 2 * n % 4, 0:P], A_DIM ** -0.5, cols[0:w, 2, i:i + 1],
                                    ALU.mult, ALU.mult).then_inc(s["kw_set"], 1)
                dve.wait_ge(s["uin"], 32 * hp + 32)
                mask = S["lower"][:].rearrange("p (a t) -> p a t", a=1).to_broadcast([P, NT, P])
                for e in range(2):
                    a = cols[:, 0, e * NT:(e + 1) * NT].rearrange("p (c a) -> p c a", a=1).to_broadcast([P, NT, P])
                    v.tensor_tensor(dm[:, e], dm[:, e], a, ALU.add).then_inc(s["dadd"], 1)
                    dve.wait_ge(s["dadd"], 4 * hp + 2 * e + 1)
                    v.tensor_tensor(dm[:, e], dm[:, e], mask, ALU.add).then_inc(s["dadd"], 1)
                dve.wait_ge(s["zin"], 160 * hp + 160)
                v.tensor_tensor(qw[:, :, 0:T], qw[:, :, 0:T], qT[:], ALU.mult).then_inc(s["set_up"], 1)
                v.memset(state[:, :, 0, :], 0.0).then_inc(s["set_up"], 1)
                dve.wait_ge(s["set_up"], 2 * hp + 2)
                dve.wait_ge(s["dexp"], 2 * hp + 2)

                def decayed(n):
                    c, e = n // 2, n % 2
                    w = tile_width(c)
                    dve.wait_ge(s["sm"], N * hp + n + 1)
                    if n >= 2:
                        dve.wait_ge(s["nm"], N * hp + n - 1)
                    v.scalar_tensor_tensor(out=sd[0:w, n % 2, 0:w], in0=pS[0:w, n % 2, 0:w], scalar=A_DIM ** -0.5,
                                           in1=dm[0:w, e, c, 0:w], op0=ALU.mult, op1=ALU.mult).then_inc(s["sdm"], 1)

                decayed(0)
                for n in range(N):
                    c, e = n // 2, n % 2
                    w = tile_width(c)
                    g = int(c == NT - 1)
                    i = e * NT + c
                    if n + 1 < N:
                        decayed(n + 1)
                    dve.wait_ge(s["nm"], N * hp + n + 1)
                    dve.wait_ge(s["um"], N * hp + n + 1)
                    if n >= 2:
                        dve.wait_ge(s["upd"], N * hp + n - 1)
                    v.scalar_tensor_tensor(out=state[:, e, g, :], in0=state[:, e, g, :], scalar=cols[:, 3, i:i + 1],
                                           in1=pU[:, n % 2, 0:E1], op0=ALU.mult, op1=ALU.add).then_inc(s["upd"], 1)
                    v.tensor_scalar(den[0:w, n:n + 1], pN[0:w, n % 2, A_DIM:E1], -1.0, cols[0:w, 1, i:i + 1],
                                    ALU.mult, ALU.max).then_inc(s["dn"], 1)
                    dve.wait_ge(s["dn"], 2 * N * hp + 2 * n + 1)
                    v.tensor_tensor(den[0:w, n:n + 1], pN[0:w, n % 2, A_DIM:E1], den[0:w, n:n + 1], ALU.max)\
                     .then_inc(s["dn"], 1)
                    dve.wait_ge(s["dn"], 2 * N * hp + 2 * n + 2)
                    v.reciprocal(den[0:w, n:n + 1], den[0:w, n:n + 1]).then_inc(s["rd"], 1)
                    dve.wait_ge(s["rd"], (4 + N) * hp + 4 + n + 1)
                    v.tensor_scalar(h[0:w, n, :], pN[0:w, n % 2, 0:A_DIM], den[0:w, n:n + 1], None, ALU.mult)\
                     .then_inc(s["hs"], 1)
                dve.wait_ge(s["sq"], N * hp + N)
                v.tensor_scalar(ssq[:], ssq[:], 1.0 / A_DIM, EPS, ALU.mult, ALU.add).then_inc(s["mv"], 1)
                dve.wait_ge(s["mv"], 2 * hp + 1)
                v.reciprocal(ssq[:], ssq[:]).then_inc(s["mv"], 1)
                dve.wait_ge(s["rt"], hp + 1)
                for n in range(N):
                    w = tile_width(n // 2)
                    v.tensor_scalar(h[0:w, n, :], h[0:w, n, :], ssq[0:w, n:n + 1], None, ALU.mult).then_inc(s["hn"], 1)
                dve.wait_ge(s["sg"], hp + 1)
                for n in range(N):
                    c, e = n // 2, n % 2
                    w = tile_width(c)
                    dve.wait_ge(s["ht"], N * hp + n + 1)
                    if n == 0:
                        dve.wait_ge(s["lo"], N * hp + 4)
                    elif n >= 4:
                        dve.wait_ge(s["lo"], N * hp + n + 1)
                    g = bass.ds(2 * hp + G_H + e, 1)
                    v.scalar_tensor_tensor(out=gated[:, n % 4, 0:w], in0=pT[:, n % 4, 0:w], scalar=S["gains"][:, g],
                                           in1=oT[:, e, c * P:c * P + w], op0=ALU.mult, op1=ALU.mult)\
                     .then_inc(s["gt"], 1)


def ffn_stage(nc, S, name, g0, w_gate, w_up, w_down):
    xT, hhi, hlo = S["xT"], S["hhi"], S["hlo"]
    parts = D_FF // UNIT
    F = UNIT // P
    srcs = [w_gate.rearrange("(k p) n -> p k n", p=P), w_up.rearrange("(k p) n -> p k n", p=P),
            w_down.rearrange("(a f p) n -> a p f n", f=F, p=P)]
    W = CHUNKS[0][1]
    with Stage(nc, name) as st:
        stage = [st.sb(f"stage{m}", [P, KT * UNIT]) for m in range(3)]
        whi = [st.sb(f"whi{m}", [P, KT * UNIT], F32R) for m in range(3)]
        wlo = [st.sb(f"wlo{m}", [P, KT * UNIT], F32R) for m in range(3)]
        ahi = st.sb("ahi", [P, F, T], F32R)
        alo = st.sb("alo", [P, F, T], F32R)
        silu = st.sb("silu", [P, F, W])
        act32 = st.sb("act32", [P, F, W])
        banks = st.ps("banks", [P, 8, 512])
        w_in = [st.sem(f"w_in{m}") for m in range(3)]
        w_hi = [st.sem(f"w_hi{m}") for m in range(3)]
        w_lo = [st.sem(f"w_lo{m}") for m in range(3)]
        gate_sum, up_sum, silu_done, product = (st.sem(n) for n in ("gate_sum", "up_sum", "silu_done", "product"))
        a_hi, a_lo = st.sem("a_hi"), st.sem("a_lo")
        out_sum, added = st.sem("out_sum"), st.sem("added")
        sq = [stage[2][:, 0:KT // 2 * W].rearrange("p (k n) -> p k n", n=W), st.sb("sq", [P, KT // 2, W])]
        norm = Norm(nc, S, st, g0, sq, [x[:, f, :] for x in (silu, act32) for f in range(F)], st.sb("var", [P, W]),
                    [banks[:, 4], banks[:, 5]], [banks[:, 6], banks[:, 7]])
        G = NC * F
        O = NC * KT

        block = st.block()

        def cols(m, tiles):
            return tiles[m][:].rearrange("p (k f n) -> p f k n", k=KT, f=F)

        @block.sync
        def _(sp):
            def load(i, m):
                src = srcs[m][:, :, bass.ds(i * UNIT, UNIT)] if m < 2 else \
                    srcs[m][bass.ds(i, 1), :, :, :].rearrange("a p f n -> p (a f) n")
                dst = stage[m][:].rearrange("p (a n) -> p a n", a=KT if m < 2 else F)
                sp.dma_start(dst, src).then_inc(w_in[m], 16)

            for m in range(3):
                if m == 2:
                    sp.wait_ge(norm.summed, 2 * NC)
                load(0, m)
            with sp.Fori(1, parts) as i:
                for m in range(3):
                    sp.wait_ge(w_lo[m], i)
                    load(i, m)

        @block.scalar
        def _(act):
            def split(i, m):
                act.wait_ge(w_in[m], 16 * i + 16)
                if m < 2:
                    act.wait_ge(up_sum, G * i + G)
                else:
                    act.wait_ge(out_sum, O * i + O)
                nc.scalar.activation(whi[m][:], stage[m][:], ACT.Copy).then_inc(w_hi[m], 1)

            def hidden(i):
                for c, (c0, w) in enumerate(CHUNKS):
                    for f in range(F):
                        n = G * i + c * F + f
                        act.wait_ge(gate_sum, n + 1)
                        act.wait_ge(product, n + 1)
                        nc.scalar.activation(silu[:, f, 0:w], banks[:, 2 * f, 0:w], ACT.Silu).then_inc(silu_done, 1)
                    for f in range(F):
                        n = G * i + c * F + f
                        act.wait_ge(product, n + 1 + F)
                        nc.scalar.activation(ahi[:, f, c0:c0 + w], act32[:, f, 0:w], ACT.Copy).then_inc(a_hi, 1)

            norm.square(act, 0)
            split(0, 0)
            norm.square(act, 1)
            split(0, 1)
            norm.root(act, 0)
            norm.square(act, 2)
            norm.high(act, 0)
            norm.root(act, 1)
            norm.high(act, 1)
            norm.root(act, 2)
            norm.high(act, 2)
            act.wait_ge(norm.lo_done, NC * KT)
            with act.Fori(0, parts - 1) as i:
                split(i, 2)
                hidden(i)
                split(i + 1, 0)
                split(i + 1, 1)
            split(parts - 1, 2)
            hidden(parts - 1)

        @block.gpsimd
        def _(pool):
            pool.sem_inc(a_lo, F)

            def split(i, m):
                pool.wait_ge(w_hi[m], i + 1)
                nc.gpsimd.tensor_tensor(wlo[m][:], stage[m][:], whi[m][:], ALU.subtract).then_inc(w_lo[m], 1)

            def hidden(i):
                for c, (c0, w) in enumerate(CHUNKS):
                    for f in range(F):
                        n = G * i + c * F + f
                        pool.wait_ge(a_hi, n + 1)
                        nc.gpsimd.tensor_tensor(alo[:, f, c0:c0 + w], act32[:, f, 0:w], ahi[:, f, c0:c0 + w],
                                                ALU.subtract).then_inc(a_lo, 1)

            split(0, 0)
            split(0, 1)
            for c in range(NC):
                norm.low(pool, c)
            with pool.Fori(0, parts - 1) as i:
                split(i, 2)
                hidden(i)
                split(i + 1, 0)
                split(i + 1, 1)
            split(parts - 1, 2)
            hidden(parts - 1)

        @block.tensor
        def _(pe):
            pe.sem_inc(up_sum, G)
            pe.sem_inc(out_sum, O)

            def part(i, first=False):
                pe.wait_ge(w_lo[0], i + 1)
                pe.wait_ge(w_lo[1], i + 1)
                for c, (c0, w) in enumerate(CHUNKS):
                    if first:
                        norm.ready(pe, c)
                    for f in range(F):
                        pe.wait_ge(product, G * i + c * F + f + 1)
                        for m, done in ((0, gate_sum), (1, up_sum)):
                            three_pass(nc, banks[:, 2 * f + m, 0:w], cols(m, whi)[:, f], cols(m, wlo)[:, f],
                                       hhi, hlo, KT, c0, w).then_inc(done, 1)
                pe.wait_ge(w_lo[2], i + 1)
                down = [t[2][:].rearrange("p (f k n) -> p k f n", f=F, k=KT) for t in (whi, wlo)]
                for c, (c0, w) in enumerate(CHUNKS):
                    pe.wait_ge(a_lo, G * i + (c + 2) * F)
                    for k in range(KT):
                        pe.wait_ge(added, O * i + c * KT + k + 1)
                        three_pass(nc, banks[:, 4 + k % 4, 0:w], down[0][:, k], down[1][:, k],
                                   ahi, alo, F, c0, w).then_inc(out_sum, 1)

            for c in range(NC):
                norm.total(pe, c)
            part(0, first=True)
            with pe.Fori(1, parts) as i:
                part(i)

        @block.vector
        def _(dve):
            dve.sem_inc(product, F)
            norm.on_vector(dve)
            dve.sem_inc(added, 4)
            dve.wait_ge(norm.lo_done, NC * KT)
            with dve.Fori(0, parts) as i:
                for c, (c0, w) in enumerate(CHUNKS):
                    for f in range(F):
                        n = G * i + c * F + f
                        dve.wait_ge(silu_done, n + 1)
                        dve.wait_ge(up_sum, n + 1 + G)
                        dve.wait_ge(a_lo, n + 1)
                        nc.vector.tensor_tensor(act32[:, f, 0:w], silu[:, f, 0:w], banks[:, 2 * f + 1, 0:w],
                                                ALU.mult).then_inc(product, 1)
                for c, (c0, w) in enumerate(CHUNKS):
                    for k in range(KT):
                        dve.wait_ge(out_sum, O * i + c * KT + k + 1 + O)
                        x = xT[:, k, c0:c0 + w]
                        nc.vector.tensor_tensor(x, x, banks[:, 4 + k % 4, 0:w], ALU.add).then_inc(added, 1)


def final_stage(nc, S, D):
    xT = S["xT"]
    with Stage(nc, "final") as st:
        gain = st.sb("gain", [P, D_MODEL])
        sq = st.sb("sq", [P, 2, D_MODEL])
        var = st.sb("var", [P, NT])
        out = st.sb("out", [P, 3, D_MODEL])
        banks = st.ps("banks", [P, 3, 2, 512])
        gain_in, turned, squared, eps_added, recip, rooted, scaled = (
            st.sem(x) for x in ("gain_in", "turned", "squared", "eps_added", "recip", "rooted", "scaled"))
        stored = [st.sem(f"stored{i}") for i in range(3)]
        block = st.block()

        def rows_of(t):
            return banks[0:tile_width(t), t % 3].rearrange("p b n -> p (b n)")

        @block.tensor
        def _(pe):
            for t in range(NT):
                w = tile_width(t)
                if t >= 3:
                    pe.wait_ge(scaled, t - 2)
                for k in range(KT):
                    last = nc.tensor.transpose(banks[0:w, t % 3, k // 4, k % 4 * P:(k % 4 + 1) * P],
                                               xT[:, k, t * P:t * P + w], S["ident"][:])
                last.then_inc(turned, 1)

        @block.scalar
        def _(act):
            for t in range(NT + 1):
                if t < NT:
                    w = tile_width(t)
                    act.wait_ge(turned, t + 1)
                    if t >= 2:
                        act.wait_ge(squared, t - 1)
                    nc.scalar.activation(sq[0:w, t % 2, :], rows_of(t), ACT.Square, accum_out=var[0:w, t:t + 1])\
                        .then_inc(squared, 1)
                if t:
                    w = tile_width(t - 1)
                    act.wait_ge(recip, t)
                    nc.scalar.activation(var[0:w, t - 1:t], var[0:w, t - 1:t], ACT.Sqrt).then_inc(rooted, 1)

        @block.vector
        def _(dve):
            v = nc.vector
            dve.wait_ge(gain_in, 16)

            def reciprocal(t):
                w = tile_width(t)
                dve.wait_ge(squared, t + 1)
                v.tensor_scalar(var[0:w, t:t + 1], var[0:w, t:t + 1], 1.0 / D_MODEL, EPS, ALU.mult, ALU.add)\
                    .then_inc(eps_added, 1)
                dve.wait_ge(eps_added, t + 1)
                v.reciprocal(var[0:w, t:t + 1], var[0:w, t:t + 1]).then_inc(recip, 1)

            reciprocal(0)
            for t in range(NT):
                w = tile_width(t)
                if t + 1 < NT:
                    reciprocal(t + 1)
                dve.wait_ge(rooted, t + 1)
                if t >= 3:
                    dve.wait_ge(stored[t % 3], 16 * (t // 3))
                v.scalar_tensor_tensor(out=out[0:w, t % 3, :], in0=rows_of(t), scalar=var[0:w, t:t + 1],
                                       in1=gain[0:w, :], op0=ALU.mult, op1=ALU.mult).then_inc(scaled, 1)

        @block.sync
        def _(sp):
            sp.dma_start(gain[:], D["g_final"].to_broadcast([P, D_MODEL])).then_inc(gain_in, 16)
            for t in range(NT):
                w = tile_width(t)
                sp.wait_ge(scaled, t + 1)
                dst = D["y_prompt"][t * P:t * P + w, :] if t < SEQ // P else D["y_sample"]
                sp.dma_start(dst, out[0:w, t % 3, :]).then_inc(stored[t % 3], 16)
            for i in range(3):
                sp.wait_ge(stored[i], 16 * ((NT - i + 2) // 3))


def latent_stage(nc, S, D):
    RQ, RK = Q_RANK // P, KV_RANK // P
    CT = PAST_LEN // P
    cqT, ckvT, kr = S["cqT"], S["ckvT"], S["kr"]
    lo, hi = B_NOPE, B_NOPE + B_ROPE
    with Stage(nc, "latent") as st:
        sq = st.sb("sq", [P, RQ, T])
        var = st.sb("var", [P, 2, T])
        krs = st.sb("krs", [P, T])
        cs = st.sb("cs", [P, 2, T])
        cache = st.sb("cache", [P, CT, KV_RANK])
        rcache = st.sb("rcache", [P, CT, B_ROPE])
        rows = st.sb("rows", [P, NT, KV_RANK])
        rrows = st.sb("rrows", [P, NT, B_ROPE])
        mean = st.ps("mean", [P, 2, NC, 512])
        turn = st.ps("turn", [P, 2, 512])
        z_in, c_in = st.sem("z_in"), st.sem("c_in")
        squared, summed, var_done, rooted, normed = (st.sem(x) for x in ("squared", "summed", "var_done", "rooted", "normed"))
        dve_step, turned, copied, rows_kept, out, krope = (st.sem(x) for x in ("dve_step", "turned", "copied", "rows_kept", "out", "krope"))
        block = st.block()
        lat = [(ckvT, RK, G_KV, KV_RANK), (cqT, RQ, G_Q, Q_RANK)]

        @block.sync
        def _(sp):
            sp.dma_start(cqT[:], D["z"][Z_CQ:Z_CKV, :].rearrange("(k p) t -> p k t", p=P)).then_inc(z_in, 16)
            sp.dma_start(ckvT[:, :, 0:T], D["z"][Z_CKV:Z_MISC, :].rearrange("(k p) t -> p k t", p=P)).then_inc(z_in, 16)
            sp.dma_start(kr[lo:hi, 0:T], D["z"][Z_KR:Z_KR + B_ROPE, :]).then_inc(c_in, 16)
            sp.dma_start(krs[lo:hi, :], D["z"][Z_KRS:Z_KRS + B_ROPE, :]).then_inc(c_in, 16)
            sp.dma_start(cs[lo:hi], D["rope_k"]).then_inc(c_in, 16)
            sp.dma_start(cache[:], D["c_ckv"].rearrange("(c p) r -> p c r", p=P)).then_inc(c_in, 16)
            sp.dma_start(rcache[:], D["c_krope"].rearrange("(c p) r -> p c r", p=P)).then_inc(c_in, 16)
            sp.wait_ge(rows_kept, 2 * NT)
            for dst, src in (("ckv", rows), ("krope", rrows)):
                sp.dma_start(D["p_" + dst].rearrange("(c p) r -> p c r", p=P), src[:, 0:NT - 1, :]).then_inc(out, 16)
                sp.dma_start(D["s_" + dst], src[0:DEC_SEQ, NT - 1, :]).then_inc(out, 16)
            sp.wait_ge(out, 64)

        @block.scalar
        def _(act):
            for i, (x, kts, _, _) in enumerate(lat):
                act.wait_ge(z_in, 32)
                if i:
                    act.wait_ge(summed, NC)
                nc.scalar.activation(sq[:, 0:kts, :], x[:, :, 0:T], ACT.Square).then_inc(squared, 1)
            for i in range(2):
                act.wait_ge(var_done, 2 * NC * (i + 1))
                nc.scalar.activation(var[:, i], var[:, i], ACT.Sqrt).then_inc(rooted, 1)
            m = 2 * CT
            for c in range(NT):
                w = tile_width(c)
                act.wait_ge(turned, m + 1)
                nc.scalar.activation(rows[0:w, c, :], turn[0:w, m % 2, 0:KV_RANK], ACT.Copy).then_inc(rows_kept, 1)
                m += 1
            for c in range(NT):
                w = tile_width(c)
                act.wait_ge(turned, m + 1)
                nc.scalar.activation(rrows[0:w, c, :], turn[0:w, m % 2, 0:B_ROPE], ACT.Copy).then_inc(rows_kept, 1)
                m += 1

        @block.tensor
        def _(pe):
            for i, (_, kts, _, _) in enumerate(lat):
                pe.wait_ge(squared, i + 1)
                for c, (c0, w) in enumerate(CHUNKS):
                    for k in range(kts):
                        last = nc.tensor.matmul(mean[:, i, c, 0:w], S["ones"][:], sq[:, k, c0:c0 + w],
                                                start=(k == 0), stop=(k == kts - 1))
                    last.then_inc(summed, 1)
            pe.wait_ge(c_in, 16 * 5)
            m = 0
            for c in range(CT):
                if m >= 2:
                    pe.wait_ge(copied, m - 1)
                for k in range(RK):
                    last = nc.tensor.transpose(turn[:, m % 2, k * P:(k + 1) * P], cache[:, c, k * P:(k + 1) * P], S["ident"][:])
                last.then_inc(turned, 1)
                m += 1
            for c in range(CT):
                pe.wait_ge(copied, m - 1)
                nc.tensor.transpose(turn[0:B_ROPE, m % 2, 0:P], rcache[:, c, :], S["ident"][:]).then_inc(turned, 1)
                m += 1
            pe.wait_ge(normed, RK)
            pe.wait_ge(krope, 1)
            pe.wait_ge(copied, 2 * CT)
            for c in range(NT):
                w = tile_width(c)
                if m >= 2 * CT + 2:
                    pe.wait_ge(rows_kept, m - 2 * CT - 1)
                for k in range(RK):
                    last = nc.tensor.transpose(turn[0:w, m % 2, k * P:(k + 1) * P], ckvT[:, k, c * P:c * P + w], S["ident"][:])
                last.then_inc(turned, 1)
                m += 1
            for c in range(NT):
                w = tile_width(c)
                if m >= 2 * CT + 2:
                    pe.wait_ge(rows_kept, m - 2 * CT - 1)
                nc.tensor.transpose(turn[0:w, m % 2, 0:B_ROPE], kr[lo:hi, c * P:c * P + w],
                                    S["ident"][lo:hi, lo:hi]).then_inc(turned, 1)
                m += 1

        @block.vector
        def _(dve):
            v = nc.vector
            dve.wait_ge(c_in, 16 * 5)
            new = kr[lo:hi, 0:T]
            v.tensor_tensor(new, new, cs[lo:hi, 0], ALU.mult).then_inc(dve_step, 1)
            v.tensor_tensor(krs[lo:hi], krs[lo:hi], cs[lo:hi, 1], ALU.mult).then_inc(dve_step, 1)
            dve.wait_ge(dve_step, 2)
            v.tensor_tensor(new, new, krs[lo:hi], ALU.add).then_inc(krope, 1)
            n = 0
            for i, (x, kts, g0, rank) in enumerate(lat):
                for c, (c0, w) in enumerate(CHUNKS):
                    dve.wait_ge(summed, NC * i + c + 1)
                    v.tensor_scalar(var[:, i, c0:c0 + w], mean[:, i, c, 0:w], 1.0 / rank, EPS, ALU.mult, ALU.add)\
                     .then_inc(var_done, 1)
                    n += 1
                    dve.wait_ge(var_done, n)
                    v.reciprocal(var[:, i, c0:c0 + w], var[:, i, c0:c0 + w]).then_inc(var_done, 1)
                    n += 1

            def norm(i):
                x, kts, g0, _ = lat[i]
                dve.wait_ge(rooted, i + 1)
                for k in range(kts):
                    v.scalar_tensor_tensor(out=x[:, k, 0:T], in0=x[:, k, 0:T], scalar=S["gains"][:, g0 + k:g0 + k + 1],
                                           in1=var[:, i], op0=ALU.mult, op1=ALU.mult).then_inc(normed, 1)

            norm(0)
            m = 0
            for c in range(CT):
                dve.wait_ge(turned, m + 1)
                v.tensor_copy(ckvT[:, :, T + c * P:T + (c + 1) * P],
                              turn[:, m % 2, 0:RK * P].rearrange("p (k n) -> p k n", k=RK)).then_inc(copied, 1)
                m += 1
            for c in range(CT):
                dve.wait_ge(turned, m + 1)
                v.tensor_copy(kr[lo:hi, T + c * P:T + (c + 1) * P], turn[0:B_ROPE, m % 2, 0:P]).then_inc(copied, 1)
                m += 1
            norm(1)


def heads_stage(nc, S, D):
    RQ, RK = Q_RANK // P, KV_RANK // P
    SPAN = KEYS // 4
    WIDTH = B_HEADS * B_VDIM
    cqT, ckvT = S["cqT"], S["ckvT"]
    tiles = [("w_qn", i, "q", i) for i in range(4)]
    tiles += [(w, j, "q", 4 + j) for j in range(2) for w in ("w_qr", "w_qs")]
    tiles += [("w_uk", i, "kv", 6 + i) for i in range(4)]
    spans = {"q": CHUNKS, "kv": [(c, SPAN) for c in range(0, KEYS, SPAN)]}
    items = [(i, c0, w) for i, x in enumerate(tiles) for c0, w in spans[x[2]]]
    FIRST_V = len(items)
    v_tiles = [(j * P, tile_width(j)) for j in range(NT)] + [(T + c * P, P) for c in range(PAST_LEN // P)]
    items += [("v", c0, w) for c0, w in v_tiles]
    by_act = [x[0] != "v" and tiles[x[0]][0] in ("w_qn", "w_uk") for x in items]

    def copies(m, act):
        return sum(by_act[:m]) if act else m - sum(by_act[:m])

    def end_of(i):
        return sum(1 for x in items if x[0] != "v" and x[0] <= i)

    with Stage(nc, "heads") as st:
        q_hi, q_lo = S["hhi"][:, 4:4 + RQ, :], S["hlo"][:, 4:4 + RQ, :]
        kv_hi, kv_lo = (st.sb(x, [P, RK, KEYS], F32R) for x in ("kv_hi", "kv_lo"))
        w_in = st.sb("w_in", [P, 2, RQ, P])
        w_hi, w_lo = (st.sb(x, [P, 2, RQ, P], F32R) for x in ("w_hi", "w_lo"))
        v_in = st.sb("v_in", [P, RK, WIDTH])
        v_hi, v_lo = (st.sb(x, [P, RK, WIDTH], F32R) for x in ("v_hi", "v_lo"))
        rope = st.sb("rope", [P, 2, T])
        turned = st.sb("turned", [P, T])
        out = st.sb("out", [P, 2, KEYS])
        bank = st.ps("bank", [P, 8, 512])
        names = ("w_loaded0", "w_loaded1", "v_loaded", "rope_in", "hi", "lo", "w_hi", "w_lo", "v_hi", "v_lo", "brought",
                 "act_kept", "dve_kept", "swapped", "parked0", "parked1")
        s = {x: st.sem(x) for x in names}
        block = st.block()
        OUTS = 10

        @block.sync
        def _(sp):
            def load(i):
                name, j, lat, _ = tiles[i]
                kts = RQ if lat == "q" else RK
                if i >= 2:
                    sp.wait_ge(s["w_lo"], i - 1)
                src = D[name].rearrange("(k p) n -> p k n", p=P)[:, :, j * P:(j + 1) * P]
                sp.dma_start(w_in[:, i % 2, 0:kts, :], src).then_inc(s[f"w_loaded{i % 2}"], 16)

            def park(o):
                i = max(i for i, x in enumerate(tiles) if x[3] == o)
                m = end_of(i)
                act = by_act[m - 1]
                sp.wait_ge(s["act_kept" if act else "dve_kept"], copies(m, act))
                if o < 6:
                    sp.dma_start(D["heads_q"][o * P:(o + 1) * P, :], out[:, o % 2, 0:T]).then_inc(s[f"parked{o % 2}"], 16)
                else:
                    sp.dma_start(D["heads_k"][(o - 6) * P:(o - 5) * P, :], out[:, o % 2, :]).then_inc(s[f"parked{o % 2}"], 16)

            load(0)
            load(1)
            sp.dma_start(rope[:], D["rope_q"]).then_inc(s["rope_in"], 16)
            sp.dma_start(v_in[:], D["w_uv"].rearrange("(k p) n -> p k n", p=P)).then_inc(s["v_loaded"], 16)
            done = 0
            for i in range(2, len(tiles)):
                load(i)
                while done < tiles[i - 2][3]:
                    park(done)
                    done += 1
            while done < OUTS:
                park(done)
                done += 1
            for n, (c0, w) in enumerate(v_tiles):
                sp.wait_ge(s["dve_kept"], copies(FIRST_V + n + 1, False))
                sp.dma_start(D["heads_v"][c0:c0 + w, :], out[0:w, n % 2, 0:WIDTH]).then_inc(s[f"parked{n % 2}"], 16)
            for half in range(2):
                sp.wait_ge(s[f"parked{half}"], 16 * ((OUTS + len(v_tiles) + 1 - half) // 2))

        @block.tensor
        def _(pe):
            pe.wait_ge(s["lo"], 1)
            for m, (i, c0, w) in enumerate(items):
                if m >= 8:
                    act = by_act[m - 8]
                    pe.wait_ge(s["act_kept" if act else "dve_kept"], copies(m - 7, act))
                dst = bank[:, m % 8, 0:WIDTH if i == "v" else w]
                if i == "v":
                    pe.wait_ge(s["v_lo"], 1)
                    cols = slice(c0, c0 + P)
                    passes = [(x[:, k, cols], y[:, k, :]) for k in range(RK)
                              for x, y in ((kv_hi, v_hi), (kv_lo, v_hi), (kv_hi, v_lo))]
                else:
                    pe.wait_ge(s["w_lo"], i + 1)
                    kv = tiles[i][2] == "kv"
                    if kv:
                        pe.wait_ge(s["lo"], 2)
                    xs = (kv_hi, kv_lo) if kv else (q_hi, q_lo)
                    passes = [(y[:, i % 2, k, :], x[:, k, c0:c0 + w]) for k in range(RK if kv else RQ)
                              for x, y in ((xs[0], w_hi), (xs[1], w_hi), (xs[0], w_lo))]
                for n, (lhsT, rhs) in enumerate(passes):
                    ins = nc.tensor.matmul(dst, lhsT, rhs, start=(n == 0), stop=(n == len(passes) - 1))
                ins.then_inc(s["brought"], 1)

        @block.scalar
        def _(act):
            def split_w(i):
                kts = RQ if tiles[i][2] == "q" else RK
                act.wait_ge(s[f"w_loaded{i % 2}"], 16 * (i // 2 + 1))
                if i >= 2:
                    act.wait_ge(s["brought"], end_of(i - 2))
                act.activation(w_hi[:, i % 2, 0:kts, :], w_in[:, i % 2, 0:kts, :], ACT.Copy).then_inc(s["w_hi"], 1)

            act.activation(q_hi, cqT[:], ACT.Copy).then_inc(s["hi"], 1)
            split_w(0)
            split_w(1)
            act.activation(kv_hi[:], ckvT[:], ACT.Copy).then_inc(s["hi"], 1)
            act.wait_ge(s["v_loaded"], 16)
            act.activation(v_hi[:], v_in[:], ACT.Copy).then_inc(s["v_hi"], 1)
            for m, (i, c0, w) in enumerate(items[:FIRST_V]):
                if by_act[m]:
                    name, _, _, o = tiles[i]
                    act.wait_ge(s["brought"], m + 1)
                    if c0 == 0 and o >= 2:
                        act.wait_ge(s[f"parked{o % 2}"], 16 * (o // 2))
                    act.activation(out[:, o % 2, c0:c0 + w], bank[:, m % 8, 0:w], ACT.Copy,
                                   scale=MLA_SCALE if name == "w_qn" else 1.0).then_inc(s["act_kept"], 1)
                if m + 1 == end_of(i) and i + 2 < len(tiles):
                    split_w(i + 2)

        @block.gpsimd
        def _(pool):
            for i in range(len(tiles)):
                kts = RQ if tiles[i][2] == "q" else RK
                pool.wait_ge(s["w_hi"], i + 1)
                pool.tensor_tensor(w_lo[:, i % 2, 0:kts, :], w_in[:, i % 2, 0:kts, :], w_hi[:, i % 2, 0:kts, :],
                                   ALU.subtract).then_inc(s["w_lo"], 1)
                if i == 1:
                    pool.wait_ge(s["v_hi"], 1)
                    pool.tensor_tensor(v_lo[:], v_in[:], v_hi[:], ALU.subtract).then_inc(s["v_lo"], 1)

        @block.vector
        def _(dve):
            for n, (x, hi_, lo_) in enumerate(((cqT, q_hi, q_lo), (ckvT, kv_hi[:], kv_lo[:]))):
                dve.wait_ge(s["hi"], n + 1)
                dve.tensor_tensor(lo_, x[:], hi_, ALU.subtract).then_inc(s["lo"], 1)
            dve.wait_ge(s["rope_in"], 16)
            turns = 0
            for m, (i, c0, w) in enumerate(items):
                if by_act[m]:
                    continue
                dve.wait_ge(s["brought"], m + 1)
                src = bank[:, m % 8, 0:w]
                if i == "v":
                    n = m - FIRST_V
                    dve.wait_ge(s[f"parked{n % 2}"], 16 * ((OUTS + n) // 2))
                    dve.tensor_copy(out[0:w, n % 2, 0:WIDTH], bank[0:w, m % 8, 0:WIDTH]).then_inc(s["dve_kept"], 1)
                elif tiles[i][0] == "w_qr":
                    if turns:
                        dve.wait_ge(s["dve_kept"], copies(m, False))
                    dve.tensor_tensor(turned[:, c0:c0 + w], rope[:, 0, c0:c0 + w], src, ALU.mult).then_inc(s["dve_kept"], 1)
                else:
                    o = tiles[i][3]
                    if c0 == 0:
                        dve.wait_ge(s[f"parked{o % 2}"], 16 * (o // 2))
                    dst = out[:, o % 2, c0:c0 + w]
                    dve.tensor_tensor(dst, rope[:, 1, c0:c0 + w], src, ALU.mult).then_inc(s["swapped"], 1)
                    turns += 1
                    dve.wait_ge(s["swapped"], turns)
                    dve.wait_ge(s["dve_kept"], copies(m, False))
                    dve.tensor_tensor(dst, dst, turned[:, c0:c0 + w], ALU.add).then_inc(s["dve_kept"], 1)


def mla_stage(nc, S, D):
    H, K = B_VDIM, B_NOPE + B_ROPE
    TILES = [0, 1, 2, 3, NT - 1, 4, 5, 6, 7]
    N = len(TILES)
    CT = PAST_LEN // P
    VT = NT + CT
    pairs = B_HEADS // 2
    LOADS = 3
    CAT0 = A_HEADS * A_DIM // P
    hhi, hlo = S["hhi"], S["hlo"]

    def key_tiles(t):
        if t == NT - 1:
            return [(T + c * P, P, NT + c) for c in range(CT)] + [(SEQ, DEC_SEQ, NT - 1)]
        return [(j * P, P, j) for j in range(t + 1)]

    def width_of(t):
        return sum(x[1] for x in key_tiles(t))

    with Stage(nc, "mla") as st:
        q_in, k_in = st.sb("q_in", [K, T]), st.sb("k_in", [B_NOPE, KEYS])
        qhi, qlo = (st.sb(x, [K, 2, NT * P], F32R) for x in ("qhi", "qlo"))
        khi, klo = (st.sb(x, [K, 2, KEYS], F32R) for x in ("khi", "klo"))
        V = st.sb("V", [P, 2, VT, P])
        p, pT = st.sb("p", [P, 2, SEQ]), st.sb("pT", [P, 2, SEQ])
        neg_max, total, inv = (st.sb(x, [P, 2 * N]) for x in ("neg_max", "total", "inv"))
        diag = st.sb("diag", [P, 2, P])
        halves = st.sb("halves", [1, 2 * P + CHUNK], F32R)
        pS = st.ps("pS", [P, 2, 2, 512])
        pP = st.ps("pP", [P, 1024])
        pO = st.ps("pO", [P, 2, 512])
        names = ("loaded", "v_in", "q_hi", "k_hi", "q_lo", "k_lo", "scored", "maxed", "exped", "inverted", "diag_set",
                 "turned", "p_kept", "summed", "hi", "lo", "apart", "rope_hi", "set_up")
        s = {x: st.sem(x) for x in names}
        block = st.block()
        rot = slice(B_NOPE, K)

        def own(e):
            return slice(H * e, H * e + H)

        def step_of(hp, m):
            return 2 * N * hp + m, (m // N) % 2, TILES[m % N]

        def waits_apart(eng, *waits):
            for name, count in waits:
                eng.wait_ge(s[name], count)
                eng.sem_inc(s["apart"], 1)

        def out_of(hp, m):
            _, e, t = step_of(hp, m)
            pair = bass.ds((hp if m >= 0 else hp - 1) + CAT0, 1)
            cols = slice(t * P, t * P + tile_width(t))
            return [x[own(e), pair, cols].rearrange("p a n -> p (a n)") for x in (hhi, hlo)]

        @block.sync
        def _(sp):
            def load(h):
                sp.dma_start(q_in[0:B_NOPE, :], D["heads_q"][bass.ds(h * B_NOPE, B_NOPE), :]).then_inc(s["loaded"], 16)
                sp.dma_start(q_in[rot, :], D["heads_q"][bass.ds(h * B_ROPE + B_HEADS * B_NOPE, B_ROPE), :])\
                  .then_inc(s["loaded"], 16)
                sp.dma_start(k_in[:], D["heads_k"][bass.ds(h * B_NOPE, B_NOPE), :]).then_inc(s["loaded"], 16)

            def load_v(pair, e):
                cols = bass.ds(pair * P, P)
                for rows, dst in ((slice(0, SEQ), V[:, e, 0:NT - 1, :]), (slice(T, KEYS), V[:, e, NT:VT, :])):
                    sp.dma_start(dst, D["heads_v"][rows, :].rearrange("(c p) n -> p c n", p=P)[:, :, cols])\
                      .then_inc(s["v_in"], 16)
                sp.dma_start(V[0:DEC_SEQ, e, NT - 1, :], D["heads_v"][SEQ:T, cols]).then_inc(s["v_in"], 16)

            def wait_split(h):
                waits_apart(sp, ("q_lo", h + 1), ("k_lo", h + 1))

            def head(hp, e, last):
                h = 2 * hp + e
                if not (last and e == 1):
                    waits_apart(sp, ("summed", N * h + 1))
                    load_v(hp + e, 1 - e)
                    if not last:
                        wait_split(h + 1)
                        load(h + 2)

            load(0)
            load_v(0, 0)
            wait_split(0)
            load(1)
            with sp.Fori(0, pairs - 1) as hp:
                for e in range(2):
                    head(hp, e, False)
            for e in range(2):
                head(pairs - 1, e, True)

        @block.tensor
        def _(pe):
            def score(hp, m):
                g, e, t = step_of(hp, m)
                if m % N == 0:
                    h = 2 * hp + m // N
                    waits_apart(pe, ("q_lo", h + 1), ("k_lo", h + 1))
                pe.wait_ge(s["exped"], g + 1)
                out = pS[:, m % 2].rearrange("p b n -> p (b n)")
                qs = slice(t * P, t * P + P)
                W, c, runs = width_of(t), 0, []
                for k0, kw, _ in key_tiles(t):
                    if runs and runs[-1][1] + runs[-1][2] == k0 and c % 512:
                        runs[-1][2] += kw
                    else:
                        runs.append([c, k0, kw])
                    c += kw
                for c, k0, kw in runs:
                    cols, keys = out[:, c:c + kw], slice(k0, k0 + kw)
                    parts = [(cols, qhi[:, e, qs], khi[:, e, keys]), (cols, qhi[:, e, qs], klo[:, e, keys]),
                             (cols, qlo[:, e, qs], khi[:, e, keys])]
                    if c + kw == W and t < NT - 1:
                        parts.append((out[:, W - CHUNK:W], halves[0:1, 0:P], halves[0:1, 2 * P:2 * P + CHUNK]))
                    for q, (dst, lhsT, rhs) in enumerate(parts):
                        ins = nc.tensor.matmul(dst, lhsT, rhs, start=(q == 0), stop=(q == len(parts) - 1))
                ins.then_inc(s["scored"], 1)

            def turn(hp, m):
                g, _, t = step_of(hp, m)
                w = tile_width(t)
                pe.wait_ge(s["p_kept"], g + 1)
                pe.wait_ge(s["diag_set"], g + 1)
                if w < P:
                    pe.sem_inc(s["apart"], 1)
                c = 0
                for b, (_, kw, _) in enumerate(key_tiles(t)):
                    ins = nc.tensor.matmul(pP[0:kw, b * P:b * P + w], p[0:w, m % 2, c:c + kw], diag[0:w, m % 2, 0:w],
                                           start=True, stop=True)
                    c += kw
                ins.then_inc(s["turned"], 1)

            def weigh(hp, m):
                g, e, t = step_of(hp, m)
                w = tile_width(t)
                tiles = key_tiles(t)
                if m % N == 0:
                    waits_apart(pe, ("v_in", 16 * LOADS * (2 * hp + m // N + 1)))
                pe.wait_ge(s["lo"], g + 1)
                pe.wait_ge(s["p_kept"], g + 2)
                if w < P:
                    pe.sem_inc(s["apart"], 1)
                for b, (_, kw, vt) in enumerate(tiles):
                    ins = nc.tensor.matmul(pO[:, m % 2, 0:w], V[0:kw, e, vt, :], pT[0:kw, m % 2, b * P:b * P + w],
                                           start=(b == 0), stop=(b == len(tiles) - 1))
                ins.then_inc(s["summed"], 1)

            def steps(hp, first, last):
                for m in range(2 * N):
                    if not (last and m == 2 * N - 1):
                        score(hp, m + 1)
                    turn(hp, m)
                    if not (first and m == 0):
                        weigh(hp, m - 1)

            pe.wait_ge(s["set_up"], 6)
            score(0, 0)
            steps(0, True, False)
            with pe.Fori(1, pairs - 1) as hp:
                steps(hp, False, False)
            steps(pairs - 1, False, True)
            weigh(pairs - 1, 2 * N - 1)

        @block.scalar
        def _(act):
            act.sem_inc(s["exped"], 2)
            act.sem_inc(s["p_kept"], 1)
            for e in range(2):
                act.activation(khi[rot, e, :], S["kr"][rot, :], ACT.Copy).then_inc(s["rope_hi"], 1)

            def split_q(h, e):
                act.wait_ge(s["loaded"], 16 * LOADS * (h + 1))
                act.activation(qhi[:, e, 0:T], q_in[:], ACT.Copy).then_inc(s["q_hi"], 1)

            def split_k(h, e):
                act.activation(khi[0:B_NOPE, e, :], k_in[:], ACT.Copy).then_inc(s["k_hi"], 1)

            def exp(hp, m):
                g, _, t = step_of(hp, m)
                w, W = tile_width(t), width_of(t)
                col = slice(m % (2 * N), m % (2 * N) + 1)
                act.wait_ge(s["maxed"], g + 1)
                act.activation(p[0:w, m % 2, 0:W], pS[0:w, m % 2].rearrange("p b n -> p (b n)")[:, 0:W], ACT.Exp,
                               bias=neg_max[0:w, col], accum_out=total[0:w, col]).then_inc(s["exped"], 1)

            def keep(hp, m):
                g, _, t = step_of(hp, m)
                w = tile_width(t)
                n = len(key_tiles(t))
                act.wait_ge(s["turned"], g + 1)
                if w == P:
                    act.activation(pT[:, m % 2, 0:n * P], pP[:, 0:n * P], ACT.Copy).then_inc(s["p_kept"], 1)
                else:
                    wide = lambda x: x.rearrange("p (b n) -> p b n", n=P)[:, 0:CT, 0:w]
                    act.activation(wide(pT[:, m % 2, :]), wide(pP[:]), ACT.Copy)
                    act.activation(pT[0:DEC_SEQ, m % 2, CT * P:CT * P + w], pP[0:DEC_SEQ, CT * P:CT * P + w],
                                   ACT.Copy).then_inc(s["p_kept"], 1)

            def high(hp, m):
                g, e, t = step_of(hp, m)
                act.wait_ge(s["summed"], g + 1)
                act.activation(out_of(hp, m)[0], pO[own(e), m % 2, 0:tile_width(t)], ACT.Copy).then_inc(s["hi"], 1)

            def steps(hp, first, last):
                for m in range(2 * N):
                    if not (first and m < 2):
                        high(hp, m - 2)
                    if not (last and m == 2 * N - 1):
                        exp(hp, m + 1)
                    keep(hp, m)
                    if not (last and m >= N):
                        h, e, i = 2 * hp + m // N + 1, 1 - m // N, m % N
                        if i == 1:
                            split_q(h, e)
                        if i == 3:
                            split_k(h, e)

            split_q(0, 0)
            split_k(0, 0)
            exp(0, 0)
            steps(0, True, False)
            with act.Fori(1, pairs - 1) as hp:
                steps(hp, False, False)
            steps(pairs - 1, False, True)
            high(pairs - 1, 2 * N - 2)
            high(pairs - 1, 2 * N - 1)

        @block.vector
        def _(dve):
            dve.sem_inc(s["lo"], 2)
            dve.tensor_copy(halves[:], S["halves"][:]).then_inc(s["set_up"], 1)
            for e in range(2):
                for x in (qhi, qlo):
                    ins = dve.tensor_scalar(x[:, e, T:NT * P], S["ones"][0:K, 0:NT * P - T], 0.0, None, ALU.mult)
                    ins.then_inc(s["set_up"], 1)
                dve.wait_ge(s["rope_hi"], e + 1)
                ins = dve.tensor_tensor(klo[rot, e, :], S["kr"][rot, :], khi[rot, e, :], ALU.subtract)
                if e == 1:
                    ins.then_inc(s["set_up"], 1)

            def split_q(h, e):
                dve.wait_ge(s["q_hi"], h + 1)
                dve.tensor_tensor(qlo[:, e, 0:T], q_in[:], qhi[:, e, 0:T], ALU.subtract).then_inc(s["q_lo"], 1)

            def maximum(hp, m):
                g, _, t = step_of(hp, m)
                w, W = tile_width(t), width_of(t)
                dve.wait_ge(s["scored"], g + 1)
                dve.tensor_reduce(neg_max[0:w, m % (2 * N):m % (2 * N) + 1], pS[0:w, m % 2].rearrange("p b n -> p (b n)")[:, 0:W],
                                  AX_X, ALU.max, negate=True).then_inc(s["maxed"], 1)

            def inverse(hp, m):
                g, _, t = step_of(hp, m)
                w = tile_width(t)
                col = slice(m % (2 * N), m % (2 * N) + 1)
                dve.wait_ge(s["exped"], g + 3)
                dve.reciprocal(inv[0:w, col], total[0:w, col]).then_inc(s["inverted"], 1)
                dve.wait_ge(s["inverted"], g + 1)
                dve.tensor_scalar(diag[0:w, m % 2, 0:w], S["ident"][0:w, 0:w], inv[0:w, col], None, ALU.mult)\
                   .then_inc(s["diag_set"], 1)

            def low(hp, m):
                g, e, t = step_of(hp, m)
                hi_, lo_ = out_of(hp, m)
                dve.wait_ge(s["hi"], g + 1)
                dve.tensor_tensor(lo_, pO[own(e), m % 2, 0:tile_width(t)], hi_, ALU.subtract).then_inc(s["lo"], 1)

            def steps(hp, first, last):
                for m in range(2 * N):
                    if not (last and m == 2 * N - 1):
                        maximum(hp, m + 1)
                    if not (first and m < 2):
                        low(hp, m - 2)
                    if not (last and m == 2 * N - 1):
                        inverse(hp, m + 1)
                    if m % N == 3 and not (last and m >= N):
                        split_q(2 * hp + m // N + 1, 1 - m // N)

            split_q(0, 0)
            maximum(0, 0)
            inverse(0, 0)
            steps(0, True, False)
            with dve.Fori(1, pairs - 1) as hp:
                steps(hp, False, False)
            steps(pairs - 1, False, True)
            low(pairs - 1, 2 * N - 2)
            low(pairs - 1, 2 * N - 1)

        @block.gpsimd
        def _(pool):
            def split_k(h, e):
                pool.wait_ge(s["k_hi"], h + 1)
                pool.sem_inc(s["apart"], 1)
                pool.tensor_tensor(klo[0:B_NOPE, e, :], k_in[:], khi[0:B_NOPE, e, :], ALU.subtract).then_inc(s["k_lo"], 1)

            split_k(0, 0)
            split_k(1, 1)
            with pool.Fori(1, pairs) as hp:
                for e in range(2):
                    split_k(2 * hp + e, e)


def band_stage(nc, S, D):
    H = C_DIM
    TILES = [4, 0, 5, 1, NT - 1, 2, 6, 3, 7]
    N = len(TILES)
    CT = PAST_LEN // P
    VT = NT + CT
    pairs = C_HEADS // 2
    TURNS = 3
    STAGE_AT = {2: 0, 4: 1, 6: 2}
    LOADS, STORES = 8, 4
    hhi, hlo = S["hhi"], S["hlo"]

    def key_tiles(t):
        if t == NT - 1:
            return [(T + c * P, P, NT + c) for c in range(CT)] + [(SEQ, DEC_SEQ, NT - 1)]
        return [(j * P, P, j) for j in range(max(0, t - 4), t + 1)]

    def score_cols(t):
        W = sum(x[1] for x in key_tiles(t))
        c0 = 2 * P if W > 512 else 0
        return c0, c0 + W

    with Stage(nc, "band") as st:
        q_in, k_in, v_in = st.sb("q_in", [P, T]), st.sb("k_in", [P, T]), st.sb("v_in", [H, T])
        c_in = st.sb("c_in", [P, CT, 2, H])
        b_in = st.sb("b_in", [P, 2 * P])
        q2, k2 = st.sb("q2", [P, 2, NT * P], F32R), st.sb("k2", [P, 2, KEYS], F32R)
        klo = st.sb("klo", [H, 2, KEYS], F32R)
        V = st.sb("V", [P, 2, VT, P])
        ktok = st.sb("ktok", [P, 5, H])
        near = st.sb("near", [P, 2 * P])
        bias = st.sb("bias", [P, 2, 2, 2 * P], F32R)
        ident = st.sb("ident", [P, P], F32R)
        p, pT = st.sb("p", [P, 2, 640]), st.sb("pT", [P, 2, 640])
        neg_max, total, inv = (st.sb(x, [P, 2 * N]) for x in ("neg_max", "total", "inv"))
        diag = st.sb("diag", [P, 2, P])
        halves = st.sb("halves", [1, 2 * P + CHUNK], F32R)
        pS = st.ps("pS", [P, 2, 2, 512])
        pP = st.ps("pP", [P, 1024])
        pO = st.ps("pO", [P, 512])
        spare = st.ps("spare", [P, 512])
        names = ("loaded", "cv_in", "q_hi", "k_hi", "q_lo", "k_lo", "kc_hi", "turned_in", "taken", "scored",
                 "maxed", "exped", "inverted", "diag_set", "turned", "p_kept", "summed", "hi", "lo", "apart", "stored",
                 "near_set", "bias_hi", "bias_lo", "rolled", "set_up")
        s = {x: st.sem(x) for x in names}
        block = st.block()

        def own(e):
            return slice(H * e, H * e + H)

        def step_of(hp, m):
            return 2 * N * hp + m, (m // N) % 2, TILES[m % N]

        def waits_apart(eng, *waits):
            for name, count in waits:
                eng.wait_ge(s[name], count)
                eng.sem_inc(s["apart"], 1)

        @block.sync
        def _(sp):
            def load(h):
                for half in range(2):
                    rows = slice(half * H, half * H + H)
                    sp.dma_start(q_in[rows, :], D["z"][bass.ds(h * H, H), :]).then_inc(s["loaded"], 16)
                    sp.dma_start(k_in[rows, :], D["z"][bass.ds(h * H + D_MODEL, H), :]).then_inc(s["loaded"], 16)
                    sp.dma_start(c_in[:, :, half, :], D["c_k"].rearrange("(c p) n -> p c n", p=P)[:, :, bass.ds(h * H, H)])\
                      .then_inc(s["loaded"], 16)
                sp.dma_start(v_in[:], D["z"][bass.ds(h * H + 2 * D_MODEL, H), :]).then_inc(s["loaded"], 16)
                sp.dma_start(b_in[:], D["bias"][bass.ds(h, 1), :, :].rearrange("h p j -> p (h j)")).then_inc(s["loaded"], 16)

            def load_cv(h, e):
                sp.dma_start(V[:, e, NT:VT, own(e)], D["c_v"].rearrange("(c p) n -> p c n", p=P)[:, :, bass.ds(h * H, H)])\
                  .then_inc(s["cv_in"], 16)

            def wait_used(h):
                waits_apart(sp, ("q_lo", h + 1), ("k_lo", 2 * h + 2), ("taken", TURNS * h + TURNS), ("bias_lo", h + 1))

            def store(h, e):
                col = bass.ds(h * H, H)
                for src, new, kv in ((ktok[:, 0:4, :], ktok[0:DEC_SEQ, 4, :], "bk"),
                                     (V[:, e, 4:8, own(e)], V[0:DEC_SEQ, e, 8, own(e)], "bv")):
                    sp.dma_start(D["p_" + kv].rearrange("(c p) n -> p c n", p=P)[:, :, col], src).then_inc(s["stored"], 16)
                    sp.dma_start(D["s_" + kv][PAST_LEN - DEC_SEQ:PAST_LEN, col], new).then_inc(s["stored"], 16)

            def head(hp, e, last):
                h = 2 * hp + e
                if not (last and e == 1):
                    waits_apart(sp, ("summed", N * h + 1))
                    load_cv(h + 1, 1 - e)
                    wait_used(h + 1)
                    if not last:
                        load(h + 2)
                    store(h + 1, 1 - e)

            load(0)
            load_cv(0, 0)
            for kv in ("k", "v"):
                sp.dma_start(D["s_b" + kv][0:PAST_LEN - DEC_SEQ, :], D["c_" + kv][DEC_SEQ:PAST_LEN, :]).then_inc(s["rolled"], 16)
            wait_used(0)
            load(1)
            store(0, 0)
            with sp.Fori(0, pairs - 1) as hp:
                for e in range(2):
                    head(hp, e, False)
            for e in range(2):
                head(pairs - 1, e, True)
            sp.wait_ge(s["stored"], 16 * STORES * (C_HEADS + 1))
            sp.wait_ge(s["rolled"], 32)

        @block.tensor
        def _(pe):
            def turn_in(h, which):
                if not (isinstance(h, int) and h == 0 and which == 0):
                    pe.wait_ge(s["taken"], TURNS * h + which)
                pe.sem_inc(s["apart"], 1)
                if which == 0:
                    pe.wait_ge(s["loaded"], 16 * LOADS * (h + 1))
                    pe.sem_inc(s["apart"], 1)
                    for c in range(8):
                        ins = nc.tensor.transpose(spare[:, c * H:(c + 1) * H], v_in[:, c * P:(c + 1) * P], S["ident"][0:H, 0:H])
                elif which == 1:
                    for q, c in enumerate(range(4, NT)):
                        w = tile_width(c)
                        nc.tensor.transpose(spare[0:w, q * H:(q + 1) * H], k_in[0:H, c * P:c * P + w], S["ident"][0:H, 0:H])
                    ins = nc.tensor.transpose(spare[0:DEC_SEQ, 5 * H:6 * H], v_in[:, SEQ:T], S["ident"][0:H, 0:H])
                else:
                    for c in range(CT):
                        ins = nc.tensor.transpose(spare[:, c * P:(c + 1) * P], c_in[:, c].rearrange("p a n -> p (a n)"),
                                                  S["ident"][:])
                ins.then_inc(s["turned_in"], 1)

            def score(hp, m):
                g, e, t = step_of(hp, m)
                tiles = key_tiles(t)
                if m % N == 0:
                    h = 2 * hp + m // N
                    waits_apart(pe, ("q_lo", h + 1), ("k_lo", 2 * h + 2), ("taken", TURNS * h + TURNS), ("bias_lo", h + 1))
                pe.wait_ge(s["exped"], g + 1)
                out = pS[:, m % 2].rearrange("p b n -> p (b n)")
                end = score_cols(t)[1]
                runs, c = [], score_cols(t)[0]
                for k0, kw, _ in tiles:
                    if runs and runs[-1][1] + runs[-1][2] == k0 and c % 512:
                        runs[-1][2] += kw
                    else:
                        runs.append([c, k0, kw])
                    c += kw
                qs = slice(t * P, t * P + P)
                width, b0 = (P, P) if t == 0 else (192, 0) if t == NT - 1 else (2 * P, 0)
                for r, (c, k0, kw) in enumerate(runs):
                    cols, keys = out[:, c:c + kw], slice(k0, k0 + kw)
                    parts = [(cols, q2[:, e, qs], k2[:, e, keys]), (cols, q2[0:H, e, qs], klo[:, e, keys])]
                    if r == 0 and 4 <= t < NT - 1:
                        parts.append((out[:, c:c + CHUNK], halves[0:1, P:2 * P], halves[0:1, 2 * P:2 * P + CHUNK]))
                    lo_, hi_ = max(c, end - width), c + kw
                    if lo_ < hi_:
                        b = b0 + lo_ - (end - width)
                        parts += [(out[:, lo_:hi_], ident[:], bias[:, e, part, b:b + hi_ - lo_]) for part in range(2)]
                    for q, (dst, lhsT, rhs) in enumerate(parts):
                        ins = nc.tensor.matmul(dst, lhsT, rhs, start=(q == 0), stop=(q == len(parts) - 1))
                ins.then_inc(s["scored"], 1)

            def turn(hp, m):
                g, _, t = step_of(hp, m)
                w = tile_width(t)
                pe.wait_ge(s["p_kept"], g + 1)
                pe.wait_ge(s["diag_set"], g + 1)
                if w < P:
                    pe.sem_inc(s["apart"], 1)
                c = 0
                for b, (_, kw, _) in enumerate(key_tiles(t)):
                    ins = nc.tensor.matmul(pP[0:kw, b * P:b * P + w], p[0:w, m % 2, c:c + kw], diag[0:w, m % 2, 0:w],
                                           start=True, stop=True)
                    c += kw
                ins.then_inc(s["turned"], 1)

            def weigh(hp, m):
                g, e, t = step_of(hp, m)
                w = tile_width(t)
                tiles = key_tiles(t)
                if m % N == 0:
                    waits_apart(pe, ("cv_in", 16 * (2 * hp + m // N + 1)))
                pe.wait_ge(s["lo"], g + 1)
                pe.wait_ge(s["p_kept"], g + 2)
                if w < P:
                    pe.sem_inc(s["apart"], 1)
                for b, (_, kw, vt) in enumerate(tiles):
                    ins = nc.tensor.matmul(pO[:, 0:w], V[0:kw, e, vt, :], pT[0:kw, m % 2, b * P:b * P + w],
                                           start=(b == 0), stop=(b == len(tiles) - 1))
                ins.then_inc(s["summed"], 1)

            def steps(hp, first, last):
                for m in range(2 * N):
                    if not (last and m == 2 * N - 1):
                        score(hp, m + 1)
                    turn(hp, m)
                    if not (first and m == 0):
                        weigh(hp, m - 1)
                    if m % N in STAGE_AT and not (last and m >= N):
                        turn_in(2 * hp + m // N + 1, STAGE_AT[m % N])

            for which in range(TURNS):
                turn_in(0, which)
            pe.wait_ge(s["set_up"], 6)
            score(0, 0)
            steps(0, True, False)
            with pe.Fori(1, pairs - 1) as hp:
                steps(hp, False, False)
            steps(pairs - 1, False, True)
            weigh(pairs - 1, 2 * N - 1)

        @block.scalar
        def _(act):
            act.sem_inc(s["exped"], 2)
            act.sem_inc(s["p_kept"], 1)
            act.sem_inc(s["stored"], 16 * STORES)

            def split_q(h, e):
                act.wait_ge(s["loaded"], 16 * LOADS * (h + 1))
                act.activation(q2[:, e, 0:T], q_in[:], ACT.Copy, scale=C_SCALE).then_inc(s["q_hi"], 1)

            def split_k(h, e):
                act.activation(k2[:, e, 0:T], k_in[:], ACT.Copy).then_inc(s["k_hi"], 1)

            def split_bias(h, e):
                act.wait_ge(s["near_set"], 2 * h + 2)
                act.activation(bias[:, e, 0, :], near[:], ACT.Copy).then_inc(s["bias_hi"], 1)

            def take(h, e, which):
                act.wait_ge(s["turned_in"], TURNS * h + which + 1)
                if which == 1:
                    act.wait_ge(s["stored"], 16 * STORES * (h + 1))
                    act.activation(ktok[:, 0:4, :].rearrange("p c n -> p (c n)"), spare[:, 0:4 * H], ACT.Copy)
                    act.activation(ktok[0:DEC_SEQ, 4, :], spare[0:DEC_SEQ, 4 * H:5 * H], ACT.Copy)
                    act.activation(V[0:DEC_SEQ, e, NT - 1, own(e)], spare[0:DEC_SEQ, 5 * H:6 * H], ACT.Copy)\
                       .then_inc(s["taken"], 1)
                elif which == 2:
                    act.activation(k2[:, e, T:KEYS], spare[:], ACT.Copy).then_inc(s["kc_hi"], 1)

            def exp(hp, m):
                g, _, t = step_of(hp, m)
                w = tile_width(t)
                c0, c1 = score_cols(t)
                act.wait_ge(s["maxed"], g + 1)
                act.activation(p[0:w, m % 2, 0:c1 - c0], pS[0:w, m % 2].rearrange("p b n -> p (b n)")[:, c0:c1], ACT.Exp,
                               bias=neg_max[0:w, m % (2 * N):m % (2 * N) + 1],
                               accum_out=total[0:w, m % (2 * N):m % (2 * N) + 1]).then_inc(s["exped"], 1)

            def keep(hp, m):
                g, _, t = step_of(hp, m)
                w = tile_width(t)
                n = len(key_tiles(t))
                act.wait_ge(s["turned"], g + 1)
                if w == P:
                    act.activation(pT[:, m % 2, 0:n * P], pP[:, 0:n * P], ACT.Copy).then_inc(s["p_kept"], 1)
                else:
                    wide = lambda x: x.rearrange("p (b n) -> p b n", n=P)[:, 0:CT, 0:w]
                    act.activation(wide(pT[:, m % 2, :]), wide(pP[:, 0:640]), ACT.Copy)
                    act.activation(pT[0:DEC_SEQ, m % 2, CT * P:CT * P + w], pP[0:DEC_SEQ, CT * P:CT * P + w],
                                   ACT.Copy).then_inc(s["p_kept"], 1)

            def high(hp, m):
                g, e, t = step_of(hp, m)
                w = tile_width(t)
                pair = hp if m >= 0 else hp - 1
                act.wait_ge(s["summed"], g + 1)
                act.activation(hhi[own(e), bass.ds(pair, 1), t * P:t * P + w].rearrange("p a n -> p (a n)"),
                               pO[own(e), 0:w], ACT.Copy).then_inc(s["hi"], 1)

            def steps(hp, first, last):
                for m in range(2 * N):
                    if not (last and m == 2 * N - 1):
                        exp(hp, m + 1)
                    keep(hp, m)
                    if not (first and m == 0):
                        high(hp, m - 1)
                    if not (last and m >= N):
                        h, e, i = 2 * hp + m // N + 1, 1 - m // N, m % N
                        if i == 0:
                            split_q(h, e)
                        if i == 1:
                            split_k(h, e)
                        if i in STAGE_AT:
                            take(h, e, STAGE_AT[i])
                        if i == 5:
                            split_bias(h, e)

            split_q(0, 0)
            split_k(0, 0)
            split_bias(0, 0)
            for which in range(TURNS):
                take(0, 0, which)
            exp(0, 0)
            steps(0, True, False)
            with act.Fori(1, pairs - 1) as hp:
                steps(hp, False, False)
            steps(pairs - 1, False, True)
            high(pairs - 1, 2 * N - 1)

        @block.vector
        def _(dve):
            dve.sem_inc(s["lo"], 1)
            for e in range(2):
                dve.memset(V[:, e, :, own(1 - e)], 0.0).then_inc(s["set_up"], 1)
                dve.tensor_scalar(q2[:, e, T:NT * P], S["ones"][:, 0:NT * P - T], 0.0, None, ALU.mult)\
                   .then_inc(s["set_up"], 1)
            dve.tensor_copy(halves[:], S["halves"][:]).then_inc(s["set_up"], 1)
            dve.tensor_copy(ident[:], S["ident"][:]).then_inc(s["set_up"], 1)

            def split_q(h, e):
                dve.wait_ge(s["q_hi"], h + 1)
                dve.scalar_tensor_tensor(out=q2[H:P, e, 0:T], in0=q_in[H:P, :], scalar=C_SCALE, in1=q2[H:P, e, 0:T],
                                         op0=ALU.mult, op1=ALU.subtract).then_inc(s["q_lo"], 1)

            def set_bias(h, e):
                dve.wait_ge(s["loaded"], 16 * LOADS * (h + 1))
                dve.tensor_scalar(near[:], b_in[:], b_in[:, 0:1], None, ALU.subtract).then_inc(s["near_set"], 1)
                dve.wait_ge(s["near_set"], 2 * h + 1)
                dve.memset(near[0:CHUNK, 2 * P - CHUNK:2 * P], NEG).then_inc(s["near_set"], 1)

            def split_bias(h, e):
                dve.wait_ge(s["bias_hi"], h + 1)
                dve.tensor_tensor(bias[:, e, 1, :], near[:], bias[:, e, 0, :], ALU.subtract).then_inc(s["bias_lo"], 1)

            def take(h, e, which):
                if which == 0:
                    dve.wait_ge(s["turned_in"], TURNS * h + 1)
                    if not (isinstance(h, int) and h == 0):
                        dve.wait_ge(s["stored"], 16 * STORES * h)
                    dve.tensor_copy(V[:, e, 0:8, own(e)], spare[:].rearrange("p (c n) -> p c n", n=H))\
                       .then_inc(s["taken"], 1)
                elif which == 2:
                    dve.wait_ge(s["kc_hi"], h + 1)
                    dve.tensor_tensor(klo[:, e, T:KEYS], spare[0:H, :], k2[0:H, e, T:KEYS], ALU.subtract)\
                       .then_inc(s["taken"], 1)

            def maximum(hp, m):
                g, e, t = step_of(hp, m)
                w = tile_width(t)
                c0, c1 = score_cols(t)
                dve.wait_ge(s["scored"], g + 1)
                dve.tensor_reduce(neg_max[0:w, m % (2 * N):m % (2 * N) + 1], pS[0:w, m % 2].rearrange("p b n -> p (b n)")[:, c0:c1],
                                  AX_X, ALU.max, negate=True).then_inc(s["maxed"], 1)

            def inverse(hp, m):
                g, _, t = step_of(hp, m)
                w = tile_width(t)
                col = slice(m % (2 * N), m % (2 * N) + 1)
                dve.wait_ge(s["exped"], g + 3)
                dve.reciprocal(inv[0:w, col], total[0:w, col]).then_inc(s["inverted"], 1)
                dve.wait_ge(s["inverted"], g + 1)
                dve.tensor_scalar(diag[0:w, m % 2, 0:w], S["ident"][0:w, 0:w], inv[0:w, col], None, ALU.mult)\
                   .then_inc(s["diag_set"], 1)

            def low(hp, m):
                g, e, t = step_of(hp, m)
                w = tile_width(t)
                pair = bass.ds(hp if m >= 0 else hp - 1, 1)
                part = [x[own(e), pair, t * P:t * P + w].rearrange("p a n -> p (a n)") for x in (hhi, hlo)]
                dve.wait_ge(s["hi"], g + 1)
                dve.tensor_tensor(part[1], pO[own(e), 0:w], part[0], ALU.subtract).then_inc(s["lo"], 1)

            def steps(hp, first, last):
                for m in range(2 * N):
                    if not (last and m == 2 * N - 1):
                        maximum(hp, m + 1)
                        inverse(hp, m + 1)
                    if not (first and m == 0):
                        low(hp, m - 1)
                    if not (last and m >= N):
                        h, e, i = 2 * hp + m // N + 1, 1 - m // N, m % N
                        if i == 1:
                            split_q(h, e)
                        if i in STAGE_AT:
                            take(h, e, STAGE_AT[i])
                        if i == 3:
                            set_bias(h, e)
                        if i == 5:
                            split_bias(h, e)

            set_bias(0, 0)
            split_q(0, 0)
            split_bias(0, 0)
            for which in range(TURNS):
                take(0, 0, which)
            maximum(0, 0)
            inverse(0, 0)
            steps(0, True, False)
            with dve.Fori(1, pairs - 1) as hp:
                steps(hp, False, False)
            steps(pairs - 1, False, True)
            low(pairs - 1, 2 * N - 1)

        @block.gpsimd
        def _(pool):
            def split_k(h, e, half):
                pool.wait_ge(s["k_hi"], h + 1)
                pool.sem_inc(s["apart"], 1)
                cols = slice(half * (T // 2), (half + 1) * (T // 2))
                pool.tensor_tensor(klo[:, e, cols], k_in[0:H, cols], k2[0:H, e, cols], ALU.subtract).then_inc(s["k_lo"], 1)

            for half in range(2):
                split_k(0, 0, half)
            split_k(1, 1, 0)
            split_k(1, 1, 1)
            with pool.Fori(1, pairs) as hp:
                for e in range(2):
                    for half in range(2):
                        split_k(2 * hp + e, e, half)


def build(nc, D):
    with ExitStack() as ctx:
        def sb(name, shape, dt=F32):
            return ctx.enter_context(nc.sbuf_tensor(name, shape, dt))
        S = {"ident": sb("ident", [P, P]), "ones": sb("ones", [P, P]), "gains": sb("gains", [P, G_COLS]),
             "halves": sb("halves", [1, 2 * P + CHUNK]),
             "xT": sb("xT", [P, KT, T]), "hhi": sb("hhi", [P, KT, T], F32R), "hlo": sb("hlo", [P, KT, T], F32R)}
        load_stage(nc, S, D)
        project_stage(nc, S, "in0", D["w_in"], Z_ROWS // UNIT, D["z"], G_MIX0)
        with Stage(nc, "recur") as st:
            S["aT"], S["enm"], S["wk"], S["decay"] = (st.sb(x, [P, R]) for x in ("aT", "enm", "wk", "decay"))
            S["upper"], S["lower"] = st.sb("upper", [P, P]), st.sb("lower", [P, P])
            for x in "qkvo":
                S[x] = st.sb(x, [P, 2, T])
            gate_stage(nc, S, D)
            mlstm_stage(nc, S, D)
        with Stage(nc, "rotary") as st:
            S["kr"] = st.sb("kr", [B_NOPE + B_ROPE, KEYS])
            with Stage(nc, "latents") as inner:
                S["cqT"], S["ckvT"] = (inner.sb("cqT", [P, Q_RANK // P, T]), inner.sb("ckvT", [P, KV_RANK // P, KEYS]))
                latent_stage(nc, S, D)
                heads_stage(nc, S, D)
            mla_stage(nc, S, D)
        project_stage(nc, S, "out0", D["w_out0"], D_MODEL // UNIT)
        ffn_stage(nc, S, "ffn0", G_FFN0, D["w_gate"][0], D["w_up"][0], D["w_down"][0])
        project_stage(nc, S, "in1", D["w_qkv"], 3 * D_MODEL // UNIT, D["z"], G_MIX1)
        band_stage(nc, S, D)
        project_stage(nc, S, "out1", D["w_out1"], D_MODEL // UNIT)
        ffn_stage(nc, S, "ffn1", G_FFN1, D["w_gate"][1], D["w_up"][1], D["w_down"][1])
        final_stage(nc, S, D)


_OUTS = [("y_prompt", (1024, 1024), (1, 1024, 1024)), ("y_sample", (64, 1024), (1, 64, 1024)),
         ("p_ckv", (1024, 256), (1, 1, 1024, 256)), ("p_krope", (1024, 32), (1, 1, 1024, 32)),
         ("p_C", (4, 128, 128), (1, 1, 4, 128, 128)), ("p_n", (4, 128, 1), (1, 1, 4, 128)), ("p_m", (1, 4), (1, 1, 4)),
         ("p_bk", (512, 1024), (1, 1, 512, 16, 64)), ("p_bv", (512, 1024), (1, 1, 512, 16, 64)),
         ("s_ckv", (64, 256), (1, 1, 64, 256)), ("s_krope", (64, 32), (1, 1, 64, 32)),
         ("s_C", (4, 128, 128), (1, 1, 4, 128, 128)), ("s_n", (4, 128, 1), (1, 1, 4, 128)), ("s_m", (1, 4), (1, 1, 4)),
         ("s_bk", (512, 1024), (1, 1, 512, 16, 64)), ("s_bv", (512, 1024), (1, 1, 512, 16, 64))]
_SCRATCH = [("z", (3072, T)), ("gates", (2, A_HEADS, NT * P)), ("u", (A_HEADS, NT * P)), ("w", (A_HEADS, NT * P)),
            ("bias", (C_HEADS, P, 2 * P)),
            ("heads_q", (B_HEADS * (B_NOPE + B_ROPE), T)), ("heads_k", (B_HEADS * B_NOPE, KEYS)),
            ("heads_v", (KEYS, B_HEADS * B_VDIM))]


def _rope_tables():
    half = B_ROPE // 2
    inv = np.float32(10000.0) ** (-np.arange(half, dtype=np.float32) / np.float32(half))
    pos = np.concatenate([np.arange(SEQ), PAST_LEN + np.arange(DEC_SEQ)]).astype(np.float32)
    ang = (pos[:, None] * inv[None, :]).astype(np.float32)
    cos, sin = np.cos(ang).T, np.sin(ang).T
    return np.stack([np.concatenate([cos, cos]), np.concatenate([-sin, sin])], 1).astype(np.float32)


def _layout(i):
    def cols(g):
        return g.reshape(-1, P).T

    w = i["w_in_ab"][0]
    a = 4 * A_HEADS * A_DIM
    b = a + 2 * A_HEADS
    kr = w[:, b + Q_RANK + KV_RANK:]
    pad = np.zeros((D_MODEL, 32 - A_HEADS), np.float32)
    w_in = np.concatenate([w[:, :a], w[:, b:], kr[:, 16:], kr[:, :16], w[:, a:a + A_HEADS], pad,
                           w[:, a + A_HEADS:b], pad], 1)
    uq = i["mla_w_uq"][0].reshape(Q_RANK, B_HEADS, B_NOPE + B_ROPE)
    rot = uq[:, :, B_NOPE:]
    rel = i["rel_bias_c"][0]
    gains = [i["norm_mix"][0], i["norm_ffn"][0], i["norm_mix"][1], i["norm_ffn"][1],
             i["mla_q_norm"][0], i["mla_kv_norm"][0], i["mlstm_hnorm"][0]]
    table = _rope_tables()
    halves = np.concatenate([np.repeat([1, 0, 0, 1], CHUNK), np.full(CHUNK, NEG)]).astype(np.float32)
    return {
        "x_prompt": i["x_prompt"][0], "x_sample": i["x_sample"][0], "w_in": w_in,
        "gains": np.concatenate([cols(g) for g in gains], 1),
        "g_final": i["norm_final"].reshape(1, -1),
        "b_gates": i["b_gates"].reshape(2, A_HEADS).T,
        "s_C0": i["state_mlstm_C"][0, 0], "s_n0": i["state_mlstm_n"].reshape(A_HEADS, A_DIM, 1),
        "s_m0": i["state_mlstm_m"].reshape(1, A_HEADS),
        "c_ckv": i["cache_mla_ckv"][0, 0], "c_krope": i["cache_mla_krope"][0, 0],
        "w_qn": uq[:, :, :B_NOPE].reshape(Q_RANK, -1), "w_qr": rot.reshape(Q_RANK, -1),
        "w_qs": np.concatenate([rot[:, :, 16:], rot[:, :, :16]], 2).reshape(Q_RANK, -1),
        "w_uk": i["mla_w_uk"][0].reshape(KV_RANK, -1), "w_uv": i["mla_w_uv"][0].reshape(KV_RANK, -1),
        "w_out0": i["w_out_ab"][0], "w_qkv": i["w_qkv_c"][0], "w_out1": i["w_out_c"][0],
        "c_k": i["cache_band_k"].reshape(PAST_LEN, -1), "c_v": i["cache_band_v"].reshape(PAST_LEN, -1),
        "rel": np.concatenate([np.repeat(rel[:, 2 * MAX_REL:], P - 1, 1), rel[:, :0:-1]], 1),
        "w_gate": i["w_gate"], "w_up": i["w_up"], "w_down": i["w_down"],
        "rope_k": table, "rope_q": np.concatenate([table] * (P // B_ROPE)) * np.float32(MLA_SCALE), "halves": halves[None],
        "ident": np.eye(P, dtype=np.float32), "ones": np.ones((P, P), np.float32),
        "upper": np.triu(np.ones((P, P), np.float32)), "lower": np.tril(np.full((P, P), NEG, np.float32), -1),
    }


def kernel(**inputs):
    import concourse.bacc as _bacc
    from concourse.bass_utils import run_bass_kernel_spmd as _run

    nc = _bacc.Bacc("TRN2", target_bir_lowering=False, num_devices=1)
    arrays = {"in_" + n: np.ascontiguousarray(v) for n, v in _layout(inputs).items()}
    D = {n[3:]: nc.dram_tensor(n, a.shape, F32, kind="ExternalInput").ap() for n, a in arrays.items()}
    for n, shape, _ in _OUTS:
        D[n] = nc.dram_tensor("out_" + n, shape, F32, kind="ExternalOutput").ap()
    for n, shape in _SCRATCH:
        D[n] = nc.dram_tensor("park_" + n, shape, F32, kind="Internal").ap()
    build(nc, D)
    r = _run(nc, [arrays], core_ids=[0])
    return tuple(r.results[0]["out_" + n].reshape(shape) for n, _, shape in _OUTS)
```
